# Optimizing a Trainium2 kernel written in Bass

```python
import math
import jax
import jax.numpy as jnp
from jax import lax
import numpy as np

D_MODEL = 1024
BATCH = 1
SEQ = 256
DEPTH = 2

GRID_W = 64
CTX_LEN = 256
N_MOD = 6
HEAD_DIM = 64
N_DIR = 2
RMS_EPS = 1e-6

DN_HEADS = (3 * D_MODEL) // (8 * HEAD_DIM)
DN_HEAD_DIM = HEAD_DIM
DN_WIDTH = DN_HEADS * DN_HEAD_DIM
DN_CONV = 3
DN_CHUNK = 64

SW_Q_HEADS = (3 * D_MODEL) // (8 * HEAD_DIM)
SW_KV_HEADS = SW_Q_HEADS // 3
SW_HEAD_DIM = HEAD_DIM
SW_WIDTH = SW_Q_HEADS * SW_HEAD_DIM
SW_KV_WIDTH = SW_KV_HEADS * SW_HEAD_DIM
SW_WINDOW = 128
SW_BLOCK = 128
ROPE_THETA = 10000.0
NEG_INF = -1e30

HY_CH = D_MODEL - DN_WIDTH - SW_WIDTH
HY_ORDER = 2
HY_CONV = 3
HY_BANDS = 16
HY_EMB = 1 + 2 * HY_BANDS
HY_FFN = 64
HY_FAST_DECAY = 0.3
HY_SLOW_DECAY = 1.5
HY_TARGET = 1e-2

IN_SIZES = (3 * DN_WIDTH, DN_WIDTH, N_DIR * DN_HEADS, N_DIR * DN_HEADS, (HY_ORDER + 1) * HY_CH, SW_WIDTH, SW_KV_WIDTH, SW_KV_WIDTH)
N_IN = sum(IN_SIZES)

DENSE_FF = 256 * ((8 * D_MODEL // 3 + 255) // 256)
N_EXPERTS = 8
TOP_K = 2
EXPERT_FF = 7 * D_MODEL // 2
N_DENSE = (DEPTH + 1) // 2
N_MOE = DEPTH // 2

kernel_name = "hybrid_deltanet_hyena_swa_moe_dit"

def rms_norm(x, g):
    xf = x.astype(jnp.float32)
    y = xf * lax.rsqrt(jnp.mean(xf * xf, axis=-1, keepdims=True) + RMS_EPS)
    return (y * g.astype(jnp.float32)).astype(x.dtype)

def modulate(h, shift, scale):
    return h * (1 + scale) + shift

def split_columns(p):
    bounds = [int(b) for b in np.cumsum(IN_SIZES)[:-1]]
    return jnp.split(p, bounds, axis=-1)

def centred_depthwise_conv(x, w):
    k = w.shape[0]
    return lax.conv_general_dilated(x, w[:, None, :].astype(x.dtype), window_strides=(1,), padding=[(k // 2, k // 2)], dimension_numbers=('NWC', 'WIO', 'NWC'), feature_group_count=x.shape[-1])

def l2_normalize(x):
    return x * lax.rsqrt(jnp.sum(x * x, axis=-1, keepdims=True) + RMS_EPS)

def delta_inputs(qkv, a, b, conv_w, a_log, dt_bias):
    B, L, _ = qkv.shape
    qkv = jax.nn.silu(centred_depthwise_conv(qkv, conv_w).astype(jnp.float32))
    q, k, v = jnp.split(qkv, 3, axis=-1)
    shp = (B, L, DN_HEADS, DN_HEAD_DIM)
    q = l2_normalize(q.reshape(shp)) * (DN_HEAD_DIM ** -0.5)
    k = l2_normalize(k.reshape(shp))
    v = v.reshape(shp)
    a = a.astype(jnp.float32).reshape(B, L, N_DIR, DN_HEADS)
    b = b.astype(jnp.float32).reshape(B, L, N_DIR, DN_HEADS)
    g = -jnp.exp(a_log.astype(jnp.float32)) * jax.nn.softplus(a + dt_bias.astype(jnp.float32))
    beta = jax.nn.sigmoid(b)
    return q, k, v, g, beta

def gated_delta_chunked(q, k, v, g, beta, s0):
    B, L, H, D = q.shape
    n = L // DN_CHUNK

    def chunks(t):
        t = t.reshape((B, n, DN_CHUNK, H) + t.shape[3:])
        return jnp.moveaxis(t, 3, 1)

    q, k, v, g, beta = (chunks(t) for t in (q, k, v, g, beta))
    gcum = jnp.cumsum(g, axis=-1)
    incl = jnp.tril(jnp.ones((DN_CHUNK, DN_CHUNK), dtype=bool))
    strict = jnp.tril(jnp.ones((DN_CHUNK, DN_CHUNK), dtype=bool), -1)
    diff = gcum[..., :, None] - gcum[..., None, :]
    decay = jnp.where(incl, jnp.exp(jnp.where(incl, diff, 0.0)), 0.0)
    kb = k * beta[..., None]
    a_mat = jnp.where(strict, jnp.einsum('bhncd,bhnsd->bhncs', kb, k) * decay, 0.0)
    rhs = jnp.concatenate([v * beta[..., None], kb * jnp.exp(gcum)[..., None]], axis=-1)
    sol = lax.linalg.triangular_solve(a_mat + jnp.eye(DN_CHUNK, dtype=jnp.float32), rhs, left_side=True, lower=True, unit_diagonal=True)
    u, w = sol[..., :D], sol[..., D:]
    qk = jnp.where(incl, jnp.einsum('bhncd,bhnsd->bhncs', q, k) * decay, 0.0)
    q_dec = q * jnp.exp(gcum)[..., None]
    k_dec = k * jnp.exp(gcum[..., -1:] - gcum)[..., None]
    g_tot = jnp.exp(gcum[..., -1])
    xs = tuple(jnp.moveaxis(t, 2, 0) for t in (qk, q_dec, k_dec, u, w, g_tot))

    def step(s, inp):
        qk_i, qd_i, kd_i, u_i, w_i, gt_i = inp
        v_new = u_i - jnp.einsum('bhck,bhkv->bhcv', w_i, s)
        o_i = jnp.einsum('bhck,bhkv->bhcv', qd_i, s) + jnp.einsum('bhcs,bhsv->bhcv', qk_i, v_new)
        s = s * gt_i[..., None, None] + jnp.einsum('bhck,bhcv->bhkv', kd_i, v_new)
        return s, o_i

    s_fin, o = lax.scan(step, s0, xs)
    o = jnp.transpose(o, (1, 0, 3, 2, 4)).reshape(B, L, H, D)
    return o, s_fin

def delta_bidirectional(ctx_in, lat_in):
    qc, kc, vc, gc, bc = ctx_in
    qx, kx, vx, gx, bx = lat_in
    flip = lambda t: jnp.flip(t, axis=1)
    s0 = jnp.zeros((qc.shape[0], DN_HEADS, DN_HEAD_DIM, DN_HEAD_DIM), jnp.float32)
    oc_f, s_f = gated_delta_chunked(qc, kc, vc, gc[:, :, 0], bc[:, :, 0], s0)
    oc_b, s_b = gated_delta_chunked(flip(qc), flip(kc), flip(vc), flip(gc[:, :, 1]), flip(bc[:, :, 1]), s0)
    ox_f, _ = gated_delta_chunked(qx, kx, vx, gx[:, :, 0], bx[:, :, 0], s_f)
    ox_b, _ = gated_delta_chunked(flip(qx), flip(kx), flip(vx), flip(gx[:, :, 1]), flip(bx[:, :, 1]), s_b)
    return oc_f + flip(oc_b), ox_f + flip(ox_b)

def gated_head_norm(o, z, g):
    B, L, H, D = o.shape
    on = o * lax.rsqrt(jnp.mean(o * o, axis=-1, keepdims=True) + RMS_EPS) * g.astype(jnp.float32)
    return (on * jax.nn.silu(z.astype(jnp.float32).reshape(B, L, H, D))).reshape(B, L, H * D)

def hyena_filter_spectrum(length, w1, b1, f1, w2, b2, f2, w3, b3):
    w1, b1, f1, w2, b2, f2, w3, b3 = (p.astype(jnp.float32) for p in (w1, b1, f1, w2, b2, f2, w3, b3))
    t = jnp.linspace(0.0, 1.0, length, dtype=jnp.float32)[:, None]
    omega = 2.0 * math.pi * jnp.arange(length, dtype=jnp.float32) / length
    bands = jnp.linspace(1e-4, HY_BANDS - 1, HY_BANDS, dtype=jnp.float32)
    ang = omega[:, None] * bands[None, :]
    feats = jnp.concatenate([t, jnp.cos(ang), -jnp.sin(ang)], axis=-1)
    h = jnp.sin(f1 * (feats @ w1 + b1))
    h = jnp.sin(f2 * (h @ w2 + b2))
    h = (h @ w3 + b3).reshape(length, N_DIR, HY_ORDER, HY_CH)
    max_decay = math.log(HY_TARGET) / HY_FAST_DECAY
    min_decay = math.log(HY_TARGET) / HY_SLOW_DECAY
    deltas = jnp.abs(jnp.linspace(min_decay, max_decay, HY_CH, dtype=jnp.float32))
    h = h * jnp.exp(-t * deltas[None, :])[:, None, None, :]
    fwd, bwd = h[:, 0], h[:, 1]
    kern = jnp.concatenate([fwd, jnp.zeros_like(fwd[:1]), bwd[:0:-1]], axis=0)
    kern = kern * lax.rsqrt(jnp.sum(kern * kern, axis=0, keepdims=True) + RMS_EPS)
    return jnp.fft.rfft(kern, axis=0)

def bidir_long_conv(u, spec, skip):
    L = u.shape[1]
    U = jnp.fft.rfft(u, n=2 * L, axis=1)
    y = jnp.fft.irfft(U * spec[None], n=2 * L, axis=1)[:, :L]
    return y + skip.astype(jnp.float32) * u

def hyena_stream(p, conv_w, spec, skip):
    z = centred_depthwise_conv(p, conv_w).astype(jnp.float32)
    v, x1, x2 = jnp.split(z, 3, axis=-1)
    y = x1 * bidir_long_conv(v, spec[:, 0], skip[0])
    y = x2 * bidir_long_conv(y, spec[:, 1], skip[1])
    return y.astype(p.dtype)

def rope_1d(x, pos):
    n = x.shape[-1] // 2
    inv = jnp.power(ROPE_THETA, -jnp.arange(n, dtype=jnp.float32) / n)
    ang = pos.astype(jnp.float32)[:, None] * inv[None, :]
    cos = jnp.cos(ang)[None, :, None, :]
    sin = jnp.sin(ang)[None, :, None, :]
    xf = x.astype(jnp.float32)
    a, b = xf[..., :n], xf[..., n:]
    return jnp.concatenate([a * cos - b * sin, b * cos + a * sin], axis=-1).astype(x.dtype)

def axial_rope(x, row, col):
    half = x.shape[-1] // 2
    return jnp.concatenate([rope_1d(x[..., :half], row), rope_1d(x[..., half:], col)], axis=-1)

def window_attention_latent(q, k, v, kc, vc, sink):
    B, L, _, D = q.shape
    nb = L // SW_BLOCK
    G = SW_Q_HEADS // SW_KV_HEADS
    qb = q.astype(jnp.float32).reshape(B, nb, SW_BLOCK, SW_KV_HEADS, G, D) * (D ** -0.5)

    def band(t):
        tb = t.astype(jnp.float32).reshape(B, nb, SW_BLOCK, SW_KV_HEADS, D)
        tp = jnp.pad(tb, ((0, 0), (1, 1), (0, 0), (0, 0), (0, 0)))
        return jnp.concatenate([tp[:, :-2], tp[:, 1:-1], tp[:, 2:]], axis=2)

    kw, vw = band(k), band(v)
    s_loc = jnp.einsum('bnqhgd,bnkhd->bnhgqk', qb, kw)
    blk = jnp.arange(nb)[:, None, None]
    qpos = blk * SW_BLOCK + jnp.arange(SW_BLOCK)[None, :, None]
    kpos = (blk - 1) * SW_BLOCK + jnp.arange(3 * SW_BLOCK)[None, None, :]
    valid = (jnp.abs(kpos - qpos) <= SW_WINDOW) & (kpos >= 0) & (kpos < L)
    s_loc = jnp.where(valid[None, :, None, None], s_loc, NEG_INF)
    s_ctx = jnp.einsum('bnqhgd,bkhd->bnhgqk', qb, kc.astype(jnp.float32))
    s_sink = jnp.broadcast_to(sink.astype(jnp.float32).reshape(1, 1, SW_KV_HEADS, G, 1, 1), s_loc.shape[:-1] + (1,))
    p = jax.nn.softmax(jnp.concatenate([s_loc, s_ctx, s_sink], axis=-1), axis=-1)
    nk = 3 * SW_BLOCK
    o = jnp.einsum('bnhgqk,bnkhd->bnqhgd', p[..., :nk], vw) + jnp.einsum('bnhgqk,bkhd->bnqhgd', p[..., nk:nk + kc.shape[1]], vc.astype(jnp.float32))
    return o.reshape(B, L, SW_Q_HEADS * D)

def context_attention(q, k, v, sink):
    B, Lc, _, D = q.shape
    G = SW_Q_HEADS // SW_KV_HEADS
    qg = q.astype(jnp.float32).reshape(B, Lc, SW_KV_HEADS, G, D) * (D ** -0.5)
    s = jnp.einsum('bqhgd,bkhd->bhgqk', qg, k.astype(jnp.float32))
    s_sink = jnp.broadcast_to(sink.astype(jnp.float32).reshape(1, SW_KV_HEADS, G, 1, 1), s.shape[:-1] + (1,))
    p = jax.nn.softmax(jnp.concatenate([s, s_sink], axis=-1), axis=-1)
    o = jnp.einsum('bhgqk,bkhd->bqhgd', p[..., :-1], v.astype(jnp.float32))
    return o.reshape(B, Lc, SW_Q_HEADS * D)

def swiglu(h, w_gate, w_up, w_down):
    return (jax.nn.silu(h @ w_gate) * (h @ w_up)) @ w_down

def moe_swiglu(h, router, w_gate, w_up, w_down):
    logits = (h @ router).astype(jnp.float32)
    top_logit, top_idx = lax.top_k(logits, TOP_K)
    top_w = jax.nn.softmax(top_logit, axis=-1)
    gate = jnp.sum(jax.nn.one_hot(top_idx, N_EXPERTS, dtype=jnp.float32) * top_w[..., None], axis=-2).astype(h.dtype)
    out = jnp.zeros_like(h)
    for e in range(N_EXPERTS):
        out = out + gate[..., e:e + 1] * swiglu(h, w_gate[e], w_up[e], w_down[e])
    return out

def setup_inputs(seed: int = 0) -> dict:
    key = jax.random.key(seed)
    ks = iter(jax.random.split(key, 48))
    nrm = lambda shape, s: jax.random.normal(next(ks), shape, jnp.float32) * s
    D = D_MODEL
    a_init = jax.random.uniform(next(ks), (DEPTH, N_DIR, DN_HEADS), jnp.float32, 1.0, 16.0)
    dt = jnp.exp(jax.random.uniform(next(ks), (DEPTH, N_DIR, DN_HEADS), jnp.float32, math.log(1e-3), math.log(1e-1)))
    hy_out = N_DIR * HY_ORDER * HY_CH
    return {
        "x": nrm((BATCH, SEQ, D), 1.0),
        "c": nrm((BATCH, D), 1.0),
        "ctx": nrm((BATCH, CTX_LEN, D), 1.0),
        "c_ctx": nrm((D,), 1.0),
        "w_mod": nrm((DEPTH, D, N_MOD * D), 0.5 * D ** -0.5),
        "b_mod": nrm((DEPTH, N_MOD * D), 0.02),
        "norm_mix_g": 1.0 + nrm((DEPTH, D), 0.1),
        "norm_ffn_g": 1.0 + nrm((DEPTH, D), 0.1),
        "w_in": nrm((DEPTH, D, N_IN), D ** -0.5),
        "dn_conv_w": nrm((DEPTH, DN_CONV, 3 * DN_WIDTH), DN_CONV ** -0.5),
        "dn_a_log": jnp.log(a_init),
        "dn_dt_bias": dt + jnp.log(-jnp.expm1(-dt)),
        "dn_norm_g": 1.0 + nrm((DEPTH, DN_HEAD_DIM), 0.1),
        "hy_conv_w": nrm((DEPTH, HY_CONV, (HY_ORDER + 1) * HY_CH), HY_CONV ** -0.5),
        "hy_w1": nrm((DEPTH, HY_EMB, HY_FFN), HY_EMB ** -0.5),
        "hy_b1": nrm((DEPTH, HY_FFN), 0.1),
        "hy_freq1": 1.0 + nrm((DEPTH, HY_FFN), 0.1),
        "hy_w2": nrm((DEPTH, HY_FFN, HY_FFN), HY_FFN ** -0.5),
        "hy_b2": nrm((DEPTH, HY_FFN), 0.1),
        "hy_freq2": 1.0 + nrm((DEPTH, HY_FFN), 0.1),
        "hy_w3": nrm((DEPTH, HY_FFN, hy_out), HY_FFN ** -0.5),
        "hy_b3": nrm((DEPTH, hy_out), 0.1),
        "hy_skip": nrm((DEPTH, HY_ORDER, HY_CH), 1.0),
        "sw_sink": nrm((DEPTH, SW_Q_HEADS), 0.5),
        "w_out": nrm((DEPTH, D, D), D ** -0.5),
        "ffn_w_gate": nrm((N_DENSE, D, DENSE_FF), D ** -0.5),
        "ffn_w_up": nrm((N_DENSE, D, DENSE_FF), D ** -0.5),
        "ffn_w_down": nrm((N_DENSE, DENSE_FF, D), DENSE_FF ** -0.5),
        "moe_router": nrm((N_MOE, D, N_EXPERTS), D ** -0.5),
        "moe_w_gate": nrm((N_MOE, N_EXPERTS, D, EXPERT_FF), D ** -0.5),
        "moe_w_up": nrm((N_MOE, N_EXPERTS, D, EXPERT_FF), D ** -0.5),
        "moe_w_down": nrm((N_MOE, N_EXPERTS, EXPERT_FF, D), EXPERT_FF ** -0.5),
        "final_norm_g": 1.0 + nrm((D,), 0.1),
    }

def reference(x, c, ctx, c_ctx, w_mod, b_mod, norm_mix_g, norm_ffn_g, w_in, dn_conv_w, dn_a_log, dn_dt_bias, dn_norm_g, hy_conv_w, hy_w1, hy_b1, hy_freq1, hy_w2, hy_b2, hy_freq2, hy_w3, hy_b3, hy_skip, sw_sink, w_out, ffn_w_gate, ffn_w_up, ffn_w_down, moe_router, moe_w_gate, moe_w_up, moe_w_down, final_norm_g):
    B, L, _ = x.shape
    Lc = ctx.shape[1]
    rows = L // GRID_W
    row = jnp.repeat(jnp.arange(rows), GRID_W)
    col = jnp.tile(jnp.arange(GRID_W), rows)
    silu_c = jax.nn.silu(c)
    silu_cc = jax.nn.silu(c_ctx)

    for layer in range(DEPTH):
        last = layer == DEPTH - 1
        mod_x = jnp.split((silu_c @ w_mod[layer] + b_mod[layer])[:, None, :], N_MOD, axis=-1)
        mod_c = jnp.split(silu_cc @ w_mod[layer] + b_mod[layer], N_MOD, axis=-1)

        hx = modulate(rms_norm(x, norm_mix_g[layer]), mod_x[0], mod_x[1])
        hc = modulate(rms_norm(ctx, norm_mix_g[layer]), mod_c[0], mod_c[1])
        px = split_columns(hx @ w_in[layer])
        pc = split_columns(hc @ w_in[layer])

        dn_c_in = delta_inputs(pc[0], pc[2], pc[3], dn_conv_w[layer], dn_a_log[layer], dn_dt_bias[layer])
        dn_x_in = delta_inputs(px[0], px[2], px[3], dn_conv_w[layer], dn_a_log[layer], dn_dt_bias[layer])
        dn_o_c, dn_o_x = delta_bidirectional(dn_c_in, dn_x_in)
        dn_x = gated_head_norm(dn_o_x, px[1], dn_norm_g[layer]).astype(x.dtype)

        hy_p = (hy_w1[layer], hy_b1[layer], hy_freq1[layer], hy_w2[layer], hy_b2[layer], hy_freq2[layer], hy_w3[layer], hy_b3[layer])
        hy_x = hyena_stream(px[4], hy_conv_w[layer], hyena_filter_spectrum(L, *hy_p), hy_skip[layer])

        sw_q_x = axial_rope(px[5].reshape(B, L, SW_Q_HEADS, SW_HEAD_DIM), row, col)
        sw_k_x = axial_rope(px[6].reshape(B, L, SW_KV_HEADS, SW_HEAD_DIM), row, col)
        sw_v_x = px[7].reshape(B, L, SW_KV_HEADS, SW_HEAD_DIM)
        sw_k_c = pc[6].reshape(B, Lc, SW_KV_HEADS, SW_HEAD_DIM)
        sw_v_c = pc[7].reshape(B, Lc, SW_KV_HEADS, SW_HEAD_DIM)
        sw_x = window_attention_latent(sw_q_x, sw_k_x, sw_v_x, sw_k_c, sw_v_c, sw_sink[layer]).astype(x.dtype)

        mix_x = jnp.concatenate([dn_x, hy_x, sw_x], axis=-1) @ w_out[layer]
        x = x + mod_x[2] * mix_x

        if not last:
            dn_c = gated_head_norm(dn_o_c, pc[1], dn_norm_g[layer]).astype(ctx.dtype)
            hy_c = hyena_stream(pc[4], hy_conv_w[layer], hyena_filter_spectrum(Lc, *hy_p), hy_skip[layer])
            sw_c = context_attention(pc[5].reshape(B, Lc, SW_Q_HEADS, SW_HEAD_DIM), sw_k_c, sw_v_c, sw_sink[layer]).astype(ctx.dtype)
            mix_c = jnp.concatenate([dn_c, hy_c, sw_c], axis=-1) @ w_out[layer]
            ctx = ctx + mod_c[2] * mix_c

        i = layer // 2
        hx2 = modulate(rms_norm(x, norm_ffn_g[layer]), mod_x[3], mod_x[4])
        if layer % 2 == 0:
            x = x + mod_x[5] * swiglu(hx2, ffn_w_gate[i], ffn_w_up[i], ffn_w_down[i])
        else:
            x = x + mod_x[5] * moe_swiglu(hx2, moe_router[i], moe_w_gate[i], moe_w_up[i], moe_w_down[i])
        if not last:
            hc2 = modulate(rms_norm(ctx, norm_ffn_g[layer]), mod_c[3], mod_c[4])
            if layer % 2 == 0:
                ctx = ctx + mod_c[5] * swiglu(hc2, ffn_w_gate[i], ffn_w_up[i], ffn_w_down[i])
            else:
                ctx = ctx + mod_c[5] * moe_swiglu(hc2, moe_router[i], moe_w_gate[i], moe_w_up[i], moe_w_down[i])

    return rms_norm(x, final_norm_g)


_drawn_inputs = setup_inputs


def setup_inputs(seed=0):
    import zlib

    import numpy as np

    out = dict(_drawn_inputs(seed))
    spreads = {}
    factors = {'dn_norm_g': 3.18, 'sw_sink': 26.443}
    for name, (base, spread) in spreads.items():
        noise = np.random.default_rng([zlib.crc32(name.encode()), seed]).standard_normal(out[name].shape)
        drawn = base * np.exp(spread * noise) if base else spread * noise
        out[name] = jnp.asarray(drawn.astype(out[name].dtype))
    for name, factor in factors.items():
        out[name] = (out[name] * factor).astype(out[name].dtype)
    return out
```

```python
from contextlib import ExitStack

import numpy as np

import concourse.bass as bass
from concourse import mybir

P = 128
ALU = mybir.AluOpType
ACT = mybir.ActivationFunctionType
F32 = mybir.dt.float32
U32 = mybir.dt.uint32
X_AXIS = mybir.AxisListType.X

D_MODEL = 1024
SEQ = 256
N_TOK = 2 * SEQ
N_LAYERS = 2
HEAD = 64
DN_HEADS = 6
SW_HEADS = 6
HY_CH = 256
FFN_DENSE = 2816
N_EXPERTS = 8
FFN_EXPERT = 3584
RMS_EPS = 1e-6
TINY = 1e-30
ROUND = 1.5 * 2.0 ** 23
TWO_PI = (6.28125, 1.9350051879882812e-3, 3.0199159795074593e-7)
PI_BELOW = 3.1415925
GRID_W = 64
SW_WINDOW = 128

KT = D_MODEL // P
TT = N_TOK // P
N_MOD_TILES = 6 * KT
PAIRS = DN_HEADS // 2
DIRS = 2
PROBS = DIRS * DN_HEADS
DN_TILES = 3 * PAIRS
HY_TILES = 3 * HY_CH // P
SW_TILES = SW_HEADS // 2
CHUNK = P
LEVELS = 7

C_DN, C_Z, C_A = 0, 1152, 1536
C_HY, C_Q, C_K, C_V = 1560, 2328, 2712, 2840
ABV = 24 + 2 * HEAD

SLOT = 2048
RING = 7
MOD_SLOTS = N_MOD_TILES // 2
IN_SLOTS = 12
OUT_SLOTS = KT // 2
ROUND_F = 2 * P
DENSE_ROUNDS = FFN_DENSE // ROUND_F
MOE_ROUNDS = FFN_EXPERT // ROUND_F

(K_ID, K_ONE, K_BLK, K_INC, K_LVL, K_COS, K_SIN, K_ROT, K_BAND, K_IOTA, K_END) = np.cumsum(
    [0, P, P, P, 2 * P, 2 * LEVELS * P, SEQ, SEQ, P, 2 * N_TOK, 8]).tolist()
(H_C, H_S, H_CT, H_ST, H_WIN, H_FEAT, H_END) = np.cumsum(
    [0, 2 * SEQ, 2 * SEQ, 2 * SEQ, 2 * SEQ, 2 * 2 * HY_CH, SEQ]).tolist()

(V_GMIX, V_GFFN, V_BMOD, V_DNC, V_HYC, V_DNG, V_FR1, V_B1, V_FR2, V_B2, V_END) = np.cumsum(
    [0, KT, KT, N_MOD_TILES, 3 * DN_TILES, 3 * HY_TILES, 1, 1, 1, 1, 1]).tolist()


def shape_constants():
    t = np.arange(P)
    k = np.zeros((P, K_END), np.float32)
    k[:, K_ID:K_ID + P] = np.eye(P)
    k[:, K_ONE:K_ONE + P] = 1.0
    k[:, K_BLK:K_BLK + P] = (t[:, None] // HEAD) == (t[None] // HEAD)
    k[:, K_INC:K_INC + P] = t[None] >= t[:, None]
    k[:, K_INC + P:K_INC + 2 * P] = t[None] <= t[:, None]
    for lv in range(LEVELS):
        b = 1 << lv
        same = (t[:, None] // (2 * b)) == (t[None] // (2 * b))
        fwd = same & (t[:, None] // b % 2 == 0) & (t[None] // b % 2 == 1)
        k[:, K_LVL + lv * P:K_LVL + (lv + 1) * P] = fwd
        k[:, K_LVL + (LEVELS + lv) * P:K_LVL + (LEVELS + lv + 1) * P] = fwd.T
    half, n = HEAD // 2, HEAD // 4
    inv = np.power(np.float32(10000.0), -np.arange(n, dtype=np.float32) / np.float32(n)).astype(np.float32)
    pos = np.arange(SEQ)
    for ch in range(P):
        c = ch % HEAD
        where = (pos // GRID_W if c < half else pos % GRID_W).astype(np.float32)
        ang = where * inv[c % n]
        k[ch, K_COS:K_COS + SEQ] = np.cos(ang)
        k[ch, K_SIN:K_SIN + SEQ] = np.sin(ang)
        first = c % half < n
        k[ch + n if first else ch - n, K_ROT + ch] = -1.0 if first else 1.0
    for qt in range(2):
        q = qt * P + t
        far = np.abs(q[:, None] - pos[None]) > SW_WINDOW
        k[:, K_BAND + qt * N_TOK + SEQ:K_BAND + (qt + 1) * N_TOK] = np.where(far, -1e30, 0.0)
    k[:, K_IOTA:K_IOTA + 8] = np.arange(8)

    h = np.zeros((P, H_END), np.float32)
    m = np.arange(SEQ)
    ang = np.pi * np.mod(m[:, None] * (2 * m[None] + 1), 4 * SEQ) / (2 * SEQ)
    for base, tab in ((H_C, np.cos(ang)), (H_S, np.sin(ang)), (H_CT, np.cos(ang).T / SEQ),
                      (H_ST, -np.sin(ang).T / SEQ)):
        h[:, base:base + 2 * SEQ] = tab.reshape(2, P, SEQ).transpose(1, 0, 2).reshape(P, 2 * SEQ)
    tl = np.linspace(0.0, 1.0, SEQ, dtype=np.float32)
    omega = (np.float32(2.0 * np.pi) * m.astype(np.float32) / np.float32(SEQ)).astype(np.float32)
    bands = np.linspace(1e-4, 15, 16, dtype=np.float32)
    fa = (omega[:, None] * bands[None]).astype(np.float32)
    feats = np.concatenate([tl[:, None], np.cos(fa), -np.sin(fa)], axis=1).astype(np.float32)
    h[0:feats.shape[1], H_FEAT:H_FEAT + SEQ] = feats.T
    deltas = np.abs(np.linspace(np.log(1e-2) / 1.5, np.log(1e-2) / 0.3, HY_CH, dtype=np.float32))
    win = np.exp(-tl[:, None] * deltas[None]).astype(np.float32)
    both = np.stack([win, win], axis=1)
    both[0, 1] = 0.0
    h[:, H_WIN:H_WIN + 4 * HY_CH] = both.reshape(2, P, 2 * HY_CH).transpose(1, 0, 2).reshape(P, -1)
    return k, h


def build(nc, a, out):
    with ExitStack() as ctx:
        def sb(name, shape, dt=F32):
            return ctx.enter_context(nc.sbuf_tensor(name, shape, dt))

        def sem(name):
            return ctx.enter_context(nc.semaphore(name))

        ps = [ctx.enter_context(nc.psum_tensor(f"bank{i}", [P, 512], F32)) for i in range(8)]

        ring = sb("ring", [P, RING, SLOT])
        con = sb("con", [P, K_END])
        xT = sb("xT", [P, KT, N_TOK])
        hT = sb("hT", [P, KT, N_TOK])
        vrow = sb("vrow", [P, P])
        vcol = sb("vcol", [P, P])
        vrow2 = sb("vrow2", [P, P])
        vcol2 = sb("vcol2", [P, 3 * KT])
        cs = sb("cs", [P, KT, 2])
        mod = sb("mod", [P, N_MOD_TILES, 2])
        amul = sb("amul", [P, 2, KT, 2])
        rows = sb("rows", [P, 2 * PROBS + SW_HEADS])
        qkv = sb("qkv", [P, DN_TILES, N_TOK])
        zz = sb("zz", [P, PAIRS, N_TOK])
        abv = sb("abv", [P, TT, ABV])
        misc = sb("misc", [P, 2])
        WORK = 18500
        work = sb("work", [P, WORK])

        def carve(at, *shape):
            n = int(np.prod(shape))
            assert at + n <= WORK, (at, shape)
            v = work[:, at:at + n]
            if len(shape) == 2:
                v = v.rearrange("p (a b) -> p a b", a=shape[0])
            elif len(shape) == 3:
                v = v.rearrange("p (a b c) -> p a b c", a=shape[0], b=shape[1])
            return v, at + n

        SEG = lambda lo: (N_TOK - lo) // SEQ
        hy, at = carve(0, HY_TILES, N_TOK)
        qT, at = carve(at, SW_TILES, N_TOK)
        kT, after_proj = carve(at, N_TOK)
        hc, at = carve(after_proj, H_END)
        w3, at = carve(at, 4 * HY_CH)
        w12, at = carve(at, P)
        kre, at = carve(at, 2, 2 * HY_CH)
        kim, at = carve(at, 2, 2 * HY_CH)
        hy_scratch = at
        kern, at = carve(at, 2, 2, 2 * HY_CH)
        hh1, at = carve(at, SEQ)
        hh2, at = carve(at, SEQ)
        htmp, at = carve(at, SEQ)
        htmp2, at = carve(at, SEQ)
        hnorm, at = carve(at, 2 * HY_CH)
        hskip, at = carve(at, 2 * HY_CH)
        ut, at = carve(hy_scratch, 2, N_TOK)
        x1t, at = carve(at, 2, N_TOK)
        pre, at = carve(at, 2, N_TOK)
        pim, at = carve(at, 2, N_TOK)
        ptmp, at = carve(at, N_TOK)
        sc, at = carve(after_proj, 2, N_TOK)
        pT, at = carve(at, 2, N_TOK)
        rot, at = carve(at, 4, SEQ)
        st, at = carve(at, 2, 8)
        ktok, at = carve(0, TT, DN_HEADS * HEAD)
        vtok, at = carve(at, TT, DN_HEADS * HEAD)
        gt, at = carve(at, TT, PROBS)
        bt, at = carve(at, TT, PROBS)
        gc, at = carve(at, TT, PROBS)
        eg, at = carve(at, TT, PROBS)
        gtmp, at = carve(at, TT, PROBS)
        gtmp2, at = carve(at, TT, PROBS)
        kds, at = carve(at, PROBS)
        Amat, at = carve(at, PROBS, CHUNK)
        Xm, at = carve(at, PROBS, CHUNK)
        XT, at = carve(at, PROBS, CHUNK)
        Bm, at = carve(at, PROBS, CHUNK)
        QK, at = carve(at, PROBS, CHUNK)
        egb, at = carve(at, 2 * PAIRS, CHUNK)
        kb, at = carve(at, 2 * PAIRS, CHUNK)
        state, at = carve(at, 2 * PAIRS, P)
        kd, at = carve(at, 2 * PAIRS, P)
        rhs, at = carve(at, PROBS, HEAD)
        Am, at = carve(at, PROBS, CHUNK)
        qd, at = carve(at, 2 * PAIRS, CHUNK)
        vnew = kb.rearrange("p a b -> p (a b)").rearrange("p (q d) -> p q d", q=PROBS)
        sil, at = carve(0, 2, N_TOK)
        act, at = carve(at, 2, 2, N_TOK)
        geb, at = carve(at, N_EXPERTS, SEQ)
        lg, at = carve(at, 2, 8)
        gate, at = carve(at, 2, 8)
        top, at = carve(at, 2, 8)
        tix, at = carve(at, 2, 8)
        tmp8, at = carve(at, 2, 8)
        wr, at = carve(at, KT, N_EXPERTS)
        topi = sb("topi", [P, 2, 8], U32)
        rms_r, at = carve(0, N_TOK)
        rms_s, at = carve(at, N_TOK)

        ident = con[:, K_ID:K_ID + P]
        ones = con[:, K_ONE:K_ONE + P]
        blk = con[:, K_BLK:K_BLK + P]

        eps_col, one_col = misc[:, 0:1], misc[:, 1:2]

        def XT_flat(i):
            return Xm.rearrange("p a b -> p (a b)")[:, i * N_TOK:(i + 1) * N_TOK] if i < 3 else \
                XT.rearrange("p a b -> p (a b)")[:, (i - 3) * N_TOK:(i - 2) * N_TOK]

        def row_loads(layer):
            def rows128(at, v):
                v = v.rearrange("(r p) -> r p", p=P)
                return vrow[at:at + v.shape[0], :], v
            flat = lambda v: v.rearrange("a b -> (a b)")
            every = lambda v: v.partition_broadcast(P)
            return [
                rows128(V_GMIX, a["norm_mix_g"][layer]), rows128(V_GFFN, a["norm_ffn_g"][layer]),
                rows128(V_BMOD, a["b_mod"][layer]), rows128(V_DNC, flat(a["dn_conv_w"][layer])),
                rows128(V_HYC, flat(a["hy_conv_w"][layer])),
                (vrow[V_DNG:V_DNG + 1, 0:HEAD], a["dn_norm_g"][layer:layer + 1, :]),
                (vrow[V_DNG:V_DNG + 1, HEAD:P], a["dn_norm_g"][layer:layer + 1, :]),
                (vrow[V_FR1:V_FR1 + 1, 0:HEAD], a["hy_freq1"][layer:layer + 1, :]),
                (vrow[V_B1:V_B1 + 1, 0:HEAD], a["hy_b1"][layer:layer + 1, :]),
                (vrow[V_FR2:V_FR2 + 1, 0:HEAD], a["hy_freq2"][layer:layer + 1, :]),
                (vrow[V_B2:V_B2 + 1, 0:HEAD], a["hy_b2"][layer:layer + 1, :]),
                (rows[:, 0:PROBS], every(flat(a["dn_a_log"][layer]))),
                (rows[:, PROBS:2 * PROBS], every(flat(a["dn_dt_bias"][layer]))),
                (rows[:, 2 * PROBS:2 * PROBS + SW_HEADS], every(a["sw_sink"][layer])),
                (hc[:, :], a["k_hy"]), (w12[0:33, 0:HEAD], a["hy_w1"][layer]), (w12[0:HEAD, HEAD:P], a["hy_w2"][layer]),
                (w3[0:HEAD, :], a["hy_w3"][layer]), (w3[HEAD:HEAD + 1, :], a["hy_b3"][layer:layer + 1, :]),
                (hskip[:, :], every(flat(a["hy_skip"][layer]))),
            ]

        ROW_LOADS = 20
        HY_PHASES = 23
        phase = sem("phase")
        dve_chain, act_chain, pool_chain = sem("dve_chain"), sem("act_chain"), sem("pool_chain")
        slot_full = [sem(f"slot_full{i}") for i in range(RING)]
        setup_in, rows_in, router_in = sem("setup_in"), sem("rows_in"), sem("router_in")
        mod_ready = sem("mod_ready")
        normed = sem("normed")
        proj_ready = sem("proj_ready")
        conv_done = sem("conv_done")
        copy_done = sem("copy_done")
        score_ready, score_read = sem("score_ready"), sem("score_read")
        max_ready, exp_ready, prob_ready = sem("max_ready"), sem("exp_ready"), sem("prob_ready")
        turn_ready, turn_read = sem("turn_ready"), sem("turn_read")
        pv_ready, pv_read = sem("pv_ready"), sem("pv_read")
        am_ready, b_ready, b_copied = sem("am_ready"), sem("b_ready"), sem("b_copied")
        p_ready, x_done = sem("p_ready"), sem("x_done")
        mix_ready, mix_added = sem("mix_ready"), sem("mix_added")
        gu_ready, sil_ready, act_ready = sem("gu_ready"), sem("sil_ready"), sem("act_ready")
        down_ready, down_added = sem("down_ready"), sem("down_added")
        up_done = sem("up_done")
        rows_out, out_done = sem("rows_out"), sem("out_done")

        w_in_v = a["w_in"].rearrange("l (k p) n -> l p k n", p=P)
        w_out_v = a["w_out"]
        w_mod_v = a["w_mod"].rearrange("l (k p) n -> l p k n", p=P)
        NS = {"mod": MOD_SLOTS, "in": IN_SLOTS, "out": OUT_SLOTS}

        def wide(s):
            return ring[:, s % RING, :].rearrange("p (k n) -> p k n", k=KT)

        def deep(s):
            return ring[:, s % RING, :].rearrange("p (k n) -> p k n", k=2)

        in_tiles = ([("dn", i) for i in range(DN_TILES)] + [("z", i) for i in range(PAIRS)]
                    + [("hy", i) for i in range(HY_TILES)] + [("q", i) for i in range(SW_TILES)] + [("k", 0)])

        def halves(dst, src):
            return [(dst[:, 0:KT // 2], src[:, 0:KT // 2]), (dst[:, KT // 2:KT], src[:, KT // 2:KT])]

        def in_slot_loads(layer, j, s):
            w = w_in_v[layer]
            if j == 0:
                return [(wide(s)[:, :, 0:24], w[:, :, C_A:C_A + 24]),
                        (wide(s)[:, :, 24:ABV], w[:, :, C_V:C_V + P])]
            pair = in_tiles[2 * (j - 1):2 * j]
            if pair[0][0] in ("q", "k") or pair[1][0] in ("q", "k"):
                loads = []
                for half, (kind, i) in enumerate(pair):
                    if kind == "q":
                        for hd in range(2):
                            c = C_Q + (i + 3 * hd) * HEAD
                            loads.append((wide(s)[:, :, half * P + hd * HEAD:half * P + (hd + 1) * HEAD],
                                          w[:, :, c:c + HEAD]))
                    else:
                        for hd in range(2):
                            loads.append((wide(s)[:, :, half * P + hd * HEAD:half * P + (hd + 1) * HEAD],
                                          w[:, :, C_K + hd * HEAD:C_K + (hd + 1) * HEAD]))
                return loads
            base = {"dn": C_DN, "z": C_Z, "hy": C_HY}[pair[0][0]] + pair[0][1] * P
            if pair[0][0] == pair[1][0]:
                return halves(wide(s), w[:, :, base:base + 2 * P])
            base2 = {"dn": C_DN, "z": C_Z, "hy": C_HY}[pair[1][0]] + pair[1][1] * P
            return [(wide(s)[:, :, 0:P], w[:, :, base:base + P]), (wide(s)[:, :, P:2 * P], w[:, :, base2:base2 + P])]

        def out_slot_loads(layer, j, s):
            cols = slice(j * 2 * P, (j + 1) * 2 * P)
            w = w_out_v[layer]
            plain = w[0:5 * P, cols].rearrange("(k p) n -> p k n", p=P)
            sw = w[5 * P:8 * P, cols].rearrange("(h i d) n -> h d i n", h=2, i=SW_TILES)
            return [(wide(s)[:, 0:5, :], plain), (wide(s)[0:HEAD, 5:8, :], sw[0]), (wide(s)[HEAD:P, 5:8, :], sw[1])]

        def gu_loads(wm, r, s):
            return halves(wide(s), wm[:, r * ROUND_F:(r + 1) * ROUND_F].rearrange("(k p) n -> p k n", p=P))

        def dn_loads(wm, r, s):
            src = wm[r * ROUND_F:(r + 1) * ROUND_F, :].rearrange("(k p) n -> p k n", p=P)
            return [(deep(s)[:, 0:1], src[:, 0:1]), (deep(s)[:, 1:2], src[:, 1:2])]

        def round_order(n):
            yield "g", 0
            yield "u", 0
            for r in range(1, n):
                yield "g", r
                yield "u", r
                yield "d", r - 1
            yield "d", n - 1

        plan = []
        for layer in range(N_LAYERS):
            for j in range(MOD_SLOTS):
                plan.append((lambda s, l=layer, j=j: halves(wide(s), w_mod_v[l][:, :, j * 2 * P:(j + 1) * 2 * P]),
                             (mod_ready, layer * MOD_SLOTS + j + 1)))
            for j in range(IN_SLOTS):
                plan.append((lambda s, l=layer, j=j: in_slot_loads(l, j, s),
                             (proj_ready, layer * 2 * IN_SLOTS + 2 * (j + 1))))
            for j in range(OUT_SLOTS):
                plan.append((lambda s, l=layer, j=j: out_slot_loads(l, j, s),
                             (mix_ready, layer * KT + 2 * (j + 1))))
            if layer == 0:
                for kind, r in round_order(DENSE_ROUNDS):
                    if kind == "d":
                        plan.append((lambda s, r=r: dn_loads(a["ffn_w_down"][0], r, s), (down_ready, KT * (r + 1))))
                    else:
                        w = a["ffn_w_gate" if kind == "g" else "ffn_w_up"][0]
                        plan.append((lambda s, r=r, w=w: gu_loads(w, r, s), (gu_ready, 2 * (r + 1))))
        S_MOE = len(plan)
        MOE_ORDER = list(round_order(MOE_ROUNDS))
        assert len(MOE_ORDER) % RING == 0

        counts, landed = [0] * RING, []
        for n, (loads, _) in enumerate(plan):
            counts[n % RING] += 16 * len(loads(n))
            landed.append(counts[n % RING])
        MOE_USE = 32
        MOE_INC = MOE_USE * len(MOE_ORDER) // RING

        def moe_landed(j):
            n = S_MOE + j
            return counts[n % RING] + MOE_USE * (j // RING + 1)

        block = ctx.enter_context(nc.Block())

        @block.sync
        def _(sp):
            def load(loads, s):
                for dst, src in loads:
                    sp.dma_start(dst, src).then_inc(slot_full[s % RING], 16)
            for s, (loads, _) in enumerate(plan):
                if s == 0:
                    sp.dma_start(con[:, :], a["k_con"]).then_inc(setup_in, 16)
                    sp.dma_start(hT[:, 0:4, :].rearrange("p (t k) n -> p t (k n)", t=2),
                                 a["ctx"][0].rearrange("(t p) n -> p t n", p=P)).then_inc(setup_in, 16)
                    sp.dma_start(hT[:, 4:8, :].rearrange("p (t k) n -> p t (k n)", t=2),
                                 a["x"][0].rearrange("(t p) n -> p t n", p=P)).then_inc(setup_in, 16)
                    sp.dma_start(vrow2[0:KT, :], a["c_ctx"].rearrange("(k p) -> k p", p=P)).then_inc(setup_in, 16)
                    sp.dma_start(vrow2[KT:2 * KT, :], a["c"][0].rearrange("(k p) -> k p", p=P)).then_inc(setup_in, 16)
                    sp.dma_start(vrow2[2 * KT:3 * KT, :],
                                 a["final_norm_g"].rearrange("(k p) -> k p", p=P)).then_inc(setup_in, 16)
                if s >= RING:
                    used, count = plan[s - RING][1]
                    sp.wait_ge(used, count)
                load(loads(s), s)

            def moe_load(e, j, w_used):
                s = S_MOE + j
                kind, r = MOE_ORDER[j]
                sp.wait_ge(*w_used)
                if kind == "d":
                    src = a["moe_w_down"][0][bass.ds(e, 1), r * ROUND_F:(r + 1) * ROUND_F, :].rearrange(
                        "e (k p) n -> p (e k) n", p=P)
                    loads = [(deep(s)[:, 0:1], src[:, 0:1]), (deep(s)[:, 1:2], src[:, 1:2])]
                else:
                    wm = a["moe_w_gate" if kind == "g" else "moe_w_up"][0]
                    src = wm[bass.ds(e, 1), :, r * ROUND_F:(r + 1) * ROUND_F].rearrange("e (k p) n -> p (e k) n", p=P)
                    loads = halves(wide(s), src)
                load(loads, s)

            def moe_used(e, j):
                kind, r = MOE_ORDER[j]
                rr = r + DENSE_ROUNDS
                return ((down_ready, e * (MOE_ROUNDS * KT) + KT * (rr + 1)) if kind == "d"
                        else (gu_ready, e * (2 * MOE_ROUNDS) + 2 * (rr + 1)))

            for j in range(len(MOE_ORDER)):
                moe_load(0, j, plan[S_MOE + j - RING][1] if j < RING else moe_used(0, j - RING))
            with sp.Fori(1, N_EXPERTS) as e:
                for j in range(len(MOE_ORDER)):
                    before = moe_used(e, j - RING) if j >= RING else moe_used(e - 1, j - RING + len(MOE_ORDER))
                    moe_load(e, j, before)
            sp.wait_ge(rows_out, 2)
            sp.dma_start(out[0].rearrange("(t p) n -> p t n", p=P),
                         hT[:, 0:4, :].rearrange("p (t k) n -> p t (k n)", t=2)).then_inc(out_done, 16)
            sp.wait_ge(out_done, 16)


        class Link:

            def __init__(self, eng, chain):
                self.eng, self.chain, self.n, self.phases, self.told = eng, chain, 0, 0, {}

            def __call__(self, ins):
                self.n += 1
                ins.then_inc(self.chain, 1)
                self.eng.wait_ge(self.chain, self.n)

            def end_phase(self):
                self.phases += 1
                self.eng.drain().then_inc(phase, 1)
                self.eng.wait_ge(phase, 4 * self.phases)

        STEP_TILES = [(0, 1), (1, 0), (2, 3), (3, 2)]
        GROUPS = [(g, g // 2, slice(3 * g, 3 * g + 3)) for g in range(4)]

        def col(q):
            return q // DN_HEADS * DN_HEADS + q % PAIRS * 2 + q // PAIRS % 2

        def cols3(g):
            return slice(col(3 * g), col(3 * g) + 2 * PAIRS - 1, 2)

        ended = []

        def three(b):
            return ps[b][:, 0:3 * P].rearrange("p (a b) -> p a b", a=3)

        def six(b):
            return ps[b][:, 0:DN_HEADS * HEAD].rearrange("p (a b) -> p a b", a=DN_HEADS)

        def seg(ap, lo):
            return ap[:, lo:N_TOK].rearrange("p (s t) -> p s t", t=SEQ)

        def mask(col, n=3):
            return con[:, col:col + P].unsqueeze(1).to_broadcast([P, n, P])

        def over(ap, n):
            return ap.unsqueeze(2).to_broadcast([P, ap.shape[1], n])

        def jobs(layer):
            lat = [(1, i, h, t) for i in range(SW_TILES) for h in range(2) for t in range(2)]
            return lat if layer == N_LAYERS - 1 else lat + [(0,) + j[1:] for j in lat]

        ATT_BASE = [0, len(jobs(0))]

        def read_before(n):
            kinds = ["abv"] * 2 + [k for k, _ in in_tiles]
            mine = ("z", "q", "k")
            per = [sum(k not in mine for k in kinds), sum(k in mine for k in kinds)]
            who = kinds[n] in mine
            return (copy_done if who else conv_done), per[who], sum((k in mine) == who for k in kinds[:n + 1])

        def lvl_index(layer, i, lv, g):
            return ((layer * 4 + i) * (LEVELS - 1) + lv - 1) * 4 + g

        @block.tensor
        def _(pe):
            link = Link(pe, None)
            T = nc.tensor
            s = 0

            def full(s):
                pe.wait_ge(slot_full[s % RING], landed[s])

            def rms(lo):
                link.end_phase()
                for k in range(KT):
                    T.matmul(ps[0][:, lo:N_TOK], ones, hT[:, k, lo:N_TOK], start=(k == 0), stop=(k == KT - 1))
                link.end_phase()
                link.end_phase()
                link.end_phase()

            pe.wait_ge(setup_in, 16 * 6)
            tok = hT[:, :, :].rearrange("p (t k) n -> p t (k n)", t=TT)
            for k in range(KT):
                for t in range(TT):
                    T.transpose(ps[k][:, t * P:(t + 1) * P], tok[:, t, k * P:(k + 1) * P], ident)
            link.end_phase()
            link.end_phase()
            T.transpose(ps[0][:, 0:3 * KT], vrow2[0:3 * KT, :], ident[0:3 * KT, 0:3 * KT])
            link.end_phase()
            link.end_phase()

            def hyena(layer, lo):
                T.matmul(ps[0][0:HEAD, 0:SEQ], w12[0:33, 0:HEAD], hc[0:33, H_FEAT:H_FEAT + SEQ], start=True, stop=True)
                link.end_phase()
                link.end_phase()
                link.end_phase()
                T.matmul(ps[0][0:HEAD, 0:SEQ], w12[0:HEAD, HEAD:P], hh1[0:HEAD, :], start=True, stop=True)
                link.end_phase()
                link.end_phase()
                link.end_phase()
                for mt in range(2):
                    for d in range(2):
                        T.matmul(ps[2 * mt + d][:, :], hh2[0:HEAD + 1, mt * P:(mt + 1) * P],
                                 w3[0:HEAD + 1, d * 2 * HY_CH:(d + 1) * 2 * HY_CH], start=True, stop=True)
                link.end_phase()
                link.end_phase()
                link.end_phase()
                sq = [kre[:, 0], kre[:, 1], kim[:, 0], kim[:, 1]]
                for n in range(4):
                    T.matmul(ps[4][:, :], ones, sq[n], start=(n == 0), stop=(n == 3))
                link.end_phase()
                link.end_phase()

                def fourier(dst, tab, src, lo=0):
                    for f in range(2):
                        for t in range(2):
                            T.matmul(ps[dst + f][:, lo:N_TOK], hc[:, tab + t * SEQ + f * P:tab + t * SEQ + (f + 1) * P],
                                     src(t), start=(t == 0), stop=(t == 1))

                fourier(0, H_C, lambda t: kre[:, t])
                fourier(2, H_S, lambda t: kern[:, t, 1])
                link.end_phase()
                link.end_phase()
                for tt in range(2):
                    for st_ in range(lo // SEQ, 2):
                        for i in range(2):
                            tok0 = st_ * SEQ + tt * P
                            at = slice(st_ * SEQ + i * P, st_ * SEQ + (i + 1) * P)
                            T.transpose(ps[tt][:, at], hy[:, i, tok0:tok0 + P], ident)
                            T.transpose(ps[2 + tt][:, at], hy[:, 2 + i, tok0:tok0 + P], ident)
                link.end_phase()
                link.end_phase()
                for order in range(2):
                    fourier(0, H_C, lambda t: ut[:, t, lo:N_TOK], lo)
                    fourier(2, H_S, lambda t: ut[:, t, lo:N_TOK], lo)
                    link.end_phase()
                    link.end_phase()
                    for t in range(2):
                        if order == 0:
                            for n, (tab, src) in enumerate([(H_CT, pre), (H_ST, pim)]):
                                for f in range(2):
                                    c = tab + f * SEQ + t * P
                                    T.matmul(ps[t][:, lo:N_TOK], hc[:, c:c + P], src[:, f, lo:N_TOK],
                                             start=(n + f == 0), stop=(n + f == 2))
                        else:
                            for st_ in range(lo // SEQ, 2):
                                for n, (tab, src) in enumerate([(H_CT, pre), (H_ST, pim)]):
                                    for f in range(2):
                                        c = st_ * SEQ + t * P
                                        T.matmul(ps[t][:, st_ * SEQ:(st_ + 1) * SEQ], src[:, f, c:c + P],
                                                 hc[:, tab + f * SEQ:tab + (f + 1) * SEQ],
                                                 start=(n + f == 0), stop=(n + f == 2))
                    link.end_phase()
                    link.end_phase()

            def attention(layer):
                for i in range(4):
                    src = qT[:, i, SEQ:N_TOK] if i < SW_TILES else kT[:, SEQ:N_TOK]
                    T.matmul(ps[i // 2][:, i % 2 * SEQ:(i % 2 + 1) * SEQ], con[:, K_ROT:K_ROT + P], src,
                             start=True, stop=True)
                link.end_phase()
                link.end_phase()
                base, todo = ATT_BASE[layer], jobs(layer)

                def scores(n):
                    lat, i, half, qt = todo[n]
                    rows_ = slice(half * HEAD, (half + 1) * HEAD)
                    if n >= 2:
                        pe.wait_ge(score_read, base + n - 1)
                    q0 = lat * SEQ + qt * P
                    keys = N_TOK if lat else SEQ
                    T.matmul(ps[n % 2][:, 0:keys], qT[rows_, i, q0:q0 + P], kT[rows_, 0:keys],
                             start=True, stop=True).then_inc(score_ready, 1)

                def turns(n):
                    pe.wait_ge(prob_ready, base + n + 1)
                    if n >= 2:
                        pe.wait_ge(turn_read, base + n - 1)
                    for kt_ in range(4 if todo[n][0] else 2):
                        last = T.transpose(ps[2 + n % 2][:, kt_ * P:(kt_ + 1) * P], sc[:, n % 2, kt_ * P:(kt_ + 1) * P],
                                           ident)
                    last.then_inc(turn_ready, 1)

                def values(n):
                    lat, i, half, qt = todo[n]
                    rows_ = slice(half * HEAD, (half + 1) * HEAD)
                    nk = 4 if lat else 2
                    pe.wait_ge(turn_read, base + n + 1)
                    if n >= 2:
                        pe.wait_ge(pv_read, base + n - 1)
                    for kt_ in range(nk):
                        last = T.matmul(ps[4 + n % 2][rows_, 0:P], abv[:, kt_, 24 + half * HEAD:24 + (half + 1) * HEAD],
                                        pT[:, n % 2, kt_ * P:(kt_ + 1) * P], start=(kt_ == 0), stop=(kt_ == nk - 1))
                    last.then_inc(pv_ready, 1)

                for it in range(len(todo) + 2):
                    if it < len(todo):
                        scores(it)
                    if 1 <= it <= len(todo):
                        turns(it - 1)
                    if it >= 2:
                        values(it - 2)
                link.end_phase()

            def delta(layer, lo):
                link.end_phase()
                for i in range(6):
                    T.matmul(ps[i][:, :], blk, XT_flat(i), start=True, stop=True)
                link.end_phase()
                link.end_phase()
                link.end_phase()
                for t in range(TT):
                    for kind in range(2):
                        for i in range(PAIRS):
                            T.transpose(ps[2 * t + kind][:, i * P:(i + 1) * P],
                                        qkv[:, (kind + 1) * PAIRS + i, t * P:(t + 1) * P], ident)
                link.end_phase()
                link.end_phase()
                for t in range(TT):
                    for d in range(DIRS):
                        c = t * PROBS + d * DN_HEADS
                        T.matmul(ps[0][:, c:c + DN_HEADS], con[:, K_INC + d * P:K_INC + (d + 1) * P],
                                 gt[:, t, d * DN_HEADS:(d + 1) * DN_HEADS], start=True, stop=True)
                link.end_phase()
                link.end_phase()
                for i in range(4):
                    want_o = not (layer == N_LAYERS - 1 and i < 2)
                    for g, d, qs in GROUPS:
                        for n, q in enumerate(range(3 * g, 3 * g + 3)):
                            tile = STEP_TILES[i][d]
                            T.matmul(ps[g][:, n * P:(n + 1) * P], gt[:, tile, col(q):col(q) + 1].to_broadcast([P, P]),
                                     con[:, K_INC + d * P:K_INC + (d + 1) * P], start=True, stop=True)
                    for d in range(DIRS):
                        tile = STEP_TILES[i][d]
                        for j in range(PAIRS):
                            for half in range(2):
                                q = d * DN_HEADS + 2 * j + half
                                r_ = slice(half * HEAD, (half + 1) * HEAD)
                                T.matmul(ps[4 + d][r_, j * P:(j + 1) * P], gt[:, tile, q:q + 1].to_broadcast([P, HEAD]),
                                         con[:, K_INC + d * P:K_INC + (d + 1) * P], start=True, stop=True)
                                T.matmul(ps[6 + d][r_, j * P:(j + 1) * P], bt[:, tile, q:q + 1].to_broadcast([P, HEAD]),
                                         ident, start=True, stop=True)
                    link.end_phase()
                    link.end_phase()
                    for g, d, qs in GROUPS:
                        for n, q in enumerate(range(3 * g, 3 * g + 3)):
                            h = col(q) % DN_HEADS
                            rows_ = slice(h % 2 * HEAD, (h % 2 + 1) * HEAD)
                            cols = slice(STEP_TILES[i][d] * P, (STEP_TILES[i][d] + 1) * P)
                            k_ = qkv[rows_, PAIRS + h // 2, cols]
                            T.matmul(ps[g][:, n * P:(n + 1) * P], k_, kb[rows_, d * PAIRS + h // 2, :],
                                     start=True, stop=True)
                            T.matmul(ps[4 + g][:, n * P:(n + 1) * P], k_, qkv[rows_, h // 2, cols],
                                     start=True, stop=True)
                    link.end_phase()
                    link.end_phase()
                    link.end_phase()
                    for g, d, qs in GROUPS:
                        for n, q in enumerate(range(3 * g, 3 * g + 3)):
                            T.transpose(ps[g][:, n * P:(n + 1) * P], XT[:, q, :], ident)
                    link.end_phase()
                    link.end_phase()
                    for lv in range(1, LEVELS):
                        for g, d, qs in GROUPS:
                            ix = lvl_index(layer, i, lv, g)
                            pe.wait_ge(am_ready, ix + 1)
                            if lv > 1:
                                pe.wait_ge(x_done, ix - 3)
                            for n, q in enumerate(range(3 * g, 3 * g + 3)):
                                last = T.matmul(ps[g][:, n * P:(n + 1) * P], Am[:, q, :], Xm[:, q, :],
                                                start=True, stop=True)
                            last.then_inc(b_ready, 1)
                        for g, d, qs in GROUPS:
                            ix = lvl_index(layer, i, lv, g)
                            pe.wait_ge(b_copied, ix + 1)
                            if g >= 2:
                                pe.wait_ge(x_done, ix - 1)
                            for n, q in enumerate(range(3 * g, 3 * g + 3)):
                                if lv < LEVELS - 1:
                                    T.matmul(ps[4 + g % 2 * 2][:, n * P:(n + 1) * P], XT[:, q, :], Bm[:, q, :],
                                             start=True, stop=True)
                                last = T.matmul(ps[5 + g % 2 * 2][:, n * P:(n + 1) * P], Bm[:, q, :], XT[:, q, :],
                                                start=True, stop=True)
                            last.then_inc(p_ready, 1)
                    link.end_phase()
                    for d in range(DIRS):
                        cols = slice(STEP_TILES[i][d] * P, (STEP_TILES[i][d] + 1) * P)
                        for j in range(PAIRS):
                            T.matmul(ps[d][:, j * P:(j + 1) * P], qkv[:, PAIRS + j, cols], state[:, d * PAIRS + j, :],
                                     start=True, stop=True)
                    link.end_phase()
                    link.end_phase()
                    for q in range(PROBS):
                        h = col(q) % DN_HEADS
                        T.matmul(ps[2 + q // DN_HEADS][:, h * HEAD:(h + 1) * HEAD], XT[:, q, :], rhs[:, col(q), :],
                                 start=True, stop=True)
                    link.end_phase()
                    link.end_phase()
                    for d in range(DIRS):
                        for j in range(PAIRS):
                            if want_o:
                                T.matmul(ps[4 + d][:, j * P:(j + 1) * P], state[:, d * PAIRS + j, :],
                                         qd[:, d * PAIRS + j, :], start=True, stop=False, skip_group_check=True)
                                for half in range(2):
                                    q = d * DN_HEADS + half * PAIRS + j
                                    T.matmul(ps[4 + d][half * HEAD:(half + 1) * HEAD, j * P:(j + 1) * P],
                                             vnew[:, col(q), :], QK[:, q, :], start=False, stop=True, skip_group_check=True)
                            q = d * DN_HEADS + 2 * j
                            T.matmul(ps[6 + d][:, j * P:(j + 1) * P], kd[:, d * PAIRS + j, :],
                                     vnew[:, q:q + 2, :].rearrange("p a b -> p (a b)"), start=True, stop=True)
                    link.end_phase()
                    link.end_phase()
                link.end_phase()
                for j in range(PAIRS):
                    T.matmul(ps[j][:, lo:N_TOK], blk, XT_flat(j)[:, lo:N_TOK], start=True, stop=True)
                link.end_phase()
                link.end_phase()
                link.end_phase()

            def gate_up(R, ft, sg, lo, first):
                if not first:
                    pe.wait_ge(act_ready, 2 * R + ft - 1)
                for which in range(2):
                    for k in range(KT):
                        last = T.matmul(ps[2 * ft + which][:, lo:N_TOK], wide(sg + which)[:, k, ft * P:(ft + 1) * P],
                                        hT[:, k, lo:N_TOK], start=(k == 0), stop=(k == KT - 1))
                last.then_inc(gu_ready, 1)

            def down(R, par, sd, lo, first):
                pe.wait_ge(act_ready, 2 * R + 2)
                for d in range(KT):
                    if not (first and d < 4):
                        pe.wait_ge(down_added, KT * R + d - 3)
                    for ft in range(2):
                        last = T.matmul(ps[4 + d % 4][:, lo:N_TOK], deep(sd)[:, ft, d * P:(d + 1) * P],
                                        act[:, par, ft, lo:N_TOK], start=(ft == 0), stop=(ft == 1))
                    last.then_inc(down_ready, 1)

            for layer in range(N_LAYERS):
                last_layer = layer == N_LAYERS - 1
                lo = SEQ if last_layer else 0
                pe.wait_ge(rows_in, ROW_LOADS * 16 * (layer + 1))
                T.transpose(ps[1][:, 0:V_END], vrow[0:V_END, :], ident[0:V_END, 0:V_END])
                for j in range(MOD_SLOTS):
                    full(s)
                    for half in range(2):
                        m = 2 * j + half
                        for k in range(KT):
                            last = T.matmul(ps[0][:, 2 * m:2 * m + 2], wide(s)[:, k, half * P:(half + 1) * P],
                                            cs[:, k, :], start=(k == 0), stop=(k == KT - 1))
                    last.then_inc(mod_ready, 1)
                    s += 1
                link.end_phase()
                link.end_phase()
                rms(0)
                for j in range(IN_SLOTS):
                    full(s)
                    for half in range(2):
                        n = 2 * j + half
                        if n - 2 >= len(in_tiles):
                            break
                        if j == 0:
                            for tt in range(2):
                                for k in range(KT):
                                    last = T.matmul(ps[half][:, tt * ABV:(tt + 1) * ABV],
                                                    hT[:, k, (2 * half + tt) * P:(2 * half + tt + 1) * P],
                                                    wide(s)[:, k, 0:ABV], start=(k == 0), stop=(k == KT - 1))
                        else:
                            t0 = lo if in_tiles[n - 2][0] in ("z", "hy", "q") else 0
                            if n >= 4:
                                who, per, upto = read_before(n - 4)
                                pe.wait_ge(who, layer * per + upto)
                            for k in range(KT):
                                last = T.matmul(ps[n % 4][:, t0:N_TOK], wide(s)[:, k, half * P:(half + 1) * P],
                                                hT[:, k, t0:N_TOK], start=(k == 0), stop=(k == KT - 1))
                        last.then_inc(proj_ready, 1)
                    s += 1
                link.end_phase()
                hyena(layer, lo)
                attention(layer)
                delta(layer, lo)
                for j in range(OUT_SLOTS):
                    full(s)
                    for half in range(2):
                        n = 2 * j + half
                        if n >= 4:
                            pe.wait_ge(mix_added, layer * KT + n - 3)
                        for k in range(KT):
                            last = T.matmul(ps[n % 4][:, lo:N_TOK], wide(s)[:, k, half * P:(half + 1) * P],
                                            hT[:, k, lo:N_TOK], start=(k == 0), stop=(k == KT - 1))
                        last.then_inc(mix_ready, 1)
                    s += 1
                link.end_phase()
                rms(lo)
                if not last_layer:
                    for r in range(DENSE_ROUNDS):
                        full(s)
                        full(s + 1)
                        for ft in range(2):
                            gate_up(r, ft, s, lo, r == 0)
                        s += 2
                        if r:
                            full(s)
                            down(r - 1, (r - 1) % 2, s, lo, r == 1)
                            s += 1
                    full(s)
                    down(DENSE_ROUNDS - 1, (DENSE_ROUNDS - 1) % 2, s, lo, False)
                    s += 1
                    link.end_phase()
                else:
                    pe.wait_ge(router_in, 16)
                    for t in range(2):
                        for k in range(KT):
                            T.matmul(ps[0][:, 8 * t:8 * t + 8], hT[:, k, SEQ + t * P:SEQ + (t + 1) * P],
                                     wr[:, k, :], start=(k == 0), stop=(k == KT - 1))
                    link.end_phase()
                    link.end_phase()
                    link.end_phase()
                    link.end_phase()
                    for e in range(N_EXPERTS):
                        for t in range(2):
                            T.matmul(ps[e // 2][:, (e % 2) * SEQ + t * P:(e % 2) * SEQ + (t + 1) * P],
                                     gate[:, t, e:e + 1].to_broadcast([P, P]), ident, start=True, stop=True)
                    link.end_phase()
                    link.end_phase()
                    with pe.Fori(0, N_EXPERTS) as e:
                        def full_moe(j):
                            pe.wait_ge(slot_full[(S_MOE + j) % RING], e * MOE_INC + moe_landed(j))
                        j = 0
                        for r in range(MOE_ROUNDS):
                            R = e * MOE_ROUNDS + (DENSE_ROUNDS + r)
                            full_moe(j)
                            full_moe(j + 1)
                            for ft in range(2):
                                gate_up(R, ft, S_MOE + j, lo, False)
                            j += 2
                            if r:
                                full_moe(j)
                                down(e * MOE_ROUNDS + (DENSE_ROUNDS + r - 1), (DENSE_ROUNDS + r - 1) % 2, S_MOE + j, lo,
                                     False)
                                j += 1
                        full_moe(j)
                        down(R, (DENSE_ROUNDS + MOE_ROUNDS - 1) % 2, S_MOE + j, lo, False)
                    link.end_phase()
            rms(SEQ)
            for k in range(KT):
                for t in range(2):
                    T.transpose(ps[k][:, t * P:(t + 1) * P], hT[:, k, SEQ + t * P:SEQ + (t + 1) * P], ident)
            link.end_phase()
            ended.append(link.phases)

        @block.scalar
        def _(ac):
            link = Link(ac, act_chain)
            A = nc.scalar

            def rms(lo):
                for k in range(4):
                    link(A.activation(hT[:, k, lo:N_TOK], xT[:, k, lo:N_TOK], ACT.Square))
                link.end_phase()
                link.end_phase()
                link(A.activation(rms_s[:, lo:N_TOK], ps[0][:, lo:N_TOK], ACT.Sqrt, scale=1.0 / D_MODEL,
                                  bias=eps_col))
                link.end_phase()

            def modulated(which, lo, base):
                for k in range(KT):
                    ac.wait_ge(normed, base + k + 1)
                    for st_ in range(lo // SEQ, 2):
                        cols = slice(st_ * SEQ, (st_ + 1) * SEQ)
                        link(A.activation(hT[:, k, cols], hT[:, k, cols], ACT.Identity,
                                          scale=amul[:, which, k, st_:st_ + 1],
                                          bias=mod[:, 3 * which * KT + k, st_:st_ + 1]))
                link.end_phase()

            link.end_phase()
            for k in range(4, KT):
                link(A.copy(xT[:, k, :], ps[k][:, :]))
            link.end_phase()
            link.end_phase()
            link(A.copy(vcol2[:, :], ps[0][:, 0:3 * KT]))
            for st_ in range(2):
                link(A.activation(cs[:, :, st_], vcol2[:, st_ * KT:(st_ + 1) * KT], ACT.Silu))
            link.end_phase()

            def hyena(lo):
                for dst in (hh1, hh2):
                    link.end_phase()
                    link.end_phase()
                    link(A.activation(dst[0:HEAD, :], htmp[0:HEAD, :], ACT.Sin))
                    link.end_phase()
                link.end_phase()
                link.end_phase()
                sq = [kre[:, 0], kre[:, 1], kim[:, 0], kim[:, 1]]
                for n in range(4):
                    link(A.activation(sq[n], kern[:, n // 2, n % 2, :], ACT.Square))
                link.end_phase()
                link.end_phase()
                link(A.activation(hnorm[:, :], ps[4][:, :], ACT.Sqrt, bias=eps_col))
                link.end_phase()
                link.end_phase()
                link.end_phase()
                link.end_phase()
                for t in range(2):
                    link(A.copy(ut[:, t, lo:N_TOK], ps[t][:, lo:N_TOK]))
                link.end_phase()
                for _ in range(8):
                    link.end_phase()

            def attention(layer):
                link.end_phase()
                link.end_phase()
                base, todo = ATT_BASE[layer], jobs(layer)

                def exps(n):
                    lat, i, half, qt = todo[n]
                    keys = N_TOK if lat else SEQ
                    b = n % 2
                    h = i + SW_TILES * half
                    ac.wait_ge(max_ready, base + n + 1)
                    link(A.activation(st[:, b, 2:3], rows[:, 24 + h:25 + h], ACT.Exp, bias=st[:, b, 0:1]))
                    A.activation(sc[:, b, 0:keys], sc[:, b, 0:keys], ACT.Exp, bias=st[:, b, 0:1],
                                 accum_out=st[:, b, 1:2]).then_inc(exp_ready, 1)
                    ac.wait_ge(exp_ready, base + n + 1)

                def copies(n):
                    nk = 4 if todo[n][0] else 2
                    ac.wait_ge(turn_ready, base + n + 1)
                    if n >= 2:
                        ac.wait_ge(pv_ready, base + n - 1)
                    A.copy(pT[:, n % 2, 0:nk * P], ps[2 + n % 2][:, 0:nk * P]).then_inc(turn_read, 1)
                    ac.wait_ge(turn_read, base + n + 1)

                for it in range(len(todo) + 1):
                    if it < len(todo):
                        exps(it)
                    if it:
                        copies(it - 1)
                link.end_phase()

            def delta(layer, lo):
                for i in range(6):
                    link(A.activation(XT_flat(i), qkv[:, i, :], ACT.Square))
                link(A.activation(bt[:, :, :], abv[:, :, 12:24], ACT.Sigmoid))
                link.end_phase()
                link.end_phase()
                for i in range(6):
                    link(A.activation(XT_flat(i), ps[i][:, :], ACT.Sqrt, bias=eps_col))
                link(A.activation(gtmp[:, :, :], gtmp[:, :, :], ACT.Exp, scale=-1.0))
                link(A.activation(gtmp2[:, :, :], gtmp[:, :, :], ACT.Ln, bias=one_col))
                link(A.activation(rows[:, 0:12], rows[:, 0:12], ACT.Exp))
                link.end_phase()
                link.end_phase()
                link.end_phase()
                for t in range(TT):
                    link(A.copy(ktok[:, t, :], ps[2 * t][:, 0:3 * P]))
                link.end_phase()
                link.end_phase()
                link(A.copy(gc[:, :, :].rearrange("p a b -> p (a b)"), ps[0][:, 0:TT * PROBS]))
                link(A.activation(eg[:, :, :], gc[:, :, :], ACT.Exp))
                link.end_phase()
                for i in range(4):
                    link.end_phase()
                    for d in range(DIRS):
                        link(A.activation(egb[:, d * PAIRS:(d + 1) * PAIRS, :], three(4 + d), ACT.Exp))
                    link.end_phase()
                    link(A.activation(kds[:, :], kds[:, :], ACT.Exp))
                    for g, d, qs in GROUPS:
                        link(A.activation(Amat[:, qs, :], Amat[:, qs, :], ACT.Exp))
                    link.end_phase()
                    link.end_phase()
                    link.end_phase()
                    link.end_phase()
                    for g in range(2):
                        link(A.copy(Xm[:, 3 * g:3 * g + 3, :], three(g)))
                    link.end_phase()
                    for lv in range(1, LEVELS):
                        for g, d, qs in GROUPS:
                            ix = lvl_index(layer, i, lv, g)
                            ac.wait_ge(b_ready, ix + 1)
                            if lv > 1:
                                ac.wait_ge(p_ready, ix - 3)
                            A.copy(Bm[:, qs, :], three(g)).then_inc(b_copied, 1)
                            ac.wait_ge(b_copied, ix + 1)
                    link.end_phase()
                    link.end_phase()
                    link.end_phase()
                    link.end_phase()
                    for d in range(DIRS):
                        link(A.copy(vnew[:, d * DN_HEADS:(d + 1) * DN_HEADS, :], six(2 + d)))
                    link.end_phase()
                    link.end_phase()
                    link.end_phase()
                for j in range(PAIRS):
                    link(A.activation(XT_flat(j)[:, lo:N_TOK], hT[:, j, lo:N_TOK], ACT.Square))
                link.end_phase()
                link.end_phase()
                for j in range(PAIRS):
                    link(A.activation(XT_flat(j)[:, lo:N_TOK], ps[j][:, lo:N_TOK], ACT.Sqrt, scale=1.0 / HEAD,
                                      bias=eps_col))
                link.end_phase()
                link.end_phase()

            def silus(R, ft, lo, first):
                ac.wait_ge(gu_ready, 2 * R + ft + 1)
                if not first:
                    ac.wait_ge(act_ready, 2 * R + ft - 1)
                A.activation(sil[:, ft, lo:N_TOK], ps[2 * ft][:, lo:N_TOK], ACT.Silu).then_inc(sil_ready, 1)

            n_normed = 0
            for layer in range(N_LAYERS):
                last_layer = layer == N_LAYERS - 1
                lo = SEQ if last_layer else 0
                link.end_phase()
                link.end_phase()
                rms(0)
                modulated(0, 0, n_normed)
                n_normed += KT
                kinds = ["abv"] * 2 + [k for k, _ in in_tiles]
                for n in range(2, len(kinds)):
                    kind, i = in_tiles[n - 2]
                    if kind == "hy":
                        continue
                    if kind == "dn":
                        who, per, upto = read_before(n)
                        ac.wait_ge(who, layer * per + upto)
                        link(A.activation(qkv[:, i, :], qkv[:, i, :], ACT.Silu))
                        continue
                    ac.wait_ge(proj_ready, layer * len(kinds) + n + 1)
                    _, per, upto = read_before(n)
                    if kind == "z":
                        A.activation(zz[:, i, lo:N_TOK], ps[n % 4][:, lo:N_TOK], ACT.Silu).then_inc(copy_done, 1)
                    elif kind == "q":
                        A.copy(qT[:, i, lo:N_TOK], ps[n % 4][:, lo:N_TOK]).then_inc(copy_done, 1)
                    else:
                        A.copy(kT[:, :], ps[n % 4][:, :]).then_inc(copy_done, 1)
                    ac.wait_ge(copy_done, layer * per + upto)
                link.end_phase()
                hyena(lo)
                attention(layer)
                delta(layer, lo)
                link.end_phase()
                rms(lo)
                modulated(1, lo, n_normed)
                n_normed += KT
                if not last_layer:
                    for r in range(DENSE_ROUNDS):
                        for ft in range(2):
                            silus(r, ft, lo, r == 0)
                    link.end_phase()
                else:
                    link.end_phase()
                    link.end_phase()
                    link(A.activation(tmp8[:, :, 0:1], tmp8[:, :, 0:1], ACT.Exp))
                    link.end_phase()
                    link.end_phase()
                    link.end_phase()
                    for e2 in range(2):
                        link(A.copy(geb[:, 2 * e2:2 * e2 + 2, :], ps[e2][:, :].rearrange("p (a b) -> p a b", a=2)))
                    link.end_phase()
                    with ac.Fori(0, N_EXPERTS) as e:
                        for r in range(MOE_ROUNDS):
                            for ft in range(2):
                                silus(e * MOE_ROUNDS + (DENSE_ROUNDS + r), ft, lo, False)
                    link.end_phase()
            rms(SEQ)
            for k in range(KT):
                ac.wait_ge(normed, n_normed + k + 1)
                link(A.activation(hT[:, k, SEQ:N_TOK], hT[:, k, SEQ:N_TOK], ACT.Copy,
                                  scale=vcol2[:, 2 * KT + k:2 * KT + k + 1]))
            link.end_phase()
            link.end_phase()
            for k in range(4):
                for t in range(2):
                    link(A.copy(hT[:, 2 * t + k // 4, k % 4 * P:(k % 4 + 1) * P], ps[k][:, t * P:(t + 1) * P]))
            ac.drain().then_inc(rows_out, 1)
            ended.append(link.phases)

        @block.vector
        def _(ve):
            link = Link(ve, dve_chain)
            V = nc.vector

            def tt(out, a_, b_, op):
                link(V.tensor_tensor(out, a_, b_, op))

            def rms(lo, base):
                for k in range(4, KT):
                    tt(hT[:, k, lo:N_TOK], xT[:, k, lo:N_TOK], xT[:, k, lo:N_TOK], ALU.mult)
                link.end_phase()
                link.end_phase()
                link.end_phase()
                link(V.reciprocal(rms_r[:, lo:N_TOK], rms_s[:, lo:N_TOK]))
                for k in range(KT):
                    V.tensor_tensor(hT[:, k, lo:N_TOK], xT[:, k, lo:N_TOK], rms_r[:, lo:N_TOK],
                                    ALU.mult).then_inc(normed, 1)
                link.end_phase()

            link(V.memset(eps_col, RMS_EPS))
            link(V.memset(one_col, 1.0))
            link.end_phase()
            for k in range(4):
                link(V.tensor_copy(xT[:, k, :], ps[k][:, :]))
            link.end_phase()
            link.end_phase()
            link.end_phase()

            def conv(dst, src, lo, w, j0, j, n):
                d3, s3 = seg(dst, lo), seg(src, lo)
                link(V.tensor_scalar(dst[:, lo:N_TOK], src[:, lo:N_TOK], vcol[:, w + n + j:w + n + j + 1], None, ALU.mult))
                link(V.scalar_tensor_tensor(out=d3[:, :, 1:SEQ], in0=s3[:, :, 0:SEQ - 1], scalar=vcol[:, w + j:w + j + 1],
                                            in1=d3[:, :, 1:SEQ], op0=ALU.mult, op1=ALU.add))
                return V.scalar_tensor_tensor(out=d3[:, :, 0:SEQ - 1], in0=s3[:, :, 1:SEQ],
                                              scalar=vcol[:, w + 2 * n + j:w + 2 * n + j + 1],
                                              in1=d3[:, :, 0:SEQ - 1], op0=ALU.mult, op1=ALU.add)

            def hyena(lo):
                for layer_b, layer_f in ((V_B1, V_FR1), (V_B2, V_FR2)):
                    link.end_phase()
                    h, n = htmp[0:HEAD, :], htmp2[0:HEAD, :]
                    link(V.tensor_scalar(h, ps[0][0:HEAD, 0:SEQ], vcol[0:HEAD, layer_b:layer_b + 1],
                                         vcol[0:HEAD, layer_f:layer_f + 1], ALU.add, ALU.mult))
                    link(V.tensor_scalar(n, h, 1.0 / (2 * np.pi), None, ALU.mult))
                    link(V.tensor_scalar(n, n, ROUND, None, ALU.add))
                    link(V.tensor_scalar(n, n, -ROUND, None, ALU.add))
                    for part in TWO_PI:
                        link(V.scalar_tensor_tensor(out=h, in0=n, scalar=-part, in1=h, op0=ALU.mult, op1=ALU.add))
                    link(V.tensor_scalar(h, h, PI_BELOW, -PI_BELOW, ALU.min, ALU.max))
                    link.end_phase()
                    link.end_phase()
                link.end_phase()
                for mt in range(2):
                    for d in range(2):
                        w = hc[:, H_WIN + (2 * mt + d) * HY_CH:H_WIN + (2 * mt + d + 1) * HY_CH]
                        tt(kern[:, mt, d, :].rearrange("p (o c) -> p o c", o=2),
                           ps[2 * mt + d][:, :].rearrange("p (o c) -> p o c", o=2),
                           w.unsqueeze(1).to_broadcast([P, 2, HY_CH]), ALU.mult)
                link.end_phase()
                link.end_phase()
                link.end_phase()
                for mt in range(2):
                    tt(kre[:, mt], kern[:, mt, 0, :], kern[:, mt, 1, :], ALU.add)
                    tt(kern[:, mt, 1, :], kern[:, mt, 1, :], kern[:, mt, 0, :], ALU.subtract)
                link.end_phase()
                link(V.reciprocal(hnorm[:, :], hnorm[:, :]))
                link.end_phase()
                for f in range(2):
                    tt(kre[:, f], ps[f][:, :], hnorm[:, :], ALU.mult)
                    tt(kre[:, f], kre[:, f], hskip[:, :], ALU.add)
                    tt(kim[:, f], ps[2 + f][:, :], hnorm[:, :], ALU.mult)
                link.end_phase()
                link.end_phase()
                for t in range(2):
                    link(V.tensor_copy(x1t[:, t, lo:N_TOK], ps[2 + t][:, lo:N_TOK]))
                link.end_phase()
                for order in range(2):
                    link.end_phase()
                    for f in range(2):
                        o = slice(order * HY_CH, (order + 1) * HY_CH)
                        kr = kre[:, f, o].unsqueeze(1).to_broadcast([P, SEG(lo), HY_CH])
                        ki = kim[:, f, o].unsqueeze(1).to_broadcast([P, SEG(lo), HY_CH])
                        ur, us = seg(ps[f], lo), seg(ps[2 + f], lo)
                        pr, pi_, tm = seg(pre[:, f], lo), seg(pim[:, f], lo), seg(ptmp, lo)
                        tt(pr, ur, kr, ALU.mult)
                        tt(tm, us, ki, ALU.mult)
                        tt(pr, pr, tm, ALU.add)
                        tt(pi_, ur, ki, ALU.mult)
                        tt(tm, us, kr, ALU.mult)
                        tt(pi_, pi_, tm, ALU.subtract)
                    link.end_phase()
                    link.end_phase()
                    for t in range(2):
                        if order == 0:
                            tt(ut[:, t, lo:N_TOK], ps[t][:, lo:N_TOK], x1t[:, t, lo:N_TOK], ALU.mult)
                        else:
                            tt(hT[:, PAIRS + t, lo:N_TOK], ps[t][:, lo:N_TOK], hy[:, 4 + t, lo:N_TOK], ALU.mult)
                    link.end_phase()

            def attention(layer):
                link.end_phase()
                for i in range(4):
                    x_ = qT[:, i, SEQ:N_TOK] if i < SW_TILES else kT[:, SEQ:N_TOK]
                    tt(rot[:, i, :], ps[i // 2][:, i % 2 * SEQ:(i % 2 + 1) * SEQ], con[:, K_SIN:K_SIN + SEQ], ALU.mult)
                    tt(x_, x_, con[:, K_COS:K_COS + SEQ], ALU.mult)
                    tt(x_, x_, rot[:, i, :], ALU.add)
                link.end_phase()
                base, todo = ATT_BASE[layer], jobs(layer)

                def maxima(n):
                    lat, i, half, qt = todo[n]
                    keys = N_TOK if lat else SEQ
                    b = n % 2
                    h = i + SW_TILES * half
                    ve.wait_ge(score_ready, base + n + 1)
                    if n >= 2:
                        ve.wait_ge(turn_ready, base + n - 1)
                    if lat:
                        band = con[:, K_BAND + qt * N_TOK:K_BAND + (qt + 1) * N_TOK]
                        V.scalar_tensor_tensor(out=sc[:, b, :], in0=ps[b][:, :], scalar=HEAD ** -0.5, in1=band,
                                               op0=ALU.mult, op1=ALU.add).then_inc(score_read, 1)
                    else:
                        V.tensor_scalar(sc[:, b, 0:keys], ps[b][:, 0:keys], HEAD ** -0.5, None,
                                        ALU.mult).then_inc(score_read, 1)
                    ve.wait_ge(score_read, base + n + 1)
                    link(V.tensor_reduce(st[:, b, 3:4], sc[:, b, 0:keys], X_AXIS, ALU.max))
                    V.tensor_scalar(st[:, b, 0:1], st[:, b, 3:4], rows[:, 24 + h:25 + h], -1.0, ALU.max,
                                    ALU.mult).then_inc(max_ready, 1)

                def divide(n):
                    b = n % 2
                    keys = N_TOK if todo[n][0] else SEQ
                    ve.wait_ge(exp_ready, base + n + 1)
                    tt(st[:, b, 4:5], st[:, b, 1:2], st[:, b, 2:3], ALU.add)
                    link(V.reciprocal(st[:, b, 5:6], st[:, b, 4:5]))
                    V.tensor_scalar(sc[:, b, 0:keys], sc[:, b, 0:keys], st[:, b, 5:6], None,
                                    ALU.mult).then_inc(prob_ready, 1)

                def outputs(n):
                    lat, i, half, qt = todo[n]
                    rows_ = slice(half * HEAD, (half + 1) * HEAD)
                    ve.wait_ge(pv_ready, base + n + 1)
                    q0 = lat * SEQ + qt * P
                    V.tensor_copy(hT[rows_, PAIRS + 2 + i, q0:q0 + P], ps[4 + n % 2][rows_, 0:P]).then_inc(pv_read, 1)

                for it in range(len(todo) + 2):
                    if it < len(todo):
                        maxima(it)
                    if 1 <= it <= len(todo):
                        divide(it - 1)
                    if it >= 2:
                        outputs(it - 2)
                link.end_phase()

            def delta(layer, lo):
                dtb = rows[:, 12:24].unsqueeze(1).to_broadcast([P, TT, PROBS])
                tt(gt[:, :, :], abv[:, :, 0:12], dtb, ALU.add)
                link(V.tensor_scalar(gtmp2[:, :, :], gt[:, :, :], -1.0, None, ALU.mult))
                tt(gtmp[:, :, :], gt[:, :, :], gtmp2[:, :, :], ALU.max)
                link.end_phase()
                link.end_phase()
                link.end_phase()
                link(V.tensor_scalar(gc[:, :, :], gtmp[:, :, :], 1.0, None, ALU.add))
                link(V.tensor_scalar(gc[:, :, :], gc[:, :, :], -1.0, None, ALU.add))
                link(V.tensor_scalar(gc[:, :, :], gc[:, :, :], TINY, None, ALU.add))
                link(V.reciprocal(eg[:, :, :], gc[:, :, :]))
                link(V.tensor_scalar(gtmp2[:, :, :], gtmp2[:, :, :], TINY, None, ALU.add))
                tt(gtmp2[:, :, :], gtmp2[:, :, :], eg[:, :, :], ALU.mult)
                tt(gtmp2[:, :, :], gtmp2[:, :, :], gtmp[:, :, :], ALU.mult)
                link(V.scalar_tensor_tensor(out=gt[:, :, :], in0=gt[:, :, :], scalar=0.0, in1=gtmp2[:, :, :],
                                            op0=ALU.max, op1=ALU.add))
                link(V.scalar_tensor_tensor(out=gt[:, :, :], in0=gt[:, :, :], scalar=-1.0,
                                            in1=rows[:, 0:12].unsqueeze(1).to_broadcast([P, TT, PROBS]),
                                            op0=ALU.mult, op1=ALU.mult))
                for i in range(6):
                    link(V.reciprocal(XT_flat(i), XT_flat(i)))
                    link(V.scalar_tensor_tensor(out=qkv[:, i, :], in0=qkv[:, i, :], scalar=(HEAD ** -0.5 if i < 3 else 1.0),
                                                in1=XT_flat(i), op0=ALU.mult, op1=ALU.mult))
                link.end_phase()
                link.end_phase()
                for t in range(TT):
                    link(V.tensor_copy(vtok[:, t, :], ps[2 * t + 1][:, 0:3 * P]))
                link.end_phase()
                link.end_phase()
                link.end_phase()
                for i in range(4):
                    link.end_phase()
                    for g, d, qs in GROUPS:
                        tile = STEP_TILES[i][d]
                        for n, q in enumerate(range(3 * g, 3 * g + 3)):
                            link(V.tensor_scalar(Amat[:, q, :], ps[g][:, n * P:(n + 1) * P], gc[:, tile, col(q):col(q) + 1], 0.0,
                                                 ALU.subtract, ALU.min))
                        end = P - 1 if d == 0 else 0
                        tt(kds[:, cols3(g)], three(g)[:, :, end:end + 1].rearrange("p a b -> p (a b)"),
                           gc[:, tile, cols3(g)],
                           ALU.subtract)
                    for d in range(DIRS):
                        cols = slice(STEP_TILES[i][d] * P, (STEP_TILES[i][d] + 1) * P)
                        tt(kb[:, d * PAIRS:(d + 1) * PAIRS, :], three(6 + d), qkv[:, PAIRS:2 * PAIRS, cols], ALU.mult)
                    link.end_phase()
                    for d in range(DIRS):
                        cols = slice(STEP_TILES[i][d] * P, (STEP_TILES[i][d] + 1) * P)
                        tt(qd[:, d * PAIRS:(d + 1) * PAIRS, :], egb[:, d * PAIRS:(d + 1) * PAIRS, :],
                           qkv[:, 0:PAIRS, cols], ALU.mult)
                    link.end_phase()
                    for g, d, qs in GROUPS:
                        tt(QK[:, qs, :], three(4 + g), Amat[:, qs, :], ALU.mult)
                        tt(Amat[:, qs, :], three(g), Amat[:, qs, :], ALU.mult)
                    link.end_phase()
                    for g, d, qs in GROUPS:
                        tt(XT[:, qs, :], Amat[:, qs, :], mask(K_LVL + d * LEVELS * P), ALU.mult)
                        tt(XT[:, qs, :], mask(K_ID), XT[:, qs, :], ALU.subtract)
                    link.end_phase()
                    link.end_phase()
                    for g in range(2, 4):
                        link(V.tensor_copy(Xm[:, 3 * g:3 * g + 3, :], three(g)))
                    link.end_phase()
                    for lv in range(1, LEVELS):
                        for g, d, qs in GROUPS:
                            ix = lvl_index(layer, i, lv, g)
                            ve.wait_ge(p_ready, ix + 1)
                            if lv < LEVELS - 1:
                                V.tensor_tensor(Xm[:, qs, :], Xm[:, qs, :], three(4 + g % 2 * 2), ALU.subtract)
                            V.tensor_tensor(XT[:, qs, :], XT[:, qs, :], three(5 + g % 2 * 2),
                                            ALU.subtract).then_inc(x_done, 1)
                            ve.wait_ge(x_done, ix + 1)
                    link.end_phase()
                    link.end_phase()
                    for d in range(DIRS):
                        tile = STEP_TILES[i][d]
                        qs = slice(d * DN_HEADS, (d + 1) * DN_HEADS)
                        tt(rhs[:, qs, :], six(d), over(eg[:, tile, qs], HEAD), ALU.mult)
                        tt(rhs[:, qs, :], vtok[:, tile, :].rearrange("p (a b) -> p a b", a=DN_HEADS), rhs[:, qs, :],
                           ALU.subtract)
                        tt(rhs[:, qs, :], rhs[:, qs, :], over(bt[:, tile, qs], HEAD), ALU.mult)
                    link.end_phase()
                    link.end_phase()
                    link.end_phase()
                    link.end_phase()
                    for d in range(DIRS):
                        end = P - 1 if d == 0 else 0
                        pd = slice(d * PAIRS, (d + 1) * PAIRS)
                        for half in range(2):
                            r_ = slice(half * HEAD, (half + 1) * HEAD)
                            tt(state[r_, pd, r_], state[r_, pd, r_],
                               egb[r_, pd, end:end + 1].to_broadcast([HEAD, PAIRS, HEAD]), ALU.mult)
                            tt(state[r_, pd, r_], three(6 + d)[r_, :, r_], state[r_, pd, r_], ALU.add)
                        tile = STEP_TILES[i][d]
                        o_ = hT[:, 0:PAIRS, tile * P:(tile + 1) * P]
                        if i % 2 == 0 and not (layer == N_LAYERS - 1 and i < 2):
                            link(V.tensor_copy(o_, three(4 + d)))
                        elif not (layer == N_LAYERS - 1 and i < 2):
                            tt(o_, three(4 + d), o_, ALU.add)
                    link.end_phase()
                link.end_phase()
                link.end_phase()
                link.end_phase()
                for j in range(PAIRS):
                    x_ = XT_flat(j)[:, lo:N_TOK]
                    link(V.reciprocal(x_, x_))
                    link(V.scalar_tensor_tensor(out=x_, in0=x_, scalar=vcol[:, V_DNG:V_DNG + 1], in1=zz[:, j, lo:N_TOK],
                                                op0=ALU.mult, op1=ALU.mult))
                    tt(hT[:, j, lo:N_TOK], hT[:, j, lo:N_TOK], x_, ALU.mult)
                link.end_phase()

            def gated(R, ft, par, lo, first, e=None):
                ve.wait_ge(sil_ready, 2 * R + ft + 1)
                if not first:
                    ve.wait_ge(down_ready, KT * (R - 1))
                if e is None:
                    V.tensor_tensor(act[:, par, ft, lo:N_TOK], sil[:, ft, lo:N_TOK], ps[2 * ft + 1][:, lo:N_TOK],
                                    ALU.mult).then_inc(act_ready, 1)
                else:
                    link_sil(V.tensor_tensor(act[:, par, ft, lo:N_TOK], sil[:, ft, lo:N_TOK],
                                             ps[2 * ft + 1][:, lo:N_TOK], ALU.mult), 2 * R + ft)
                    V.tensor_tensor(act[:, par, ft, lo:N_TOK], act[:, par, ft, lo:N_TOK],
                                    geb[:, bass.ds(e, 1), :].rearrange("p a b -> p (a b)"), ALU.mult).then_inc(act_ready, 1)

            def link_sil(ins, n):
                ins.then_inc(up_done, 1)
                ve.wait_ge(up_done, n - 2 * DENSE_ROUNDS + 1)

            def add_down(R, lo):
                for d in range(KT):
                    ve.wait_ge(down_ready, KT * R + d + 1)
                    for st_ in range(lo // SEQ, 2):
                        c = slice(st_ * SEQ, (st_ + 1) * SEQ)
                        last = V.scalar_tensor_tensor(out=xT[:, d, c], in0=ps[4 + d % 4][:, c],
                                                      scalar=mod[:, 5 * KT + d, st_:st_ + 1], in1=xT[:, d, c],
                                                      op0=ALU.mult, op1=ALU.add)
                    last.then_inc(down_added, 1)

            n_normed = 0
            for layer in range(N_LAYERS):
                last_layer = layer == N_LAYERS - 1
                lo = SEQ if last_layer else 0
                link.end_phase()
                link(V.tensor_copy(vcol[:, 0:V_END], ps[1][:, 0:V_END]))
                tt(mod[:, :, :], ps[0][:, 0:2 * N_MOD_TILES].rearrange("p (a b) -> p a b", b=2),
                   over(vcol[:, V_BMOD:V_BMOD + N_MOD_TILES], 2), ALU.add)
                for which, gcol in ((0, V_GMIX), (1, V_GFFN)):
                    m0 = (3 * which + 1) * KT
                    link(V.scalar_tensor_tensor(out=amul[:, which], in0=mod[:, m0:m0 + KT, :], scalar=1.0,
                                                in1=over(vcol[:, gcol:gcol + KT], 2), op0=ALU.add, op1=ALU.mult))
                link.end_phase()
                rms(0, n_normed)
                n_normed += KT
                kinds = ["abv"] * 2 + [k for k, _ in in_tiles]
                for n in range(len(kinds)):
                    if kinds[n] in ("z", "q", "k"):
                        continue
                    ve.wait_ge(proj_ready, layer * len(kinds) + n + 1)
                    _, per, upto = read_before(n)
                    if n < 2:
                        last = V.tensor_copy(abv[:, 2 * n:2 * n + 2, :],
                                             ps[n][:, 0:2 * ABV].rearrange("p (a b) -> p a b", a=2))
                    elif kinds[n] == "dn":
                        i = in_tiles[n - 2][1]
                        last = conv(qkv[:, i, :], ps[n % 4], 0, V_DNC, 0, i, DN_TILES)
                    else:
                        i = in_tiles[n - 2][1]
                        last = conv(hy[:, i, :], ps[n % 4], lo, V_HYC, 0, i, HY_TILES)
                    last.then_inc(conv_done, 1)
                    ve.wait_ge(conv_done, layer * per + upto)
                link.end_phase()
                hyena(lo)
                attention(layer)
                delta(layer, lo)
                for n in range(KT):
                    ve.wait_ge(mix_ready, layer * KT + n + 1)
                    for st_ in range(lo // SEQ, 2):
                        c = slice(st_ * SEQ, (st_ + 1) * SEQ)
                        last = V.scalar_tensor_tensor(out=xT[:, n, c], in0=ps[n % 4][:, c],
                                                      scalar=mod[:, 2 * KT + n, st_:st_ + 1], in1=xT[:, n, c],
                                                      op0=ALU.mult, op1=ALU.add)
                    last.then_inc(mix_added, 1)
                link.end_phase()
                rms(lo, n_normed)
                n_normed += KT
                if not last_layer:
                    for r in range(DENSE_ROUNDS):
                        for ft in range(2):
                            gated(r, ft, r % 2, lo, r < 2)
                        if r:
                            add_down(r - 1, lo)
                    add_down(DENSE_ROUNDS - 1, lo)
                    link.end_phase()
                else:
                    link.end_phase()
                    link(V.tensor_copy(lg[:, :, :], ps[0][:, 0:16].rearrange("p (a b) -> p a b", a=2)))
                    for t in range(2):
                        link(V.max(top[:, t, :], lg[:, t, :]))
                        link(V.max_index(topi[:, t, :], top[:, t, :], lg[:, t, :]))
                    link(V.tensor_copy(tix[:, :, :], topi[:, :, :]))
                    tt(tmp8[:, :, 0:1], top[:, :, 1:2], top[:, :, 0:1], ALU.subtract)
                    link.end_phase()
                    link.end_phase()
                    link(V.tensor_scalar(tmp8[:, :, 1:2], tmp8[:, :, 0:1], 1.0, None, ALU.add))
                    link(V.reciprocal(tmp8[:, :, 2:3], tmp8[:, :, 1:2]))
                    tt(tmp8[:, :, 3:4], tmp8[:, :, 2:3], tmp8[:, :, 0:1], ALU.mult)
                    for t in range(2):
                        for n in range(2):
                            link(V.tensor_scalar(top[:, t, :], con[:, K_IOTA:K_IOTA + 8], tix[:, t, n:n + 1],
                                                 tmp8[:, t, 2 + n:3 + n], ALU.is_equal, ALU.mult))
                            if n == 0:
                                link(V.tensor_copy(gate[:, t, :], top[:, t, :]))
                            else:
                                tt(gate[:, t, :], gate[:, t, :], top[:, t, :], ALU.add)
                    link.end_phase()
                    link.end_phase()
                    for e2 in range(2, 4):
                        link(V.tensor_copy(geb[:, 2 * e2:2 * e2 + 2, :], ps[e2][:, :].rearrange("p (a b) -> p a b", a=2)))
                    link.end_phase()
                    with ve.Fori(0, N_EXPERTS) as e:
                        for r in range(MOE_ROUNDS):
                            R = e * MOE_ROUNDS + (DENSE_ROUNDS + r)
                            for ft in range(2):
                                gated(R, ft, (DENSE_ROUNDS + r) % 2, lo, False, e)
                            if r:
                                add_down(e * MOE_ROUNDS + (DENSE_ROUNDS + r - 1), lo)
                        add_down(R, lo)
                    link.end_phase()
            rms(SEQ, n_normed)
            link.end_phase()
            for k in range(4, KT):
                for t in range(2):
                    link(V.tensor_copy(hT[:, 2 * t + k // 4, k % 4 * P:(k % 4 + 1) * P], ps[k][:, t * P:(t + 1) * P]))
            ve.drain().then_inc(rows_out, 1)
            ended.append(link.phases)

        @block.gpsimd
        def _(po):
            link = Link(po, pool_chain)
            G = nc.gpsimd
            link(G.memset(vrow[:, :], 0.0))
            for _ in range(4):
                link.end_phase()
            for layer in range(N_LAYERS):
                last_layer = layer == N_LAYERS - 1
                link(G.memset(hh2[HEAD:HEAD + 1, :], 1.0))
                for dst, src in row_loads(layer):
                    po.dma_start(dst, src).then_inc(rows_in, 16)
                n_before = 2 + 4 + 1
                for _ in range(n_before + HY_PHASES + 3):
                    link.end_phase()
                link(G.memset(state[:, :, :], 0.0))
                for _ in range(8):
                    link.end_phase()
                for i in range(4):
                    link.end_phase()
                    link.end_phase()
                    link.end_phase()
                    for d in range(DIRS):
                        tile = STEP_TILES[i][d]
                        qs = slice(d * DN_HEADS, (d + 1) * DN_HEADS)
                        link(G.tensor_tensor(kd[:, d * PAIRS:(d + 1) * PAIRS, :].rearrange("p a (b c) -> p (a b) c", b=2),
                                             ktok[:, tile, :].rearrange("p (a b) -> p a b", a=DN_HEADS),
                                             over(kds[:, qs], HEAD), ALU.mult))
                    link.end_phase()
                    for g, d, qs in GROUPS:
                        link(G.tensor_tensor(QK[:, qs, :], QK[:, qs, :], mask(K_INC + d * P), ALU.mult))
                    link.end_phase()
                    link.end_phase()
                    link.end_phase()
                    for lv in range(1, LEVELS):
                        for g, d, qs in GROUPS:
                            ix = lvl_index(layer, i, lv, g)
                            if lv > 1:
                                po.wait_ge(b_ready, ix - 3)
                            G.tensor_tensor(Am[:, qs, :], Amat[:, qs, :], mask(K_LVL + (d * LEVELS + lv) * P),
                                            ALU.mult).then_inc(am_ready, 1)
                    for _ in range(7):
                        link.end_phase()
                for _ in range(4):
                    link.end_phase()
                link.end_phase()
                if last_layer:
                    po.dma_start(wr[:, :, :], a["moe_router"][0].rearrange("(k p) e -> p k e", p=P)).then_inc(router_in, 16)
                for _ in range(4):
                    link.end_phase()
                for _ in range(7 if last_layer else 1):
                    link.end_phase()
            for _ in range(5):
                link.end_phase()
            ended.append(link.phases)

        assert len(set(ended)) == 1, ended


_NAMES = ["x", "c", "ctx", "c_ctx", "w_mod", "b_mod", "norm_mix_g", "norm_ffn_g", "w_in", "dn_conv_w", "dn_a_log",
          "dn_dt_bias", "dn_norm_g", "hy_conv_w", "hy_w1", "hy_b1", "hy_freq1", "hy_w2", "hy_b2", "hy_freq2", "hy_w3",
          "hy_b3", "hy_skip", "sw_sink", "w_out", "ffn_w_gate", "ffn_w_up", "ffn_w_down", "moe_router", "moe_w_gate",
          "moe_w_up", "moe_w_down", "final_norm_g"]


def kernel(**inputs):
    import concourse.bacc as bacc
    from concourse.bass_utils import run_bass_kernel_spmd

    nc = bacc.Bacc("TRN2", target_bir_lowering=False, num_devices=1)
    arrays, aps = {}, {}
    k_con, k_hy = shape_constants()
    tensors = {n: np.ascontiguousarray(inputs[n]) for n in _NAMES}
    tensors["k_con"], tensors["k_hy"] = k_con, k_hy
    for name, t in tensors.items():
        arrays[f"in_{name}"] = t
        aps[name] = nc.dram_tensor(f"in_{name}", t.shape, mybir.dt.from_np(t.dtype), kind="ExternalInput").ap()
    out = nc.dram_tensor("out", (1, SEQ, D_MODEL), F32, kind="ExternalOutput").ap()
    build(nc, aps, out)
    r = run_bass_kernel_spmd(nc, [arrays], core_ids=[0])
    return r.results[0]["out"]
```

```python
from contextlib import ExitStack

import numpy as np

import concourse.bass as bass
from concourse import mybir

P = 128
ALU = mybir.AluOpType
ACT = mybir.ActivationFunctionType
F32 = mybir.dt.float32
U32 = mybir.dt.uint32
X_AXIS = mybir.AxisListType.X

D_MODEL = 1024
SEQ = 256
N_TOK = 2 * SEQ
N_LAYERS = 2
HEAD = 64
DN_HEADS = 6
SW_HEADS = 6
HY_CH = 256
FFN_DENSE = 2816
N_EXPERTS = 8
FFN_EXPERT = 3584
RMS_EPS = 1e-6
TINY = 1e-30
ROUND = 1.5 * 2.0 ** 23
TWO_PI = (6.28125, 1.9350051879882812e-3, 3.0199159795074593e-7)
PI_BELOW = 3.1415925
GRID_W = 64
SW_WINDOW = 128

KT = D_MODEL // P
TT = N_TOK // P
N_MOD_TILES = 6 * KT
PAIRS = DN_HEADS // 2
DIRS = 2
PROBS = DIRS * DN_HEADS
DN_TILES = 3 * PAIRS
HY_TILES = 3 * HY_CH // P
SW_TILES = SW_HEADS // 2
CHUNK = P
LEVELS = 7

C_DN, C_Z, C_A = 0, 1152, 1536
C_HY, C_Q, C_K, C_V = 1560, 2328, 2712, 2840
ABV = 24 + 2 * HEAD

SLOT = 2048
RING = 7
MOD_SLOTS = N_MOD_TILES // 2
IN_SLOTS = 12
OUT_SLOTS = KT // 2
ROUND_F = 2 * P
DENSE_ROUNDS = FFN_DENSE // ROUND_F
CAP = 128
EXTRA = 3
PASSES = N_EXPERTS + EXTRA
NARROW = 64
MOE_F = 4 * P
MOE_ROUNDS = FFN_EXPERT // MOE_F

(K_ID, K_ONE, K_BLK, K_INC, K_LVL, K_COS, K_SIN, K_ROT, K_BAND, K_IOTA, K_END) = np.cumsum(
    [0, P, P, P, 2 * P, 2 * LEVELS * P, SEQ, SEQ, P, 2 * N_TOK, P]).tolist()
(H_C, H_S, H_CT, H_ST, H_WIN, H_FEAT, H_END) = np.cumsum(
    [0, 2 * SEQ, 2 * SEQ, 2 * SEQ, 2 * SEQ, 2 * 2 * HY_CH, SEQ]).tolist()

(V_GMIX, V_GFFN, V_BMOD, V_DNC, V_HYC, V_DNG, V_FR1, V_B1, V_FR2, V_B2, V_END) = np.cumsum(
    [0, KT, KT, N_MOD_TILES, 3 * DN_TILES, 3 * HY_TILES, 1, 1, 1, 1, 1]).tolist()


def shape_constants():
    t = np.arange(P)
    k = np.zeros((P, K_END), np.float32)
    k[:, K_ID:K_ID + P] = np.eye(P)
    k[:, K_ONE:K_ONE + P] = 1.0
    k[:, K_BLK:K_BLK + P] = (t[:, None] // HEAD) == (t[None] // HEAD)
    k[:, K_INC:K_INC + P] = t[None] >= t[:, None]
    k[:, K_INC + P:K_INC + 2 * P] = t[None] <= t[:, None]
    for lv in range(LEVELS):
        b = 1 << lv
        same = (t[:, None] // (2 * b)) == (t[None] // (2 * b))
        fwd = same & (t[:, None] // b % 2 == 0) & (t[None] // b % 2 == 1)
        k[:, K_LVL + lv * P:K_LVL + (lv + 1) * P] = fwd
        k[:, K_LVL + (LEVELS + lv) * P:K_LVL + (LEVELS + lv + 1) * P] = fwd.T
    half, n = HEAD // 2, HEAD // 4
    inv = np.power(np.float32(10000.0), -np.arange(n, dtype=np.float32) / np.float32(n)).astype(np.float32)
    pos = np.arange(SEQ)
    for ch in range(P):
        c = ch % HEAD
        where = (pos // GRID_W if c < half else pos % GRID_W).astype(np.float32)
        ang = where * inv[c % n]
        k[ch, K_COS:K_COS + SEQ] = np.cos(ang)
        k[ch, K_SIN:K_SIN + SEQ] = np.sin(ang)
        first = c % half < n
        k[ch + n if first else ch - n, K_ROT + ch] = -1.0 if first else 1.0
    for qt in range(2):
        q = qt * P + t
        far = np.abs(q[:, None] - pos[None]) > SW_WINDOW
        k[:, K_BAND + qt * N_TOK + SEQ:K_BAND + (qt + 1) * N_TOK] = np.where(far, -1e30, 0.0)
    k[:, K_IOTA:K_IOTA + P] = np.arange(P)

    h = np.zeros((P, H_END), np.float32)
    m = np.arange(SEQ)
    ang = np.pi * np.mod(m[:, None] * (2 * m[None] + 1), 4 * SEQ) / (2 * SEQ)
    for base, tab in ((H_C, np.cos(ang)), (H_S, np.sin(ang)), (H_CT, np.cos(ang).T / SEQ),
                      (H_ST, -np.sin(ang).T / SEQ)):
        h[:, base:base + 2 * SEQ] = tab.reshape(2, P, SEQ).transpose(1, 0, 2).reshape(P, 2 * SEQ)
    tl = np.linspace(0.0, 1.0, SEQ, dtype=np.float32)
    omega = (np.float32(2.0 * np.pi) * m.astype(np.float32) / np.float32(SEQ)).astype(np.float32)
    bands = np.linspace(1e-4, 15, 16, dtype=np.float32)
    fa = (omega[:, None] * bands[None]).astype(np.float32)
    feats = np.concatenate([tl[:, None], np.cos(fa), -np.sin(fa)], axis=1).astype(np.float32)
    h[0:feats.shape[1], H_FEAT:H_FEAT + SEQ] = feats.T
    deltas = np.abs(np.linspace(np.log(1e-2) / 1.5, np.log(1e-2) / 0.3, HY_CH, dtype=np.float32))
    win = np.exp(-tl[:, None] * deltas[None]).astype(np.float32)
    both = np.stack([win, win], axis=1)
    both[0, 1] = 0.0
    h[:, H_WIN:H_WIN + 4 * HY_CH] = both.reshape(2, P, 2 * HY_CH).transpose(1, 0, 2).reshape(P, -1)
    return k, h


def build(nc, a, out):
    with ExitStack() as ctx:
        def sb(name, shape, dt=F32):
            return ctx.enter_context(nc.sbuf_tensor(name, shape, dt))

        def sem(name):
            return ctx.enter_context(nc.semaphore(name))

        ps = [ctx.enter_context(nc.psum_tensor(f"bank{i}", [P, 512], F32)) for i in range(8)]

        ring = sb("ring", [P, RING, SLOT])
        con = sb("con", [P, K_END])
        xT = sb("xT", [P, KT, N_TOK])
        hT = sb("hT", [P, KT, N_TOK])
        vrow = sb("vrow", [P, P])
        vcol = sb("vcol", [P, P])
        vrow2 = sb("vrow2", [P, P])
        vcol2 = sb("vcol2", [P, 3 * KT])
        cs = sb("cs", [P, KT, 2])
        mod = sb("mod", [P, N_MOD_TILES, 2])
        amul = sb("amul", [P, 2, KT, 2])
        rows = sb("rows", [P, 2 * PROBS + SW_HEADS])
        qkv = sb("qkv", [P, DN_TILES, N_TOK])
        zz = sb("zz", [P, PAIRS, N_TOK])
        abv = sb("abv", [P, TT, ABV])
        misc = sb("misc", [P, 2])
        WORK = 18500
        work = sb("work", [P, WORK])

        def carve(at, *shape):
            n = int(np.prod(shape))
            assert at + n <= WORK, (at, shape)
            v = work[:, at:at + n]
            if len(shape) == 2:
                v = v.rearrange("p (a b) -> p a b", a=shape[0])
            elif len(shape) == 3:
                v = v.rearrange("p (a b c) -> p a b c", a=shape[0], b=shape[1])
            return v, at + n

        SEG = lambda lo: (N_TOK - lo) // SEQ
        hy, at = carve(0, HY_TILES, N_TOK)
        qT, at = carve(at, SW_TILES, N_TOK)
        kT, after_proj = carve(at, N_TOK)
        hc, at = carve(after_proj, H_END)
        w3, at = carve(at, 4 * HY_CH)
        w12, at = carve(at, P)
        kre, at = carve(at, 2, 2 * HY_CH)
        kim, at = carve(at, 2, 2 * HY_CH)
        hy_scratch = at
        kern, at = carve(at, 2, 2, 2 * HY_CH)
        hh1, at = carve(at, SEQ)
        hh2, at = carve(at, SEQ)
        htmp, at = carve(at, SEQ)
        htmp2, at = carve(at, SEQ)
        hnorm, at = carve(at, 2 * HY_CH)
        hskip, at = carve(at, 2 * HY_CH)
        def modr(b):
            flat = (qkv if b < DN_TILES else zz)[0:2, :, :].rearrange("p a b -> p (a b)")
            b = b if b < DN_TILES else b - DN_TILES
            return flat[:, b * 4 * P:(b + 1) * 4 * P]

        ut, at = carve(hy_scratch, 2, N_TOK)
        x1t, at = carve(at, 2, N_TOK)
        pre, at = carve(at, 2, N_TOK)
        pim, at = carve(at, 2, N_TOK)
        ptmp, at = carve(at, N_TOK)
        sc, at = carve(after_proj, 2, N_TOK)
        pT, at = carve(at, 2, N_TOK)
        rot, at = carve(at, 4, SEQ)
        st, at = carve(at, 2, 8)
        ktok, at = carve(0, TT, DN_HEADS * HEAD)
        vtok, at = carve(at, TT, DN_HEADS * HEAD)
        gt, at = carve(at, TT, PROBS)
        bt, at = carve(at, TT, PROBS)
        gc, at = carve(at, TT, PROBS)
        eg, at = carve(at, TT, PROBS)
        gtmp, at = carve(at, TT, PROBS)
        gtmp2, at = carve(at, TT, PROBS)
        kds, at = carve(at, PROBS)
        Amat, at = carve(at, PROBS, CHUNK)
        Xm, at = carve(at, PROBS, CHUNK)
        XT, at = carve(at, PROBS, CHUNK)
        Bm, at = carve(at, PROBS, CHUNK)
        QK, at = carve(at, PROBS, CHUNK)
        egb, at = carve(at, 2 * PAIRS, CHUNK)
        kb, at = carve(at, 2 * PAIRS, CHUNK)
        state, at = carve(at, 2 * PAIRS, P)
        kd, at = carve(at, 2 * PAIRS, P)
        rhs, at = carve(at, PROBS, HEAD)
        Am, at = carve(at, PROBS, CHUNK)
        qd, at = carve(at, 2 * PAIRS, CHUNK)
        vnew = kb.rearrange("p a b -> p (a b)").rearrange("p (q d) -> p q d", q=PROBS)
        sil, at = carve(0, 2, N_TOK)
        act, at = carve(at, 2, 2, N_TOK)
        htok, at = carve(0, 2, D_MODEL)
        sel, at = carve(at, 2, PASSES + 1, P)
        selT, at = carve(at, PASSES + 1, SEQ)
        xg, at = carve(at, KT, P)
        msil, at = carve(at, MOE_F)
        matok, at = carve(at, MOE_F)
        aT, at = carve(at, 2, 4, P)
        ytok, at = carve(at, D_MODEL)
        selnow, at = carve(at, SEQ)
        gplace, at = carve(at, PASSES + 1)
        gpass, at = carve(at, 1)
        lg, at = carve(at, 2, 8)
        top, at = carve(at, 2, 8)
        tix, at = carve(at, 2, 8)
        tmp8, at = carve(at, 2, 8)
        mx, at = carve(at, 2, PASSES + 1)
        gx, at = carve(at, 2, PASSES + 1)
        rx, at = carve(at, 2, PASSES + 1)
        over8, at = carve(at, 8)
        incl8, at = carve(at, 8)
        hot8, at = carve(at, 8)
        prod8, at = carve(at, 2, 8)
        metaf, at = carve(at, 1 + EXTRA + PASSES)
        rxn, at = carve(at, 2, PASSES)
        wr, at = carve(at, KT, N_EXPERTS)
        meta = sb("meta", [P, 1 + EXTRA + PASSES], mybir.dt.int32)
        topi = sb("topi", [P, 2, 8], U32)
        rms_r, at = carve(0, N_TOK)
        rms_s, at = carve(at, N_TOK)

        ident = con[:, K_ID:K_ID + P]
        ones = con[:, K_ONE:K_ONE + P]
        blk = con[:, K_BLK:K_BLK + P]

        eps_col, one_col = misc[:, 0:1], misc[:, 1:2]

        def XT_flat(i):
            return Xm.rearrange("p a b -> p (a b)")[:, i * N_TOK:(i + 1) * N_TOK] if i < 3 else \
                XT.rearrange("p a b -> p (a b)")[:, (i - 3) * N_TOK:(i - 2) * N_TOK]

        def row_loads(layer):
            def rows128(at, v):
                v = v.rearrange("(r p) -> r p", p=P)
                return vrow[at:at + v.shape[0], :], v
            flat = lambda v: v.rearrange("a b -> (a b)")
            every = lambda v: v.partition_broadcast(P)
            return [
                rows128(V_GMIX, a["norm_mix_g"][layer]), rows128(V_GFFN, a["norm_ffn_g"][layer]),
                rows128(V_BMOD, a["b_mod"][layer]), rows128(V_DNC, flat(a["dn_conv_w"][layer])),
                rows128(V_HYC, flat(a["hy_conv_w"][layer])),
                (vrow[V_DNG:V_DNG + 1, 0:HEAD], a["dn_norm_g"][layer:layer + 1, :]),
                (vrow[V_DNG:V_DNG + 1, HEAD:P], a["dn_norm_g"][layer:layer + 1, :]),
                (vrow[V_FR1:V_FR1 + 1, 0:HEAD], a["hy_freq1"][layer:layer + 1, :]),
                (vrow[V_B1:V_B1 + 1, 0:HEAD], a["hy_b1"][layer:layer + 1, :]),
                (vrow[V_FR2:V_FR2 + 1, 0:HEAD], a["hy_freq2"][layer:layer + 1, :]),
                (vrow[V_B2:V_B2 + 1, 0:HEAD], a["hy_b2"][layer:layer + 1, :]),
                (rows[:, 0:PROBS], every(flat(a["dn_a_log"][layer]))),
                (rows[:, PROBS:2 * PROBS], every(flat(a["dn_dt_bias"][layer]))),
                (rows[:, 2 * PROBS:2 * PROBS + SW_HEADS], every(a["sw_sink"][layer])),
                (hc[:, :], a["k_hy"]), (w12[0:33, 0:HEAD], a["hy_w1"][layer]), (w12[0:HEAD, HEAD:P], a["hy_w2"][layer]),
                (w3[0:HEAD, :], a["hy_w3"][layer]), (w3[HEAD:HEAD + 1, :], a["hy_b3"][layer:layer + 1, :]),
                (hskip[:, :], every(flat(a["hy_skip"][layer]))),
            ]

        ROW_LOADS = 20
        HY_PHASES = 23
        phase = sem("phase")
        dve_chain, act_chain, pool_chain = sem("dve_chain"), sem("act_chain"), sem("pool_chain")
        slot_full = [sem(f"slot_full{i}") for i in range(RING)]
        setup_in, rows_in, router_in = sem("setup_in"), sem("rows_in"), sem("router_in")
        mod_copied = sem("mod_copied")
        mod_ready = sem("mod_ready")
        normed = sem("normed")
        proj_ready = sem("proj_ready")
        conv_done = sem("conv_done")
        copy_done = sem("copy_done")
        score_ready, score_read = sem("score_ready"), sem("score_read")
        max_ready, exp_ready, prob_ready = sem("max_ready"), sem("exp_ready"), sem("prob_ready")
        turn_ready, turn_read = sem("turn_ready"), sem("turn_read")
        pv_ready, pv_read = sem("pv_ready"), sem("pv_read")
        am_ready, b_ready, b_copied = sem("am_ready"), sem("b_ready"), sem("b_copied")
        p_ready, x_done = sem("p_ready"), sem("x_done")
        r_ready, diff_ready = sem("r_ready"), sem("diff_ready")
        egb_ready, decay_ready = sem("egb_ready"), sem("decay_ready")
        kds_ready, kd_ready = sem("kds_ready"), sem("kd_ready")
        beta_ready, kb_ready = sem("beta_ready"), sem("kb_ready")
        kq_ready, qk_read, qk_ready = sem("kq_ready"), sem("qk_read"), sem("qk_ready")
        kk_ready, a_ready = sem("kk_ready"), sem("a_ready")
        x0_ready, xt_turned, xm_ready = sem("x0_ready"), sem("xt_turned"), sem("xm_ready")
        qd_ready, ks_ready, rhs_ready = sem("qd_ready"), sem("ks_ready"), sem("rhs_ready")
        v_ready, vnew_ready = sem("v_ready"), sem("vnew_ready")
        out_ready, state_ready = sem("out_ready"), sem("state_ready")
        mix_ready, mix_added = sem("mix_ready"), sem("mix_added")
        gu_ready, sil_ready, act_ready = sem("gu_ready"), sem("sil_ready"), sem("act_ready")
        down_ready, down_added = sem("down_ready"), sem("down_added")
        slot_used = sem("slot_used")
        xg_ready, matok_turned = sem("xg_ready"), sem("matok_turned")
        aT_ready, y_copied = sem("aT_ready"), sem("y_copied")
        gathered, scattered = sem("gathered"), sem("scattered")
        meta_ready, gpass_set = sem("meta_ready"), sem("gpass_set")
        rows_out, out_done = sem("rows_out"), sem("out_done")

        w_in_v = a["w_in"].rearrange("l (k p) n -> l p k n", p=P)
        w_out_v = a["w_out"]
        w_mod_v = a["w_mod"].rearrange("l (k p) n -> l p k n", p=P)
        NS = {"mod": MOD_SLOTS, "in": IN_SLOTS, "out": OUT_SLOTS}

        def wide(s):
            return ring[:, s % RING, :].rearrange("p (k n) -> p k n", k=KT)

        def deep(s):
            return ring[:, s % RING, :].rearrange("p (k n) -> p k n", k=2)

        in_tiles = ([("dn", i) for i in range(DN_TILES)] + [("z", i) for i in range(PAIRS)]
                    + [("hy", i) for i in range(HY_TILES)] + [("q", i) for i in range(SW_TILES)] + [("k", 0)])

        def halves(dst, src):
            return [(dst[:, 0:KT // 2], src[:, 0:KT // 2]), (dst[:, KT // 2:KT], src[:, KT // 2:KT])]

        def in_slot_loads(layer, j, s):
            w = w_in_v[layer]
            if j == 0:
                return [(wide(s)[:, :, 0:24], w[:, :, C_A:C_A + 24]),
                        (wide(s)[:, :, 24:ABV], w[:, :, C_V:C_V + P])]
            pair = in_tiles[2 * (j - 1):2 * j]
            if pair[0][0] in ("q", "k") or pair[1][0] in ("q", "k"):
                loads = []
                for half, (kind, i) in enumerate(pair):
                    if kind == "q":
                        for hd in range(2):
                            c = C_Q + (i + 3 * hd) * HEAD
                            loads.append((wide(s)[:, :, half * P + hd * HEAD:half * P + (hd + 1) * HEAD],
                                          w[:, :, c:c + HEAD]))
                    else:
                        for hd in range(2):
                            loads.append((wide(s)[:, :, half * P + hd * HEAD:half * P + (hd + 1) * HEAD],
                                          w[:, :, C_K + hd * HEAD:C_K + (hd + 1) * HEAD]))
                return loads
            base = {"dn": C_DN, "z": C_Z, "hy": C_HY}[pair[0][0]] + pair[0][1] * P
            if pair[0][0] == pair[1][0]:
                return halves(wide(s), w[:, :, base:base + 2 * P])
            base2 = {"dn": C_DN, "z": C_Z, "hy": C_HY}[pair[1][0]] + pair[1][1] * P
            return [(wide(s)[:, :, 0:P], w[:, :, base:base + P]), (wide(s)[:, :, P:2 * P], w[:, :, base2:base2 + P])]

        def out_slot_loads(layer, j, s):
            cols = slice(j * 2 * P, (j + 1) * 2 * P)
            w = w_out_v[layer]
            plain = w[0:5 * P, cols].rearrange("(k p) n -> p k n", p=P)
            sw = w[5 * P:8 * P, cols].rearrange("(h i d) n -> h d i n", h=2, i=SW_TILES)
            return [(wide(s)[:, 0:5, :], plain), (wide(s)[0:HEAD, 5:8, :], sw[0]), (wide(s)[HEAD:P, 5:8, :], sw[1])]

        def gu_loads(wm, r, s):
            return halves(wide(s), wm[:, r * ROUND_F:(r + 1) * ROUND_F].rearrange("(k p) n -> p k n", p=P))

        def dn_loads(wm, r, s):
            src = wm[r * ROUND_F:(r + 1) * ROUND_F, :].rearrange("(k p) n -> p k n", p=P)
            return [(deep(s)[:, 0:1], src[:, 0:1]), (deep(s)[:, 1:2], src[:, 1:2])]

        def half_k(s):
            return ring[:, s % RING, :].rearrange("p (k n) -> p k n", k=4)

        def round_order(n):
            yield "g", 0
            yield "u", 0
            for r in range(1, n):
                yield "g", r
                yield "u", r
                yield "d", r - 1
            yield "d", n - 1

        plan = []
        for layer in range(N_LAYERS):
            for j in range(MOD_SLOTS):
                plan.append((lambda s, l=layer, j=j: halves(wide(s), w_mod_v[l][:, :, j * 2 * P:(j + 1) * 2 * P]),
                             (mod_ready, layer * MOD_SLOTS + j + 1)))
            for j in range(IN_SLOTS):
                plan.append((lambda s, l=layer, j=j: in_slot_loads(l, j, s),
                             (proj_ready, layer * 2 * IN_SLOTS + 2 * (j + 1))))
            for j in range(OUT_SLOTS):
                plan.append((lambda s, l=layer, j=j: out_slot_loads(l, j, s),
                             (mix_ready, layer * KT + 2 * (j + 1))))
            if layer == 0:
                for kind, r in round_order(DENSE_ROUNDS):
                    if kind == "d":
                        plan.append((lambda s, r=r: dn_loads(a["ffn_w_down"][0], r, s), (down_ready, KT * (r + 1))))
                    else:
                        w = a["ffn_w_gate" if kind == "g" else "ffn_w_up"][0]
                        plan.append((lambda s, r=r, w=w: gu_loads(w, r, s), (gu_ready, 2 * (r + 1))))
        S_MOE = len(plan)
        MOE_ORDER = [(kind, r, h) for kind, r in round_order(MOE_ROUNDS) for h in range(2)]
        assert len(MOE_ORDER) % RING == 0

        counts, landed = [0] * RING, []
        for n, (loads, _) in enumerate(plan):
            counts[n % RING] += 16 * len(loads(n))
            landed.append(counts[n % RING])
        g_done, u_done, d_done = ([j + 1 for j, (kind, r, h) in enumerate(MOE_ORDER) if kind == x and h]
                                  for x in "gud")
        MOE_USE = 32
        MOE_INC = MOE_USE * len(MOE_ORDER) // RING

        def moe_landed(j):
            n = S_MOE + j
            return counts[n % RING] + MOE_USE * (j // RING + 1)

        block = ctx.enter_context(nc.Block())

        @block.sync
        def _(sp):
            def load(loads, s):
                for dst, src in loads:
                    sp.dma_start(dst, src).then_inc(slot_full[s % RING], 16)
            for s, (loads, _) in enumerate(plan):
                if s == 0:
                    sp.dma_start(con[:, :], a["k_con"]).then_inc(setup_in, 16)
                    sp.dma_start(hT[:, 0:4, :].rearrange("p (t k) n -> p t (k n)", t=2),
                                 a["ctx"][0].rearrange("(t p) n -> p t n", p=P)).then_inc(setup_in, 16)
                    sp.dma_start(hT[:, 4:8, :].rearrange("p (t k) n -> p t (k n)", t=2),
                                 a["x"][0].rearrange("(t p) n -> p t n", p=P)).then_inc(setup_in, 16)
                    sp.dma_start(vrow2[0:KT, :], a["c_ctx"].rearrange("(k p) -> k p", p=P)).then_inc(setup_in, 16)
                    sp.dma_start(vrow2[KT:2 * KT, :], a["c"][0].rearrange("(k p) -> k p", p=P)).then_inc(setup_in, 16)
                    sp.dma_start(vrow2[2 * KT:3 * KT, :],
                                 a["final_norm_g"].rearrange("(k p) -> k p", p=P)).then_inc(setup_in, 16)
                if s >= RING:
                    used, count = plan[s - RING][1]
                    sp.wait_ge(used, count)
                load(loads(s), s)

            def moe_load(e, j):
                s = S_MOE + j
                kind, r, h = MOE_ORDER[j]
                if kind == "d":
                    f0 = r * MOE_F + h * 2 * P
                    src = a["moe_w_down"][0][bass.ds(e, 1), f0:f0 + 2 * P, :].rearrange("e (k p) n -> p (e k) n", p=P)
                    load([(deep(s)[:, i:i + 1], src[:, i:i + 1]) for i in range(2)], s)
                else:
                    wm = a["moe_w_gate" if kind == "g" else "moe_w_up"][0]
                    src = wm[bass.ds(e, 1), h * 4 * P:(h + 1) * 4 * P, r * MOE_F:(r + 1) * MOE_F].rearrange(
                        "e (k p) n -> p (e k) n", p=P)
                    load([(half_k(s)[:, 2 * i:2 * i + 2], src[:, 2 * i:2 * i + 2]) for i in range(2)], s)

            def moe_pass(pi, e):
                for j in range(len(MOE_ORDER)):
                    sp.wait_ge(slot_used, pi * len(MOE_ORDER) + (j - RING + 1))
                    moe_load(e, j)

            for j in range(len(MOE_ORDER)):
                if j < RING:
                    sp.wait_ge(*plan[S_MOE + j - RING][1])
                else:
                    sp.wait_ge(slot_used, j - RING + 1)
                moe_load(0, j)
            with sp.Fori(1, N_EXPERTS) as e:
                moe_pass(e, e)
            sp.wait_ge(meta_ready, 1)
            n_over = sp.value_load(meta[0:1, 0:1], min_val=0, max_val=EXTRA)
            with sp.Fori(0, EXTRA) as p:
                with sp.If(p < n_over):
                    e = sp.value_load(meta[0:1, bass.ds(p + 1, 1)], min_val=0, max_val=N_EXPERTS - 1)
                    moe_pass(p + N_EXPERTS, e)
            sp.wait_ge(rows_out, 2)
            sp.dma_start(out[0].rearrange("(t p) n -> p t n", p=P),
                         hT[:, 0:4, :].rearrange("p (t k) n -> p t (k n)", t=2)).then_inc(out_done, 16)
            sp.wait_ge(out_done, 16)


        class Link:

            def __init__(self, eng, chain):
                self.eng, self.chain, self.n, self.phases, self.told = eng, chain, 0, 0, {}

            def __call__(self, ins):
                self.n += 1
                ins.then_inc(self.chain, 1)
                self.eng.wait_ge(self.chain, self.n)

            def end_phase(self):
                self.phases += 1
                self.eng.drain().then_inc(phase, 1)
                self.eng.wait_ge(phase, 4 * self.phases)

        STEP_TILES = [(0, 1), (1, 0), (2, 3), (3, 2)]
        GROUPS = [(g, g // 2, slice(3 * g, 3 * g + 3)) for g in range(4)]

        def col(q):
            return q // DN_HEADS * DN_HEADS + q % PAIRS * 2 + q // PAIRS % 2

        def cols3(g):
            return slice(col(3 * g), col(3 * g) + 2 * PAIRS - 1, 2)

        ended = []

        def three(b):
            return ps[b][:, 0:3 * P].rearrange("p (a b) -> p a b", a=3)

        def six(b):
            return ps[b][:, 0:DN_HEADS * HEAD].rearrange("p (a b) -> p a b", a=DN_HEADS)

        def seg(ap, lo):
            return ap[:, lo:N_TOK].rearrange("p (s t) -> p s t", t=SEQ)

        def mask(col, n=3):
            return con[:, col:col + P].unsqueeze(1).to_broadcast([P, n, P])

        def over(ap, n):
            return ap.unsqueeze(2).to_broadcast([P, ap.shape[1], n])

        def jobs(layer):
            lat = [(1, i, h, t) for i in range(SW_TILES) for h in range(2) for t in range(2)]
            return lat if layer == N_LAYERS - 1 else lat + [(0,) + j[1:] for j in lat]

        SIL0, A0, ADD0 = 2 * DENSE_ROUNDS, 2 * DENSE_ROUNDS, KT * DENSE_ROUNDS
        PRIME = 2

        ATT_BASE = [0, len(jobs(0))]

        def read_before(n):
            kinds = ["abv"] * 2 + [k for k, _ in in_tiles]
            mine = ("z", "q", "k")
            per = [sum(k not in mine for k in kinds), sum(k in mine for k in kinds)]
            who = kinds[n] in mine
            return (copy_done if who else conv_done), per[who], sum((k in mine) == who for k in kinds[:n + 1])

        def lvl_index(layer, i, lv, g):
            return ((layer * 4 + i) * (LEVELS - 1) + lv - 1) * 4 + g

        @block.tensor
        def _(pe):
            link = Link(pe, None)
            T = nc.tensor
            s = 0

            def full(s):
                pe.wait_ge(slot_full[s % RING], landed[s])

            def rms(lo):
                link.end_phase()
                for k in range(KT):
                    T.matmul(ps[0][:, lo:N_TOK], ones, hT[:, k, lo:N_TOK], start=(k == 0), stop=(k == KT - 1))
                link.end_phase()
                link.end_phase()
                link.end_phase()

            pe.wait_ge(setup_in, 16 * 6)
            tok = hT[:, :, :].rearrange("p (t k) n -> p t (k n)", t=TT)
            for k in range(KT):
                for t in range(TT):
                    T.transpose(ps[k][:, t * P:(t + 1) * P], tok[:, t, k * P:(k + 1) * P], ident)
            link.end_phase()
            link.end_phase()
            T.transpose(ps[0][:, 0:3 * KT], vrow2[0:3 * KT, :], ident[0:3 * KT, 0:3 * KT])
            link.end_phase()
            link.end_phase()

            def hyena(layer, lo):
                T.matmul(ps[0][0:HEAD, 0:SEQ], w12[0:33, 0:HEAD], hc[0:33, H_FEAT:H_FEAT + SEQ], start=True, stop=True)
                link.end_phase()
                link.end_phase()
                link.end_phase()
                T.matmul(ps[0][0:HEAD, 0:SEQ], w12[0:HEAD, HEAD:P], hh1[0:HEAD, :], start=True, stop=True)
                link.end_phase()
                link.end_phase()
                link.end_phase()
                for mt in range(2):
                    for d in range(2):
                        T.matmul(ps[2 * mt + d][:, :], hh2[0:HEAD + 1, mt * P:(mt + 1) * P],
                                 w3[0:HEAD + 1, d * 2 * HY_CH:(d + 1) * 2 * HY_CH], start=True, stop=True)
                link.end_phase()
                link.end_phase()
                link.end_phase()
                sq = [kre[:, 0], kre[:, 1], kim[:, 0], kim[:, 1]]
                for n in range(4):
                    T.matmul(ps[4][:, :], ones, sq[n], start=(n == 0), stop=(n == 3))
                link.end_phase()
                link.end_phase()

                def fourier(dst, tab, src, lo=0):
                    for f in range(2):
                        for t in range(2):
                            T.matmul(ps[dst + f][:, lo:N_TOK], hc[:, tab + t * SEQ + f * P:tab + t * SEQ + (f + 1) * P],
                                     src(t), start=(t == 0), stop=(t == 1))

                fourier(0, H_C, lambda t: kre[:, t])
                fourier(2, H_S, lambda t: kern[:, t, 1])
                link.end_phase()
                link.end_phase()
                for tt in range(2):
                    for st_ in range(lo // SEQ, 2):
                        for i in range(2):
                            tok0 = st_ * SEQ + tt * P
                            at = slice(st_ * SEQ + i * P, st_ * SEQ + (i + 1) * P)
                            T.transpose(ps[tt][:, at], hy[:, i, tok0:tok0 + P], ident)
                            T.transpose(ps[2 + tt][:, at], hy[:, 2 + i, tok0:tok0 + P], ident)
                link.end_phase()
                link.end_phase()
                for order in range(2):
                    fourier(0, H_C, lambda t: ut[:, t, lo:N_TOK], lo)
                    fourier(2, H_S, lambda t: ut[:, t, lo:N_TOK], lo)
                    link.end_phase()
                    link.end_phase()
                    for t in range(2):
                        if order == 0:
                            for n, (tab, src) in enumerate([(H_CT, pre), (H_ST, pim)]):
                                for f in range(2):
                                    c = tab + f * SEQ + t * P
                                    T.matmul(ps[t][:, lo:N_TOK], hc[:, c:c + P], src[:, f, lo:N_TOK],
                                             start=(n + f == 0), stop=(n + f == 2))
                        else:
                            for st_ in range(lo // SEQ, 2):
                                for n, (tab, src) in enumerate([(H_CT, pre), (H_ST, pim)]):
                                    for f in range(2):
                                        c = st_ * SEQ + t * P
                                        T.matmul(ps[t][:, st_ * SEQ:(st_ + 1) * SEQ], src[:, f, c:c + P],
                                                 hc[:, tab + f * SEQ:tab + (f + 1) * SEQ],
                                                 start=(n + f == 0), stop=(n + f == 2))
                    link.end_phase()
                    link.end_phase()

            def attention(layer):
                for i in range(4):
                    src = qT[:, i, SEQ:N_TOK] if i < SW_TILES else kT[:, SEQ:N_TOK]
                    T.matmul(ps[i // 2][:, i % 2 * SEQ:(i % 2 + 1) * SEQ], con[:, K_ROT:K_ROT + P], src,
                             start=True, stop=True)
                link.end_phase()
                link.end_phase()
                base, todo = ATT_BASE[layer], jobs(layer)

                def scores(n):
                    lat, i, half, qt = todo[n]
                    rows_ = slice(half * HEAD, (half + 1) * HEAD)
                    if n >= 2:
                        pe.wait_ge(score_read, base + n - 1)
                    q0 = lat * SEQ + qt * P
                    keys = N_TOK if lat else SEQ
                    T.matmul(ps[n % 2][:, 0:keys], qT[rows_, i, q0:q0 + P], kT[rows_, 0:keys],
                             start=True, stop=True).then_inc(score_ready, 1)

                def turns(n):
                    pe.wait_ge(prob_ready, base + n + 1)
                    if n >= 2:
                        pe.wait_ge(turn_read, base + n - 1)
                    for kt_ in range(4 if todo[n][0] else 2):
                        last = T.transpose(ps[2 + n % 2][:, kt_ * P:(kt_ + 1) * P], sc[:, n % 2, kt_ * P:(kt_ + 1) * P],
                                           ident)
                    last.then_inc(turn_ready, 1)

                def values(n):
                    lat, i, half, qt = todo[n]
                    rows_ = slice(half * HEAD, (half + 1) * HEAD)
                    nk = 4 if lat else 2
                    pe.wait_ge(turn_read, base + n + 1)
                    if n >= 2:
                        pe.wait_ge(pv_read, base + n - 1)
                    for kt_ in range(nk):
                        last = T.matmul(ps[4 + n % 2][rows_, 0:P], abv[:, kt_, 24 + half * HEAD:24 + (half + 1) * HEAD],
                                        pT[:, n % 2, kt_ * P:(kt_ + 1) * P], start=(kt_ == 0), stop=(kt_ == nk - 1))
                    last.then_inc(pv_ready, 1)

                for it in range(len(todo) + 2):
                    if it < len(todo):
                        scores(it)
                    if 1 <= it <= len(todo):
                        turns(it - 1)
                    if it >= 2:
                        values(it - 2)
                link.end_phase()

            def delta(layer, lo):
                link.end_phase()
                for i in range(6):
                    T.matmul(ps[i][:, :], blk, XT_flat(i), start=True, stop=True)
                link.end_phase()
                link.end_phase()
                link.end_phase()
                for t in range(TT):
                    for kind in range(2):
                        for i in range(PAIRS):
                            T.transpose(ps[2 * t + kind][:, i * P:(i + 1) * P],
                                        qkv[:, (kind + 1) * PAIRS + i, t * P:(t + 1) * P], ident)
                link.end_phase()
                link.end_phase()
                for t in range(TT):
                    for d in range(DIRS):
                        c = t * PROBS + d * DN_HEADS
                        T.matmul(ps[0][:, c:c + DN_HEADS], con[:, K_INC + d * P:K_INC + (d + 1) * P],
                                 gt[:, t, d * DN_HEADS:(d + 1) * DN_HEADS], start=True, stop=True)
                link.end_phase()
                link.end_phase()
                for i in range(4):
                    want_o = not (layer == N_LAYERS - 1 and i < 2)
                    G0, D0 = (layer * 4 + i) * 4, (layer * 4 + i) * DIRS

                    def rows_of(g, n):
                        h = col(3 * g + n) % DN_HEADS
                        tile = STEP_TILES[i][g // 2]
                        return slice(h % 2 * HEAD, (h % 2 + 1) * HEAD), h // 2, slice(tile * P, (tile + 1) * P)

                    for g, d, qs in GROUPS:
                        for n, q in enumerate(range(3 * g, 3 * g + 3)):
                            tile = STEP_TILES[i][d]
                            last = T.matmul(ps[g][:, n * P:(n + 1) * P], gt[:, tile, col(q):col(q) + 1].to_broadcast([P, P]),
                                            con[:, K_INC + d * P:K_INC + (d + 1) * P], start=True, stop=True)
                        last.then_inc(r_ready, 1)
                    if i:
                        pe.wait_ge(state_ready, D0)
                    for d in range(DIRS):
                        tile = STEP_TILES[i][d]
                        for j in range(PAIRS):
                            for half in range(2):
                                q = d * DN_HEADS + 2 * j + half
                                r_ = slice(half * HEAD, (half + 1) * HEAD)
                                last = T.matmul(ps[4 + d][r_, j * P:(j + 1) * P], bt[:, tile, q:q + 1].to_broadcast([P, HEAD]),
                                                ident, start=True, stop=True)
                        last.then_inc(beta_ready, 1)

                    def kq(g):
                        for n in range(3):
                            r_, j, c_ = rows_of(g, n)
                            last = T.matmul(ps[6 + g % 2][:, n * P:(n + 1) * P], qkv[r_, PAIRS + j, c_], qkv[r_, j, c_],
                                            start=True, stop=True)
                        last.then_inc(kq_ready, 1)

                    def kk(g):
                        for n in range(3):
                            r_, j, c_ = rows_of(g, n)
                            last = T.matmul(ps[4 + g % 2][:, n * P:(n + 1) * P], qkv[r_, PAIRS + j, c_],
                                            kb[r_, g // 2 * PAIRS + j, :], start=True, stop=True)
                        last.then_inc(kk_ready, 1)

                    kq(0)
                    kq(1)
                    pe.wait_ge(kb_ready, D0 + 2)
                    kk(0)
                    kk(1)
                    for g in (2, 3):
                        pe.wait_ge(qk_read, G0 + g - 1)
                        kq(g)
                    for g in (2, 3):
                        pe.wait_ge(a_ready, G0 + g - 1)
                        kk(g)
                    for d in range(DIRS):
                        pe.wait_ge(qk_read, G0 + d + 3)
                        cols = slice(STEP_TILES[i][d] * P, (STEP_TILES[i][d] + 1) * P)
                        for j in range(PAIRS):
                            last = T.matmul(ps[6 + d][:, j * P:(j + 1) * P], qkv[:, PAIRS + j, cols],
                                            state[:, d * PAIRS + j, :], start=True, stop=True)
                        last.then_inc(ks_ready, 1)
                    for g, d, qs in GROUPS:
                        pe.wait_ge(x0_ready, G0 + g + 1)
                        for n, q in enumerate(range(3 * g, 3 * g + 3)):
                            last = T.transpose(ps[g][:, n * P:(n + 1) * P], XT[:, q, :], ident)
                        last.then_inc(xt_turned, 1)
                    for lv in range(1, LEVELS):
                        for g, d, qs in GROUPS:
                            ix = lvl_index(layer, i, lv, g)
                            pe.wait_ge(am_ready, ix + 1)
                            if lv > 1:
                                pe.wait_ge(x_done, ix - 3)
                            else:
                                pe.wait_ge(xm_ready, G0 + g + 1)
                            for n, q in enumerate(range(3 * g, 3 * g + 3)):
                                last = T.matmul(ps[g][:, n * P:(n + 1) * P], Am[:, q, :], Xm[:, q, :],
                                                start=True, stop=True)
                            last.then_inc(b_ready, 1)
                        for g, d, qs in GROUPS:
                            ix = lvl_index(layer, i, lv, g)
                            pe.wait_ge(b_copied, ix + 1)
                            if g >= 2:
                                pe.wait_ge(x_done, ix - 1)
                            elif lv == 1:
                                pe.wait_ge(rhs_ready, D0 + 2)
                            for n, q in enumerate(range(3 * g, 3 * g + 3)):
                                if lv < LEVELS - 1:
                                    T.matmul(ps[4 + g % 2 * 2][:, n * P:(n + 1) * P], XT[:, q, :], Bm[:, q, :],
                                             start=True, stop=True)
                                last = T.matmul(ps[5 + g % 2 * 2][:, n * P:(n + 1) * P], Bm[:, q, :], XT[:, q, :],
                                                start=True, stop=True)
                            last.then_inc(p_ready, 1)
                    for d in range(DIRS):
                        pe.wait_ge(x_done, lvl_index(layer, i, LEVELS - 1, 2 * d + 1) + 1)
                        for q in range(d * DN_HEADS, (d + 1) * DN_HEADS):
                            h = col(q) % DN_HEADS
                            last = T.matmul(ps[2 + d][:, h * HEAD:(h + 1) * HEAD], XT[:, q, :], rhs[:, col(q), :],
                                            start=True, stop=True)
                        last.then_inc(v_ready, 1)
                    for d in range(DIRS):
                        pe.wait_ge(vnew_ready, D0 + d + 1)
                        pe.wait_ge(kd_ready, D0 + d + 1)
                        if want_o:
                            pe.wait_ge(qd_ready, D0 + d + 1)
                            pe.wait_ge(qk_ready, G0 + 2 * d + 2)
                        for j in range(PAIRS):
                            if want_o:
                                T.matmul(ps[4 + d][:, j * P:(j + 1) * P], state[:, d * PAIRS + j, :],
                                         qd[:, d * PAIRS + j, :], start=True, stop=False, skip_group_check=True)
                                for half in range(2):
                                    q = d * DN_HEADS + half * PAIRS + j
                                    T.matmul(ps[4 + d][half * HEAD:(half + 1) * HEAD, j * P:(j + 1) * P],
                                             vnew[:, col(q), :], QK[:, q, :], start=False, stop=True, skip_group_check=True)
                            q = d * DN_HEADS + 2 * j
                            last = T.matmul(ps[6 + d][:, j * P:(j + 1) * P], kd[:, d * PAIRS + j, :],
                                            vnew[:, q:q + 2, :].rearrange("p a b -> p (a b)"), start=True, stop=True)
                        last.then_inc(out_ready, 1)
                link.end_phase()
                link.end_phase()
                for j in range(PAIRS):
                    T.matmul(ps[j][:, lo:N_TOK], blk, XT_flat(j)[:, lo:N_TOK], start=True, stop=True)
                link.end_phase()
                link.end_phase()
                link.end_phase()

            def gate_up(R, ft, sg, lo, first):
                if not first:
                    pe.wait_ge(act_ready, 2 * R + ft - 1)
                for which in range(2):
                    for k in range(KT):
                        last = T.matmul(ps[2 * ft + which][:, lo:N_TOK], wide(sg + which)[:, k, ft * P:(ft + 1) * P],
                                        hT[:, k, lo:N_TOK], start=(k == 0), stop=(k == KT - 1))
                last.then_inc(gu_ready, 1)

            def down(R, par, sd, lo, first):
                pe.wait_ge(act_ready, 2 * R + 2)
                for d in range(KT):
                    if not (first and d < 4):
                        pe.wait_ge(down_added, KT * R + d - 3)
                    for ft in range(2):
                        last = T.matmul(ps[4 + d % 4][:, lo:N_TOK], deep(sd)[:, ft, d * P:(d + 1) * P],
                                        act[:, par, ft, lo:N_TOK], start=(ft == 0), stop=(ft == 1))
                    last.then_inc(down_ready, 1)

            for layer in range(N_LAYERS):
                last_layer = layer == N_LAYERS - 1
                lo = SEQ if last_layer else 0
                pe.wait_ge(rows_in, ROW_LOADS * 16 * (layer + 1))
                T.transpose(ps[1][:, 0:V_END], vrow[0:V_END, :], ident[0:V_END, 0:V_END])
                for j in range(MOD_SLOTS):
                    full(s)
                    b = j // 2
                    if j % 2 == 0 and b >= 6:
                        pe.wait_ge(mod_copied, layer * MOD_SLOTS // 2 + b - 5)
                    for k in range(KT):
                        last = T.matmul(ps[2 + b % 6][0:2, j % 2 * 2 * P:(j % 2 + 1) * 2 * P], cs[:, k, :],
                                        wide(s)[:, k, :], start=(k == 0), stop=(k == KT - 1))
                    last.then_inc(mod_ready, 1)
                    s += 1
                for b in range(MOD_SLOTS // 2):
                    pe.wait_ge(mod_copied, layer * MOD_SLOTS // 2 + b + 1)
                    for m in range(4):
                        T.transpose(ps[0][:, 8 * b + 2 * m:8 * b + 2 * m + 2], modr(b)[:, m * P:(m + 1) * P], ident[0:2, 0:2])
                link.end_phase()
                link.end_phase()
                rms(0)
                for j in range(IN_SLOTS):
                    full(s)
                    for half in range(2):
                        n = 2 * j + half
                        if n - 2 >= len(in_tiles):
                            break
                        if j == 0:
                            for tt in range(2):
                                for k in range(KT):
                                    last = T.matmul(ps[half][:, tt * ABV:(tt + 1) * ABV],
                                                    hT[:, k, (2 * half + tt) * P:(2 * half + tt + 1) * P],
                                                    wide(s)[:, k, 0:ABV], start=(k == 0), stop=(k == KT - 1))
                        else:
                            t0 = lo if in_tiles[n - 2][0] in ("z", "hy", "q") else 0
                            if n >= 4:
                                who, per, upto = read_before(n - 4)
                                pe.wait_ge(who, layer * per + upto)
                            for k in range(KT):
                                last = T.matmul(ps[n % 4][:, t0:N_TOK], wide(s)[:, k, half * P:(half + 1) * P],
                                                hT[:, k, t0:N_TOK], start=(k == 0), stop=(k == KT - 1))
                        last.then_inc(proj_ready, 1)
                    s += 1
                link.end_phase()
                hyena(layer, lo)
                attention(layer)
                delta(layer, lo)
                for j in range(OUT_SLOTS):
                    full(s)
                    for half in range(2):
                        n = 2 * j + half
                        if n >= 4:
                            pe.wait_ge(mix_added, layer * KT + n - 3)
                        for k in range(KT):
                            last = T.matmul(ps[n % 4][:, lo:N_TOK], wide(s)[:, k, half * P:(half + 1) * P],
                                            hT[:, k, lo:N_TOK], start=(k == 0), stop=(k == KT - 1))
                        last.then_inc(mix_ready, 1)
                    s += 1
                link.end_phase()
                rms(lo)
                if not last_layer:
                    for r in range(DENSE_ROUNDS):
                        full(s)
                        full(s + 1)
                        for ft in range(2):
                            gate_up(r, ft, s, lo, r == 0)
                        s += 2
                        if r:
                            full(s)
                            down(r - 1, (r - 1) % 2, s, lo, r == 1)
                            s += 1
                    full(s)
                    down(DENSE_ROUNDS - 1, (DENSE_ROUNDS - 1) % 2, s, lo, False)
                    s += 1
                    link.end_phase()
                else:
                    pe.wait_ge(router_in, 16)
                    for t in range(2):
                        for k in range(KT):
                            T.matmul(ps[0][:, 8 * t:8 * t + 8], hT[:, k, SEQ + t * P:SEQ + (t + 1) * P],
                                     wr[:, k, :], start=(k == 0), stop=(k == KT - 1))
                    for t in range(2):
                        for k in range(KT):
                            T.transpose(ps[1 + 2 * t + k // 4][:, k % 4 * P:(k % 4 + 1) * P],
                                        hT[:, k, SEQ + t * P:SEQ + (t + 1) * P], ident)
                    link.end_phase()
                    link.end_phase()
                    link.end_phase()
                    link.end_phase()
                    inc = con[:, K_INC:K_INC + P]
                    T.matmul(ps[0][:, 0:8], inc, mx[:, 0, 0:8], start=True, stop=True)
                    T.matmul(ps[0][:, 8:16], ones, mx[:, 0, 0:8], start=True, stop=False)
                    T.matmul(ps[0][:, 8:16], inc, mx[:, 1, 0:8], start=False, stop=True)
                    T.matmul(ps[0][:, 16:24], ones, mx[:, 0, 0:8], start=True, stop=False)
                    T.matmul(ps[0][:, 16:24], ones, mx[:, 1, 0:8], start=False, stop=True)
                    link.end_phase()
                    link.end_phase()
                    for p in range(PASSES):
                        for t in range(2):
                            T.transpose(ps[p // 2][:, (p % 2 * 2 + t) * P:(p % 2 * 2 + t + 1) * P], sel[:, t, p, :], ident)
                            last = T.matmul(ps[7][:, p:p + 1], sel[:, t, p, :], gx[:, t, p:p + 1],
                                            start=(t == 0), stop=(t == 1))
                            if t and p < 2:
                                last.then_inc(scattered if p else matok_turned, PRIME)
                    link.end_phase()
                    link.end_phase()

                    def gather(pi):
                        for k in range(KT):
                            for t in range(2):
                                last = T.matmul(ps[6 + k // 4][:, k % 4 * P:(k % 4 + 1) * P],
                                                htok[:, t, k * P:(k + 1) * P],
                                                sel[:, t, bass.ds(pi, 1), :].rearrange("p a b -> p (a b)"),
                                                start=(t == 0), stop=(t == 1))
                        last.then_inc(gathered, 1)

                    def expert(pi, narrow):
                        j = 0

                        def full_moe(j):
                            pe.wait_ge(slot_full[(S_MOE + j) % RING], pi * MOE_INC + moe_landed(j))

                        def project(bank, j):
                            for h in range(2):
                                full_moe(j + h)
                                for k in range(4):
                                    for ct in range(2 if narrow else 1):
                                        r_ = slice(ct * NARROW, (ct + 1) * NARROW) if narrow else slice(0, P)
                                        c_ = slice(ct * 2 * P, (ct + 1) * 2 * P) if narrow else slice(0, MOE_F)
                                        last = T.matmul(ps[bank][r_, 0:c_.stop - c_.start], xg[:, 4 * h + k, r_],
                                                        half_k(S_MOE + j + h)[:, k, c_],
                                                        start=(h + k == 0), stop=(h + k == 4))
                                last.then_inc(slot_used, 1)

                        def turn(r):
                            pe.wait_ge(act_ready, pi * MOE_ROUNDS + (A0 + r + 1))
                            if r == 0:
                                pe.wait_ge(down_added, (pi - 1) * KT + (ADD0 + 8))
                            pe.wait_ge(aT_ready, pi * MOE_ROUNDS + (PRIME + r))
                            for f in range(2 if narrow else 4):
                                last = T.transpose(ps[3][:, f * P:(f + 1) * P], matok[:, f * P:(f + 1) * P], ident)
                            last.then_inc(matok_turned, 1)

                        def down(r, j):
                            pe.wait_ge(aT_ready, pi * MOE_ROUNDS + (PRIME + r + 1))
                            if r == 0:
                                pe.wait_ge(y_copied, pi * 2 + PRIME)
                            for h in range(2):
                                full_moe(j + h)
                                for f in range(2):
                                    for half in range(2):
                                        r_ = slice(half * NARROW, (half + 1) * NARROW) if narrow else slice(0, P)
                                        last = T.matmul(ps[4 + half][r_, :], aT[:, r % 2, 2 * h + f, 0:r_.stop - r_.start],
                                                        deep(S_MOE + j + h)[:, f, half * 512:(half + 1) * 512],
                                                        start=(r + h + f == 0),
                                                        stop=(r == MOE_ROUNDS - 1 and h + f == 2))
                                last.then_inc(slot_used, 1)

                        pe.wait_ge(xg_ready, pi + 1)
                        for r in range(MOE_ROUNDS):
                            if r == 0:
                                pe.wait_ge(down_added, (pi - 1) * KT + (ADD0 + 2))
                            if r == 1:
                                pe.wait_ge(down_added, (pi - 1) * KT + (ADD0 + 4))
                            pe.wait_ge(sil_ready, pi * MOE_ROUNDS + (SIL0 + r - (r > 0)))
                            project(r % 2, j)
                            j += 2
                            if r:
                                turn(r - 1)
                            else:
                                pe.wait_ge(down_added, (pi - 1) * KT + (ADD0 + 6))
                            pe.wait_ge(act_ready, pi * MOE_ROUNDS + (A0 + r))
                            project(2, j)
                            j += 2
                            if r:
                                down(r - 1, j)
                                j += 2
                        turn(MOE_ROUNDS - 1)
                        gather(pi + 1)
                        down(MOE_ROUNDS - 1, j)
                        pe.wait_ge(y_copied, pi * 2 + (PRIME + 2))
                        for d in range(KT):
                            r_ = slice(d // 4 * NARROW, (d // 4 + 1) * NARROW) if narrow else slice(0, P)
                            last = T.matmul(ps[d // 2][:, d % 2 * SEQ:(d % 2 + 1) * SEQ], ytok[r_, d * P:(d + 1) * P],
                                            selnow[r_, :], start=True,
                                            stop=True)
                            last.then_inc(scattered, 1)

                    gather(0)
                    def either(pi):
                        slim = pe.value_load(meta[0:1, bass.ds(pi + (1 + EXTRA), 1)], min_val=0, max_val=1)
                        with pe.If(slim > 0):
                            expert(pi, True)
                        with pe.If(slim < 1):
                            expert(pi, False)

                    pe.wait_ge(meta_ready, 1)
                    with pe.Fori(0, N_EXPERTS) as pi:
                        either(pi)
                    n_over = pe.value_load(meta[0:1, 0:1], min_val=0, max_val=EXTRA)
                    with pe.Fori(0, EXTRA) as p:
                        with pe.If(p < n_over):
                            either(p + N_EXPERTS)
                    link.end_phase()
            rms(SEQ)
            for k in range(KT):
                for t in range(2):
                    T.transpose(ps[k][:, t * P:(t + 1) * P], hT[:, k, SEQ + t * P:SEQ + (t + 1) * P], ident)
            link.end_phase()
            ended.append(link.phases)

        @block.scalar
        def _(ac):
            link = Link(ac, act_chain)
            A = nc.scalar

            def rms(lo):
                for k in range(4):
                    link(A.activation(hT[:, k, lo:N_TOK], xT[:, k, lo:N_TOK], ACT.Square))
                link.end_phase()
                link.end_phase()
                link(A.activation(rms_s[:, lo:N_TOK], ps[0][:, lo:N_TOK], ACT.Sqrt, scale=1.0 / D_MODEL,
                                  bias=eps_col))
                link.end_phase()

            def modulated(which, lo, base):
                for k in range(KT):
                    ac.wait_ge(normed, base + k + 1)
                    for st_ in range(lo // SEQ, 2):
                        cols = slice(st_ * SEQ, (st_ + 1) * SEQ)
                        link(A.activation(hT[:, k, cols], hT[:, k, cols], ACT.Identity,
                                          scale=amul[:, which, k, st_:st_ + 1],
                                          bias=mod[:, 3 * which * KT + k, st_:st_ + 1]))
                link.end_phase()

            link.end_phase()
            for k in range(4, KT):
                link(A.copy(xT[:, k, :], ps[k][:, :]))
            link.end_phase()
            link.end_phase()
            link(A.copy(vcol2[:, :], ps[0][:, 0:3 * KT]))
            for st_ in range(2):
                link(A.activation(cs[:, :, st_], vcol2[:, st_ * KT:(st_ + 1) * KT], ACT.Silu))
            link.end_phase()

            def hyena(lo):
                for dst in (hh1, hh2):
                    link.end_phase()
                    link.end_phase()
                    link(A.activation(dst[0:HEAD, :], htmp[0:HEAD, :], ACT.Sin))
                    link.end_phase()
                link.end_phase()
                link.end_phase()
                sq = [kre[:, 0], kre[:, 1], kim[:, 0], kim[:, 1]]
                for n in range(4):
                    link(A.activation(sq[n], kern[:, n // 2, n % 2, :], ACT.Square))
                link.end_phase()
                link.end_phase()
                link(A.activation(hnorm[:, :], ps[4][:, :], ACT.Sqrt, bias=eps_col))
                link.end_phase()
                link.end_phase()
                link.end_phase()
                link.end_phase()
                for t in range(2):
                    link(A.copy(ut[:, t, lo:N_TOK], ps[t][:, lo:N_TOK]))
                link.end_phase()
                for _ in range(8):
                    link.end_phase()

            def attention(layer):
                link.end_phase()
                link.end_phase()
                base, todo = ATT_BASE[layer], jobs(layer)

                def exps(n):
                    lat, i, half, qt = todo[n]
                    keys = N_TOK if lat else SEQ
                    b = n % 2
                    h = i + SW_TILES * half
                    ac.wait_ge(max_ready, base + n + 1)
                    link(A.activation(st[:, b, 2:3], rows[:, 24 + h:25 + h], ACT.Exp, bias=st[:, b, 0:1]))
                    A.activation(sc[:, b, 0:keys], sc[:, b, 0:keys], ACT.Exp, bias=st[:, b, 0:1],
                                 accum_out=st[:, b, 1:2]).then_inc(exp_ready, 1)
                    ac.wait_ge(exp_ready, base + n + 1)

                def copies(n):
                    nk = 4 if todo[n][0] else 2
                    ac.wait_ge(turn_ready, base + n + 1)
                    if n >= 2:
                        ac.wait_ge(pv_ready, base + n - 1)
                    A.copy(pT[:, n % 2, 0:nk * P], ps[2 + n % 2][:, 0:nk * P]).then_inc(turn_read, 1)
                    ac.wait_ge(turn_read, base + n + 1)

                for it in range(len(todo) + 1):
                    if it < len(todo):
                        exps(it)
                    if it:
                        copies(it - 1)
                link.end_phase()

            def delta(layer, lo):
                for i in range(6):
                    link(A.activation(XT_flat(i), qkv[:, i, :], ACT.Square))
                link(A.activation(bt[:, :, :], abv[:, :, 12:24], ACT.Sigmoid))
                link.end_phase()
                link.end_phase()
                for i in range(6):
                    link(A.activation(XT_flat(i), ps[i][:, :], ACT.Sqrt, bias=eps_col))
                link(A.activation(gtmp[:, :, :], gtmp[:, :, :], ACT.Exp, scale=-1.0))
                link(A.activation(gtmp2[:, :, :], gtmp[:, :, :], ACT.Ln, bias=one_col))
                link(A.activation(rows[:, 0:12], rows[:, 0:12], ACT.Exp))
                link.end_phase()
                link.end_phase()
                link.end_phase()
                for t in range(TT):
                    link(A.copy(ktok[:, t, :], ps[2 * t][:, 0:3 * P]))
                link.end_phase()
                link.end_phase()
                link(A.copy(gc[:, :, :].rearrange("p a b -> p (a b)"), ps[0][:, 0:TT * PROBS]))
                link(A.activation(eg[:, :, :], gc[:, :, :], ACT.Exp))
                link.end_phase()
                for i in range(4):
                    G0, D0 = (layer * 4 + i) * 4, (layer * 4 + i) * DIRS
                    if i:
                        ac.wait_ge(state_ready, D0)
                    for g, d, qs in GROUPS:
                        r_ = slice(g % 2 * HEAD, (g % 2 + 1) * HEAD)
                        ac.wait_ge(r_ready, G0 + g + 1)
                        A.activation(egb[r_, d * PAIRS:(d + 1) * PAIRS, :], three(g)[r_, :, :],
                                     ACT.Exp).then_inc(egb_ready, 1)
                    for g, d, qs in GROUPS:
                        ac.wait_ge(diff_ready, G0 + g + 1)
                        A.activation(Amat[:, qs, :], Amat[:, qs, :], ACT.Exp).then_inc(decay_ready, 1)
                    A.activation(kds[:, :], kds[:, :], ACT.Exp).then_inc(kds_ready, 1)
                    for g, d, qs in GROUPS:
                        ac.wait_ge(xt_turned, G0 + g + 1)
                        A.copy(Xm[:, qs, :], three(g)).then_inc(xm_ready, 1)
                    for lv in range(1, LEVELS):
                        for g, d, qs in GROUPS:
                            ix = lvl_index(layer, i, lv, g)
                            ac.wait_ge(b_ready, ix + 1)
                            if lv > 1:
                                ac.wait_ge(p_ready, ix - 3)
                            A.copy(Bm[:, qs, :], three(g)).then_inc(b_copied, 1)
                            ac.wait_ge(b_copied, ix + 1)
                    for d in range(DIRS):
                        ac.wait_ge(v_ready, D0 + d + 1)
                        A.copy(vnew[:, d * DN_HEADS:(d + 1) * DN_HEADS, :], six(2 + d)).then_inc(vnew_ready, 1)
                link.end_phase()
                for j in range(PAIRS):
                    link(A.activation(XT_flat(j)[:, lo:N_TOK], hT[:, j, lo:N_TOK], ACT.Square))
                link.end_phase()
                link.end_phase()
                for j in range(PAIRS):
                    link(A.activation(XT_flat(j)[:, lo:N_TOK], ps[j][:, lo:N_TOK], ACT.Sqrt, scale=1.0 / HEAD,
                                      bias=eps_col))
                link.end_phase()
                link.end_phase()

            def silus(R, ft, lo, first):
                ac.wait_ge(gu_ready, 2 * R + ft + 1)
                if not first:
                    ac.wait_ge(act_ready, 2 * R + ft - 1)
                A.activation(sil[:, ft, lo:N_TOK], ps[2 * ft][:, lo:N_TOK], ACT.Silu).then_inc(sil_ready, 1)

            n_normed = 0
            for layer in range(N_LAYERS):
                last_layer = layer == N_LAYERS - 1
                lo = SEQ if last_layer else 0
                for b in range(MOD_SLOTS // 2):
                    ac.wait_ge(mod_ready, layer * MOD_SLOTS + 2 * b + 2)
                    A.copy(modr(b), ps[2 + b % 6][0:2, :]).then_inc(mod_copied, 1)
                link.end_phase()
                link.end_phase()
                rms(0)
                modulated(0, 0, n_normed)
                n_normed += KT
                kinds = ["abv"] * 2 + [k for k, _ in in_tiles]
                for n in range(2, len(kinds)):
                    kind, i = in_tiles[n - 2]
                    if kind == "hy":
                        continue
                    if kind == "dn":
                        who, per, upto = read_before(n)
                        ac.wait_ge(who, layer * per + upto)
                        link(A.activation(qkv[:, i, :], qkv[:, i, :], ACT.Silu))
                        continue
                    ac.wait_ge(proj_ready, layer * len(kinds) + n + 1)
                    _, per, upto = read_before(n)
                    if kind == "z":
                        A.activation(zz[:, i, lo:N_TOK], ps[n % 4][:, lo:N_TOK], ACT.Silu).then_inc(copy_done, 1)
                    elif kind == "q":
                        A.copy(qT[:, i, lo:N_TOK], ps[n % 4][:, lo:N_TOK]).then_inc(copy_done, 1)
                    else:
                        A.copy(kT[:, :], ps[n % 4][:, :]).then_inc(copy_done, 1)
                    ac.wait_ge(copy_done, layer * per + upto)
                link.end_phase()
                hyena(lo)
                attention(layer)
                delta(layer, lo)
                link.end_phase()
                rms(lo)
                modulated(1, lo, n_normed)
                n_normed += KT
                if not last_layer:
                    for r in range(DENSE_ROUNDS):
                        for ft in range(2):
                            silus(r, ft, lo, r == 0)
                    link.end_phase()
                else:
                    link.end_phase()
                    for n in range(4):
                        link(A.copy(htok[:, n // 2, n % 2 * 512:(n % 2 + 1) * 512], ps[1 + n][:, :]))
                    link.end_phase()
                    link(A.activation(tmp8[:, :, 0:1], tmp8[:, :, 0:1], ACT.Exp))
                    link.end_phase()
                    link.end_phase()
                    link.end_phase()
                    link.end_phase()
                    link.end_phase()
                    for b in range(6):
                        w = min(2, PASSES - 2 * b)
                        last = A.copy(selT[:, 2 * b:2 * b + w, :], ps[b][:, 0:w * SEQ].rearrange("p (a b) -> p a b", a=w))
                        if b == 4:
                            last.then_inc(aT_ready, PRIME)
                        elif b == 5:
                            last.then_inc(y_copied, PRIME)
                        else:
                            link(last)
                    ac.wait_ge(y_copied, PRIME)
                    link.end_phase()

                    def fetch(pi):
                        A.copy(xg[:, 0:4, :], ps[6][:, :].rearrange("p (a b) -> p a b", a=4))
                        A.copy(xg[:, 4:8, :], ps[7][:, :].rearrange("p (a b) -> p a b", a=4)).then_inc(xg_ready, 1)

                    def copy_turn(pi, r, narrow):
                        ac.wait_ge(matok_turned, pi * MOE_ROUNDS + (PRIME + r + 1))
                        if r >= 2:
                            ac.wait_ge(slot_used, pi * len(MOE_ORDER) + (d_done[r - 2]))
                        elif r == 0:
                            ac.wait_ge(y_copied, pi * 2 + PRIME)
                        if narrow:
                            A.copy(aT[:, r % 2, :, 0:NARROW].rearrange("p (a f) n -> p f a n", f=2),
                                   ps[3][:, 0:2 * P].rearrange("p (f a n) -> p f a n", f=2, a=2)).then_inc(aT_ready, 1)
                        else:
                            A.copy(aT[:, r % 2, :, :],
                                   ps[3][:, :].rearrange("p (a b) -> p a b", a=4)).then_inc(aT_ready, 1)

                    def expert(pi, narrow):
                        w = MOE_F // 2 if narrow else MOE_F
                        for r in range(MOE_ROUNDS):
                            ac.wait_ge(slot_used, pi * len(MOE_ORDER) + g_done[r])
                            ac.wait_ge(act_ready, pi * MOE_ROUNDS + (A0 + r))
                            A.activation(msil[:, 0:w], ps[r % 2][:, 0:w], ACT.Silu).then_inc(sil_ready, 1)
                            if r:
                                copy_turn(pi, r - 1, narrow)
                        copy_turn(pi, MOE_ROUNDS - 1, narrow)
                        fetch_next(pi)
                        ac.wait_ge(scattered, pi * KT + PRIME)
                        A.copy(selnow[:, :], selT[:, bass.ds(pi, 1), :].rearrange("p a b -> p (a b)"))
                        ac.wait_ge(slot_used, (pi + 1) * len(MOE_ORDER))
                        for half in range(2):
                            r_ = slice(half * NARROW, (half + 1) * NARROW) if narrow else slice(0, P)
                            A.copy(ytok[r_, half * 512:(half + 1) * 512], ps[4 + half][r_, :]).then_inc(y_copied, 1)

                    def fetch_next(pi):
                        ac.wait_ge(gathered, pi + 2)
                        fetch(pi + 1)

                    ac.wait_ge(gathered, 1)
                    fetch(0)
                    def either(pi):
                        slim = ac.value_load(meta[0:1, bass.ds(pi + (1 + EXTRA), 1)], min_val=0, max_val=1)
                        with ac.If(slim > 0):
                            expert(pi, True)
                        with ac.If(slim < 1):
                            expert(pi, False)

                    ac.wait_ge(meta_ready, 1)
                    with ac.Fori(0, N_EXPERTS) as pi:
                        either(pi)
                    n_over = ac.value_load(meta[0:1, 0:1], min_val=0, max_val=EXTRA)
                    with ac.Fori(0, EXTRA) as p:
                        with ac.If(p < n_over):
                            either(p + N_EXPERTS)
                    link.end_phase()
            rms(SEQ)
            for k in range(KT):
                ac.wait_ge(normed, n_normed + k + 1)
                link(A.activation(hT[:, k, SEQ:N_TOK], hT[:, k, SEQ:N_TOK], ACT.Copy,
                                  scale=vcol2[:, 2 * KT + k:2 * KT + k + 1]))
            link.end_phase()
            link.end_phase()
            for k in range(4):
                for t in range(2):
                    link(A.copy(hT[:, 2 * t + k // 4, k % 4 * P:(k % 4 + 1) * P], ps[k][:, t * P:(t + 1) * P]))
            ac.drain().then_inc(rows_out, 1)
            ended.append(link.phases)

        @block.vector
        def _(ve):
            link = Link(ve, dve_chain)
            V = nc.vector

            def tt(out, a_, b_, op):
                link(V.tensor_tensor(out, a_, b_, op))

            def rms(lo, base):
                for k in range(4, KT):
                    tt(hT[:, k, lo:N_TOK], xT[:, k, lo:N_TOK], xT[:, k, lo:N_TOK], ALU.mult)
                link.end_phase()
                link.end_phase()
                link.end_phase()
                link(V.reciprocal(rms_r[:, lo:N_TOK], rms_s[:, lo:N_TOK]))
                for k in range(KT):
                    V.tensor_tensor(hT[:, k, lo:N_TOK], xT[:, k, lo:N_TOK], rms_r[:, lo:N_TOK],
                                    ALU.mult).then_inc(normed, 1)
                link.end_phase()

            link(V.memset(eps_col, RMS_EPS))
            link(V.memset(one_col, 1.0))
            link.end_phase()
            for k in range(4):
                link(V.tensor_copy(xT[:, k, :], ps[k][:, :]))
            link.end_phase()
            link.end_phase()
            link.end_phase()

            def conv(dst, src, lo, w, j0, j, n):
                d3, s3 = seg(dst, lo), seg(src, lo)
                link(V.tensor_scalar(dst[:, lo:N_TOK], src[:, lo:N_TOK], vcol[:, w + n + j:w + n + j + 1], None, ALU.mult))
                link(V.scalar_tensor_tensor(out=d3[:, :, 1:SEQ], in0=s3[:, :, 0:SEQ - 1], scalar=vcol[:, w + j:w + j + 1],
                                            in1=d3[:, :, 1:SEQ], op0=ALU.mult, op1=ALU.add))
                return V.scalar_tensor_tensor(out=d3[:, :, 0:SEQ - 1], in0=s3[:, :, 1:SEQ],
                                              scalar=vcol[:, w + 2 * n + j:w + 2 * n + j + 1],
                                              in1=d3[:, :, 0:SEQ - 1], op0=ALU.mult, op1=ALU.add)

            def hyena(lo):
                for layer_b, layer_f in ((V_B1, V_FR1), (V_B2, V_FR2)):
                    link.end_phase()
                    h, n = htmp[0:HEAD, :], htmp2[0:HEAD, :]
                    link(V.tensor_scalar(h, ps[0][0:HEAD, 0:SEQ], vcol[0:HEAD, layer_b:layer_b + 1],
                                         vcol[0:HEAD, layer_f:layer_f + 1], ALU.add, ALU.mult))
                    link(V.tensor_scalar(n, h, 1.0 / (2 * np.pi), None, ALU.mult))
                    link(V.tensor_scalar(n, n, ROUND, None, ALU.add))
                    link(V.tensor_scalar(n, n, -ROUND, None, ALU.add))
                    for part in TWO_PI:
                        link(V.scalar_tensor_tensor(out=h, in0=n, scalar=-part, in1=h, op0=ALU.mult, op1=ALU.add))
                    link(V.tensor_scalar(h, h, PI_BELOW, -PI_BELOW, ALU.min, ALU.max))
                    link.end_phase()
                    link.end_phase()
                link.end_phase()
                for mt in range(2):
                    for d in range(2):
                        w = hc[:, H_WIN + (2 * mt + d) * HY_CH:H_WIN + (2 * mt + d + 1) * HY_CH]
                        tt(kern[:, mt, d, :].rearrange("p (o c) -> p o c", o=2),
                           ps[2 * mt + d][:, :].rearrange("p (o c) -> p o c", o=2),
                           w.unsqueeze(1).to_broadcast([P, 2, HY_CH]), ALU.mult)
                link.end_phase()
                link.end_phase()
                link.end_phase()
                for mt in range(2):
                    tt(kre[:, mt], kern[:, mt, 0, :], kern[:, mt, 1, :], ALU.add)
                    tt(kern[:, mt, 1, :], kern[:, mt, 1, :], kern[:, mt, 0, :], ALU.subtract)
                link.end_phase()
                link(V.reciprocal(hnorm[:, :], hnorm[:, :]))
                link.end_phase()
                for f in range(2):
                    tt(kre[:, f], ps[f][:, :], hnorm[:, :], ALU.mult)
                    tt(kre[:, f], kre[:, f], hskip[:, :], ALU.add)
                    tt(kim[:, f], ps[2 + f][:, :], hnorm[:, :], ALU.mult)
                link.end_phase()
                link.end_phase()
                for t in range(2):
                    link(V.tensor_copy(x1t[:, t, lo:N_TOK], ps[2 + t][:, lo:N_TOK]))
                link.end_phase()
                for order in range(2):
                    link.end_phase()
                    for f in range(2):
                        o = slice(order * HY_CH, (order + 1) * HY_CH)
                        kr = kre[:, f, o].unsqueeze(1).to_broadcast([P, SEG(lo), HY_CH])
                        ki = kim[:, f, o].unsqueeze(1).to_broadcast([P, SEG(lo), HY_CH])
                        ur, us = seg(ps[f], lo), seg(ps[2 + f], lo)
                        pr, pi_, tm = seg(pre[:, f], lo), seg(pim[:, f], lo), seg(ptmp, lo)
                        tt(pr, ur, kr, ALU.mult)
                        tt(tm, us, ki, ALU.mult)
                        tt(pr, pr, tm, ALU.add)
                        tt(pi_, ur, ki, ALU.mult)
                        tt(tm, us, kr, ALU.mult)
                        tt(pi_, pi_, tm, ALU.subtract)
                    link.end_phase()
                    link.end_phase()
                    for t in range(2):
                        if order == 0:
                            tt(ut[:, t, lo:N_TOK], ps[t][:, lo:N_TOK], x1t[:, t, lo:N_TOK], ALU.mult)
                        else:
                            tt(hT[:, PAIRS + t, lo:N_TOK], ps[t][:, lo:N_TOK], hy[:, 4 + t, lo:N_TOK], ALU.mult)
                    link.end_phase()

            def attention(layer):
                link.end_phase()
                for i in range(4):
                    x_ = qT[:, i, SEQ:N_TOK] if i < SW_TILES else kT[:, SEQ:N_TOK]
                    tt(rot[:, i, :], ps[i // 2][:, i % 2 * SEQ:(i % 2 + 1) * SEQ], con[:, K_SIN:K_SIN + SEQ], ALU.mult)
                    tt(x_, x_, con[:, K_COS:K_COS + SEQ], ALU.mult)
                    tt(x_, x_, rot[:, i, :], ALU.add)
                link.end_phase()
                base, todo = ATT_BASE[layer], jobs(layer)

                def maxima(n):
                    lat, i, half, qt = todo[n]
                    keys = N_TOK if lat else SEQ
                    b = n % 2
                    h = i + SW_TILES * half
                    ve.wait_ge(score_ready, base + n + 1)
                    if n >= 2:
                        ve.wait_ge(turn_ready, base + n - 1)
                    if lat:
                        band = con[:, K_BAND + qt * N_TOK:K_BAND + (qt + 1) * N_TOK]
                        V.scalar_tensor_tensor(out=sc[:, b, :], in0=ps[b][:, :], scalar=HEAD ** -0.5, in1=band,
                                               op0=ALU.mult, op1=ALU.add).then_inc(score_read, 1)
                    else:
                        V.tensor_scalar(sc[:, b, 0:keys], ps[b][:, 0:keys], HEAD ** -0.5, None,
                                        ALU.mult).then_inc(score_read, 1)
                    ve.wait_ge(score_read, base + n + 1)
                    link(V.tensor_reduce(st[:, b, 3:4], sc[:, b, 0:keys], X_AXIS, ALU.max))
                    V.tensor_scalar(st[:, b, 0:1], st[:, b, 3:4], rows[:, 24 + h:25 + h], -1.0, ALU.max,
                                    ALU.mult).then_inc(max_ready, 1)

                def divide(n):
                    b = n % 2
                    keys = N_TOK if todo[n][0] else SEQ
                    ve.wait_ge(exp_ready, base + n + 1)
                    tt(st[:, b, 4:5], st[:, b, 1:2], st[:, b, 2:3], ALU.add)
                    link(V.reciprocal(st[:, b, 5:6], st[:, b, 4:5]))
                    V.tensor_scalar(sc[:, b, 0:keys], sc[:, b, 0:keys], st[:, b, 5:6], None,
                                    ALU.mult).then_inc(prob_ready, 1)

                def outputs(n):
                    lat, i, half, qt = todo[n]
                    rows_ = slice(half * HEAD, (half + 1) * HEAD)
                    ve.wait_ge(pv_ready, base + n + 1)
                    q0 = lat * SEQ + qt * P
                    V.tensor_copy(hT[rows_, PAIRS + 2 + i, q0:q0 + P], ps[4 + n % 2][rows_, 0:P]).then_inc(pv_read, 1)

                for it in range(len(todo) + 2):
                    if it < len(todo):
                        maxima(it)
                    if 1 <= it <= len(todo):
                        divide(it - 1)
                    if it >= 2:
                        outputs(it - 2)
                link.end_phase()

            def delta(layer, lo):
                dtb = rows[:, 12:24].unsqueeze(1).to_broadcast([P, TT, PROBS])
                tt(gt[:, :, :], abv[:, :, 0:12], dtb, ALU.add)
                link(V.tensor_scalar(gtmp2[:, :, :], gt[:, :, :], -1.0, None, ALU.mult))
                tt(gtmp[:, :, :], gt[:, :, :], gtmp2[:, :, :], ALU.max)
                link.end_phase()
                link.end_phase()
                link.end_phase()
                link(V.tensor_scalar(gc[:, :, :], gtmp[:, :, :], 1.0, None, ALU.add))
                link(V.tensor_scalar(gc[:, :, :], gc[:, :, :], -1.0, None, ALU.add))
                link(V.tensor_scalar(gc[:, :, :], gc[:, :, :], TINY, None, ALU.add))
                link(V.reciprocal(eg[:, :, :], gc[:, :, :]))
                link(V.tensor_scalar(gtmp2[:, :, :], gtmp2[:, :, :], TINY, None, ALU.add))
                tt(gtmp2[:, :, :], gtmp2[:, :, :], eg[:, :, :], ALU.mult)
                tt(gtmp2[:, :, :], gtmp2[:, :, :], gtmp[:, :, :], ALU.mult)
                link(V.scalar_tensor_tensor(out=gt[:, :, :], in0=gt[:, :, :], scalar=0.0, in1=gtmp2[:, :, :],
                                            op0=ALU.max, op1=ALU.add))
                link(V.scalar_tensor_tensor(out=gt[:, :, :], in0=gt[:, :, :], scalar=-1.0,
                                            in1=rows[:, 0:12].unsqueeze(1).to_broadcast([P, TT, PROBS]),
                                            op0=ALU.mult, op1=ALU.mult))
                for i in range(6):
                    link(V.reciprocal(XT_flat(i), XT_flat(i)))
                    link(V.scalar_tensor_tensor(out=qkv[:, i, :], in0=qkv[:, i, :], scalar=(HEAD ** -0.5 if i < 3 else 1.0),
                                                in1=XT_flat(i), op0=ALU.mult, op1=ALU.mult))
                link.end_phase()
                link.end_phase()
                for t in range(TT):
                    link(V.tensor_copy(vtok[:, t, :], ps[2 * t + 1][:, 0:3 * P]))
                link.end_phase()
                link.end_phase()
                link.end_phase()
                for i in range(4):
                    G0, D0 = (layer * 4 + i) * 4, (layer * 4 + i) * DIRS
                    for g, d, qs in GROUPS:
                        tile = STEP_TILES[i][d]
                        end = P - 1 if d == 0 else 0
                        ve.wait_ge(egb_ready, G0 + g + 1)
                        for n, q in enumerate(range(3 * g, 3 * g + 3)):
                            V.tensor_scalar(Amat[:, q, :], ps[g][:, n * P:(n + 1) * P], gc[:, tile, col(q):col(q) + 1], 0.0,
                                            ALU.subtract, ALU.min)
                        V.tensor_tensor(kds[:, cols3(g)], three(g)[:, :, end:end + 1].rearrange("p a b -> p (a b)"),
                                        gc[:, tile, cols3(g)], ALU.subtract).then_inc(diff_ready, 1)
                    for d in range(DIRS):
                        cols = slice(STEP_TILES[i][d] * P, (STEP_TILES[i][d] + 1) * P)
                        ve.wait_ge(beta_ready, D0 + d + 1)
                        V.tensor_tensor(kb[:, d * PAIRS:(d + 1) * PAIRS, :], three(4 + d), qkv[:, PAIRS:2 * PAIRS, cols],
                                        ALU.mult).then_inc(kb_ready, 1)

                    def mask_scores(g):
                        ve.wait_ge(kq_ready, G0 + g + 1)
                        ve.wait_ge(decay_ready, G0 + g + 1)
                        V.tensor_tensor(QK[:, 3 * g:3 * g + 3, :], three(6 + g % 2), Amat[:, 3 * g:3 * g + 3, :],
                                        ALU.mult).then_inc(qk_read, 1)

                    def first_inverse(g):
                        qs = slice(3 * g, 3 * g + 3)
                        ve.wait_ge(kk_ready, G0 + g + 1)
                        V.tensor_tensor(Amat[:, qs, :], three(4 + g % 2), Amat[:, qs, :], ALU.mult).then_inc(a_ready, 1)
                        ve.wait_ge(a_ready, G0 + g + 1)
                        tt(XT[:, qs, :], Amat[:, qs, :], mask(K_LVL + g // 2 * LEVELS * P), ALU.mult)
                        V.tensor_tensor(XT[:, qs, :], mask(K_ID), XT[:, qs, :], ALU.subtract).then_inc(x0_ready, 1)

                    mask_scores(0)
                    mask_scores(1)
                    first_inverse(0)
                    first_inverse(1)
                    mask_scores(2)
                    mask_scores(3)
                    first_inverse(2)
                    first_inverse(3)
                    for d in range(DIRS):
                        tile = STEP_TILES[i][d]
                        qs = slice(d * DN_HEADS, (d + 1) * DN_HEADS)
                        ve.wait_ge(ks_ready, D0 + d + 1)
                        tt(rhs[:, qs, :], six(6 + d), over(eg[:, tile, qs], HEAD), ALU.mult)
                        tt(rhs[:, qs, :], vtok[:, tile, :].rearrange("p (a b) -> p a b", a=DN_HEADS), rhs[:, qs, :],
                           ALU.subtract)
                        V.tensor_tensor(rhs[:, qs, :], rhs[:, qs, :], over(bt[:, tile, qs], HEAD),
                                        ALU.mult).then_inc(rhs_ready, 1)
                    ve.wait_ge(egb_ready, G0 + 4)
                    for d in range(DIRS):
                        cols = slice(STEP_TILES[i][d] * P, (STEP_TILES[i][d] + 1) * P)
                        V.tensor_tensor(qd[:, d * PAIRS:(d + 1) * PAIRS, :], egb[:, d * PAIRS:(d + 1) * PAIRS, :],
                                        qkv[:, 0:PAIRS, cols], ALU.mult).then_inc(qd_ready, 1)
                    for lv in range(1, LEVELS):
                        for g, d, qs in GROUPS:
                            ix = lvl_index(layer, i, lv, g)
                            ve.wait_ge(p_ready, ix + 1)
                            if lv < LEVELS - 1:
                                V.tensor_tensor(Xm[:, qs, :], Xm[:, qs, :], three(4 + g % 2 * 2), ALU.subtract)
                            V.tensor_tensor(XT[:, qs, :], XT[:, qs, :], three(5 + g % 2 * 2),
                                            ALU.subtract).then_inc(x_done, 1)
                            ve.wait_ge(x_done, ix + 1)
                    for d in range(DIRS):
                        end = P - 1 if d == 0 else 0
                        pd = slice(d * PAIRS, (d + 1) * PAIRS)
                        ve.wait_ge(out_ready, D0 + d + 1)
                        tile = STEP_TILES[i][d]
                        o_ = hT[:, 0:PAIRS, tile * P:(tile + 1) * P]
                        if i % 2 == 0 and not (layer == N_LAYERS - 1 and i < 2):
                            V.tensor_copy(o_, three(4 + d))
                        elif not (layer == N_LAYERS - 1 and i < 2):
                            V.tensor_tensor(o_, three(4 + d), o_, ALU.add)
                        for half in range(2):
                            r_ = slice(half * HEAD, (half + 1) * HEAD)
                            tt(state[r_, pd, r_], state[r_, pd, r_],
                               egb[r_, pd, end:end + 1].to_broadcast([HEAD, PAIRS, HEAD]), ALU.mult)
                            last = V.tensor_tensor(state[r_, pd, r_], three(6 + d)[r_, :, r_], state[r_, pd, r_], ALU.add)
                        last.then_inc(state_ready, 1)
                        ve.wait_ge(state_ready, D0 + d + 1)
                link.end_phase()
                link.end_phase()
                link.end_phase()
                link.end_phase()
                for j in range(PAIRS):
                    x_ = XT_flat(j)[:, lo:N_TOK]
                    link(V.reciprocal(x_, x_))
                    link(V.scalar_tensor_tensor(out=x_, in0=x_, scalar=vcol[:, V_DNG:V_DNG + 1], in1=zz[:, j, lo:N_TOK],
                                                op0=ALU.mult, op1=ALU.mult))
                    tt(hT[:, j, lo:N_TOK], hT[:, j, lo:N_TOK], x_, ALU.mult)
                link.end_phase()

            def gated(R, ft, par, lo, first):
                ve.wait_ge(sil_ready, 2 * R + ft + 1)
                if not first:
                    ve.wait_ge(down_ready, KT * (R - 1))
                V.tensor_tensor(act[:, par, ft, lo:N_TOK], sil[:, ft, lo:N_TOK], ps[2 * ft + 1][:, lo:N_TOK],
                                ALU.mult).then_inc(act_ready, 1)

            def add_down(R, lo):
                for d in range(KT):
                    ve.wait_ge(down_ready, KT * R + d + 1)
                    for st_ in range(lo // SEQ, 2):
                        c = slice(st_ * SEQ, (st_ + 1) * SEQ)
                        last = V.scalar_tensor_tensor(out=xT[:, d, c], in0=ps[4 + d % 4][:, c],
                                                      scalar=mod[:, 5 * KT + d, st_:st_ + 1], in1=xT[:, d, c],
                                                      op0=ALU.mult, op1=ALU.add)
                    last.then_inc(down_added, 1)

            n_normed = 0
            for layer in range(N_LAYERS):
                last_layer = layer == N_LAYERS - 1
                lo = SEQ if last_layer else 0
                link.end_phase()
                link(V.tensor_copy(vcol[:, 0:V_END], ps[1][:, 0:V_END]))
                tt(mod[:, :, :], ps[0][:, 0:2 * N_MOD_TILES].rearrange("p (a b) -> p a b", b=2),
                   over(vcol[:, V_BMOD:V_BMOD + N_MOD_TILES], 2), ALU.add)
                for which, gcol in ((0, V_GMIX), (1, V_GFFN)):
                    m0 = (3 * which + 1) * KT
                    link(V.scalar_tensor_tensor(out=amul[:, which], in0=mod[:, m0:m0 + KT, :], scalar=1.0,
                                                in1=over(vcol[:, gcol:gcol + KT], 2), op0=ALU.add, op1=ALU.mult))
                link.end_phase()
                rms(0, n_normed)
                n_normed += KT
                kinds = ["abv"] * 2 + [k for k, _ in in_tiles]
                for n in range(len(kinds)):
                    if kinds[n] in ("z", "q", "k"):
                        continue
                    ve.wait_ge(proj_ready, layer * len(kinds) + n + 1)
                    _, per, upto = read_before(n)
                    if n < 2:
                        last = V.tensor_copy(abv[:, 2 * n:2 * n + 2, :],
                                             ps[n][:, 0:2 * ABV].rearrange("p (a b) -> p a b", a=2))
                    elif kinds[n] == "dn":
                        i = in_tiles[n - 2][1]
                        last = conv(qkv[:, i, :], ps[n % 4], 0, V_DNC, 0, i, DN_TILES)
                    else:
                        i = in_tiles[n - 2][1]
                        last = conv(hy[:, i, :], ps[n % 4], lo, V_HYC, 0, i, HY_TILES)
                    last.then_inc(conv_done, 1)
                    ve.wait_ge(conv_done, layer * per + upto)
                link.end_phase()
                hyena(lo)
                attention(layer)
                delta(layer, lo)
                for n in range(KT):
                    ve.wait_ge(mix_ready, layer * KT + n + 1)
                    for st_ in range(lo // SEQ, 2):
                        c = slice(st_ * SEQ, (st_ + 1) * SEQ)
                        last = V.scalar_tensor_tensor(out=xT[:, n, c], in0=ps[n % 4][:, c],
                                                      scalar=mod[:, 2 * KT + n, st_:st_ + 1], in1=xT[:, n, c],
                                                      op0=ALU.mult, op1=ALU.add)
                    last.then_inc(mix_added, 1)
                link.end_phase()
                rms(lo, n_normed)
                n_normed += KT
                if not last_layer:
                    for r in range(DENSE_ROUNDS):
                        for ft in range(2):
                            gated(r, ft, r % 2, lo, r < 2)
                        if r:
                            add_down(r - 1, lo)
                    add_down(DENSE_ROUNDS - 1, lo)
                    link.end_phase()
                else:
                    link.end_phase()
                    link(V.tensor_copy(lg[:, :, :], ps[0][:, 0:16].rearrange("p (a b) -> p a b", a=2)))
                    for t in range(2):
                        link(V.max(top[:, t, :], lg[:, t, :]))
                        link(V.max_index(topi[:, t, :], top[:, t, :], lg[:, t, :]))
                    link(V.tensor_copy(tix[:, :, :], topi[:, :, :]))
                    tt(tmp8[:, :, 0:1], top[:, :, 1:2], top[:, :, 0:1], ALU.subtract)
                    link.end_phase()
                    for x_ in (mx, gx, rx):
                        link(V.memset(x_[:, :, :], 0.0))
                    link(V.memset(sel[:, :, PASSES, :], 0.0))
                    link.end_phase()
                    link(V.tensor_scalar(tmp8[:, :, 1:2], tmp8[:, :, 0:1], 1.0, None, ALU.add))
                    link(V.reciprocal(tmp8[:, :, 2:3], tmp8[:, :, 1:2]))
                    tt(tmp8[:, :, 3:4], tmp8[:, :, 2:3], tmp8[:, :, 0:1], ALU.mult)
                    iota = con[:, K_IOTA:K_IOTA + 8]
                    for t in range(2):
                        first, second = tix[:, t, 0:1], tix[:, t, 1:2]
                        for x_, w in ((mx, None), (gx, tmp8)):
                            ops = (ALU.is_equal,) if w is None else (ALU.is_equal, ALU.mult)
                            w1, w2 = (None, None) if w is None else (w[:, t, 2:3], w[:, t, 3:4])
                            link(V.tensor_scalar(x_[:, t, 0:8], iota, first, w1, *ops))
                            link(V.tensor_scalar(top[:, t, :], iota, second, w2, *ops))
                            tt(x_[:, t, 0:8], x_[:, t, 0:8], top[:, t, :], ALU.add)
                    link.end_phase()
                    link.end_phase()
                    link(V.tensor_scalar(rx[:, :, 0:8], ps[0][:, 0:16].rearrange("p (a b) -> p a b", a=2), -1.0, None,
                                         ALU.add))
                    link(V.tensor_scalar(over8[:, :], ps[0][:, 16:24], float(CAP), None, ALU.is_gt))
                    link(V.tensor_tensor_scan(incl8[:, :], ones[:, 0:8], over8[:, :], 0.0, ALU.mult, ALU.add))
                    link(V.tensor_copy(metaf[:, 0:1], incl8[:, 7:8]))
                    slim = metaf[:, 1 + EXTRA:]
                    link(V.tensor_scalar(slim[:, 0:8], ps[0][:, 16:24], float(NARROW), None, ALU.is_le))
                    for p in range(EXTRA):
                        link(V.scalar_tensor_tensor(out=hot8[:, :], in0=incl8[:, :], scalar=float(p + 1), in1=over8[:, :],
                                                    op0=ALU.is_equal, op1=ALU.mult))
                        tt(prod8[:, 0, :], hot8[:, :], iota, ALU.mult)
                        link(V.tensor_reduce(metaf[:, p + 1:p + 2], prod8[:, 0, :], X_AXIS, ALU.add))
                        tt(prod8[:, 0, :], hot8[:, :], ps[0][:, 16:24], ALU.mult)
                        link(V.tensor_reduce(slim[:, 8 + p:9 + p], prod8[:, 0, :], X_AXIS, ALU.add))
                        link(V.tensor_scalar(slim[:, 8 + p:9 + p], slim[:, 8 + p:9 + p], float(CAP + NARROW), None, ALU.is_le))
                        for x_ in (mx, gx, rx):
                            tt(prod8[:, :, :], x_[:, :, 0:8], hot8.unsqueeze(1).to_broadcast([P, 2, 8]), ALU.mult)
                            link(V.tensor_reduce(x_[:, :, 8 + p], prod8[:, :, :], X_AXIS, ALU.add))
                        link(V.tensor_scalar(rx[:, :, 8 + p], rx[:, :, 8 + p], -float(CAP), None, ALU.add))
                    V.tensor_copy(meta[:, :], metaf[:, :]).then_inc(meta_ready, 1)
                    ve.wait_ge(meta_ready, 1)
                    for t in range(2):
                        link(V.scalar_tensor_tensor(out=rxn[:, t, :], in0=slim, scalar=float(NARROW), in1=rx[:, t, 0:PASSES],
                                                    op0=ALU.mult, op1=ALU.add))
                    for p in range(PASSES):
                        for t in range(2):
                            for c0, place in ((0, rx), (NARROW, rxn)):
                                link(V.tensor_scalar(sel[:, t, p, c0:c0 + NARROW], con[:, K_IOTA + c0:K_IOTA + c0 + NARROW],
                                                     place[:, t, p:p + 1], mx[:, t, p:p + 1], ALU.is_equal, ALU.mult))
                    link.end_phase()
                    link.end_phase()
                    link(V.tensor_copy(gplace[:, 0:PASSES], ps[7][:, 0:PASSES]))
                    link.end_phase()

                    def expert(pi, narrow):
                        w = MOE_F // 2 if narrow else MOE_F
                        V.tensor_copy(gpass[:, :], gplace[:, bass.ds(pi, 1)]).then_inc(gpass_set, 1)
                        ve.wait_ge(gpass_set, pi + 1)
                        for r in range(MOE_ROUNDS):
                            ve.wait_ge(sil_ready, pi * MOE_ROUNDS + (SIL0 + r + 1))
                            ve.wait_ge(slot_used, pi * len(MOE_ORDER) + u_done[r])
                            ve.wait_ge(matok_turned, pi * MOE_ROUNDS + (PRIME + r))
                            V.scalar_tensor_tensor(out=matok[:, 0:w], in0=msil[:, 0:w], scalar=gpass, in1=ps[2][:, 0:w],
                                                   op0=ALU.mult, op1=ALU.mult).then_inc(act_ready, 1)
                        for d in range(KT):
                            ve.wait_ge(scattered, pi * KT + (PRIME + d // 2 * 2 + 2))
                            V.scalar_tensor_tensor(out=xT[:, d, SEQ:N_TOK], in0=ps[d // 2][:, d % 2 * SEQ:(d % 2 + 1) * SEQ],
                                                   scalar=mod[:, 5 * KT + d, 1:2], in1=xT[:, d, SEQ:N_TOK],
                                                   op0=ALU.mult, op1=ALU.add).then_inc(down_added, 1)

                    def either(pi):
                        slim = ve.value_load(meta[0:1, bass.ds(pi + (1 + EXTRA), 1)], min_val=0, max_val=1)
                        with ve.If(slim > 0):
                            expert(pi, True)
                        with ve.If(slim < 1):
                            expert(pi, False)

                    ve.wait_ge(meta_ready, 1)
                    with ve.Fori(0, N_EXPERTS) as pi:
                        either(pi)
                    n_over = ve.value_load(meta[0:1, 0:1], min_val=0, max_val=EXTRA)
                    with ve.Fori(0, EXTRA) as p:
                        with ve.If(p < n_over):
                            either(p + N_EXPERTS)
                    link.end_phase()
            rms(SEQ, n_normed)
            link.end_phase()
            for k in range(4, KT):
                for t in range(2):
                    link(V.tensor_copy(hT[:, 2 * t + k // 4, k % 4 * P:(k % 4 + 1) * P], ps[k][:, t * P:(t + 1) * P]))
            ve.drain().then_inc(rows_out, 1)
            ended.append(link.phases)

        @block.gpsimd
        def _(po):
            link = Link(po, pool_chain)
            G = nc.gpsimd
            link(G.memset(vrow[:, :], 0.0))
            for _ in range(4):
                link.end_phase()
            for layer in range(N_LAYERS):
                last_layer = layer == N_LAYERS - 1
                link(G.memset(hh2[HEAD:HEAD + 1, :], 1.0))
                for dst, src in row_loads(layer):
                    po.dma_start(dst, src).then_inc(rows_in, 16)
                n_before = 2 + 4 + 1
                for _ in range(n_before + HY_PHASES + 3):
                    link.end_phase()
                link(G.memset(state[:, :, :], 0.0))
                for _ in range(8):
                    link.end_phase()
                for i in range(4):
                    G0, D0 = (layer * 4 + i) * 4, (layer * 4 + i) * DIRS
                    po.wait_ge(kds_ready, layer * 4 + i + 1)
                    for d in range(DIRS):
                        tile = STEP_TILES[i][d]
                        qs = slice(d * DN_HEADS, (d + 1) * DN_HEADS)
                        G.tensor_tensor(kd[:, d * PAIRS:(d + 1) * PAIRS, :].rearrange("p a (b c) -> p (a b) c", b=2),
                                        ktok[:, tile, :].rearrange("p (a b) -> p a b", a=DN_HEADS),
                                        over(kds[:, qs], HEAD), ALU.mult).then_inc(kd_ready, 1)
                    for lv in range(1, LEVELS):
                        for g, d, qs in GROUPS:
                            ix = lvl_index(layer, i, lv, g)
                            if lv > 1:
                                po.wait_ge(b_ready, ix - 3)
                            else:
                                po.wait_ge(a_ready, G0 + g + 1)
                            G.tensor_tensor(Am[:, qs, :], Amat[:, qs, :], mask(K_LVL + (d * LEVELS + lv) * P),
                                            ALU.mult).then_inc(am_ready, 1)
                        if lv == 1:
                            for g, d, qs in GROUPS:
                                po.wait_ge(qk_read, G0 + g + 1)
                                G.tensor_tensor(QK[:, qs, :], QK[:, qs, :], mask(K_INC + d * P),
                                                ALU.mult).then_inc(qk_ready, 1)
                link.end_phase()
                for _ in range(4):
                    link.end_phase()
                link.end_phase()
                if last_layer:
                    po.dma_start(wr[:, :, :], a["moe_router"][0].rearrange("(k p) e -> p k e", p=P)).then_inc(router_in, 16)
                for _ in range(4):
                    link.end_phase()
                for _ in range(9 if last_layer else 1):
                    link.end_phase()
            for _ in range(5):
                link.end_phase()
            ended.append(link.phases)

        assert len(set(ended)) == 1, ended


_NAMES = ["x", "c", "ctx", "c_ctx", "w_mod", "b_mod", "norm_mix_g", "norm_ffn_g", "w_in", "dn_conv_w", "dn_a_log",
          "dn_dt_bias", "dn_norm_g", "hy_conv_w", "hy_w1", "hy_b1", "hy_freq1", "hy_w2", "hy_b2", "hy_freq2", "hy_w3",
          "hy_b3", "hy_skip", "sw_sink", "w_out", "ffn_w_gate", "ffn_w_up", "ffn_w_down", "moe_router", "moe_w_gate",
          "moe_w_up", "moe_w_down", "final_norm_g"]


def kernel(**inputs):
    import concourse.bacc as bacc
    from concourse.bass_utils import run_bass_kernel_spmd

    nc = bacc.Bacc("TRN2", target_bir_lowering=False, num_devices=1)
    arrays, aps = {}, {}
    k_con, k_hy = shape_constants()
    tensors = {n: np.ascontiguousarray(inputs[n]) for n in _NAMES}
    tensors["k_con"], tensors["k_hy"] = k_con, k_hy
    for name, t in tensors.items():
        arrays[f"in_{name}"] = t
        aps[name] = nc.dram_tensor(f"in_{name}", t.shape, mybir.dt.from_np(t.dtype), kind="ExternalInput").ap()
    out = nc.dram_tensor("out", (1, SEQ, D_MODEL), F32, kind="ExternalOutput").ap()
    build(nc, aps, out)
    r = run_bass_kernel_spmd(nc, [arrays], core_ids=[0])
    return r.results[0]["out"]
```

```python
from contextlib import ExitStack

import numpy as np

import concourse.bass as bass
from concourse import mybir

P = 128
ALU = mybir.AluOpType
ACT = mybir.ActivationFunctionType
F32 = mybir.dt.float32
U32 = mybir.dt.uint32
X_AXIS = mybir.AxisListType.X

D_MODEL = 1024
SEQ = 256
N_TOK = 2 * SEQ
N_LAYERS = 2
HEAD = 64
DN_HEADS = 6
SW_HEADS = 6
HY_CH = 256
FFN_DENSE = 2816
N_EXPERTS = 8
FFN_EXPERT = 3584
RMS_EPS = 1e-6
TINY = 1e-30
ROUND = 1.5 * 2.0 ** 23
TWO_PI = (6.28125, 1.9350051879882812e-3, 3.0199159795074593e-7)
PI_BELOW = 3.1415925
GRID_W = 64
SW_WINDOW = 128

KT = D_MODEL // P
TT = N_TOK // P
N_MOD_TILES = 6 * KT
PAIRS = DN_HEADS // 2
DIRS = 2
PROBS = DIRS * DN_HEADS
DN_TILES = 3 * PAIRS
HY_TILES = 3 * HY_CH // P
SW_TILES = SW_HEADS // 2
CHUNK = P
LEVELS = 7

C_DN, C_Z, C_A = 0, 1152, 1536
C_HY, C_Q, C_K, C_V = 1560, 2328, 2712, 2840
ABV = 24 + 2 * HEAD

SLOT = 2048
RING = 7
MOD_SLOTS = N_MOD_TILES // 2
IN_SLOTS = 12
OUT_SLOTS = KT // 2
ROUND_F = 2 * P
DENSE_ROUNDS = FFN_DENSE // ROUND_F
CAP = 128
EXTRA = 3
PASSES = N_EXPERTS + EXTRA
QUAD = 32
NARROW = 64
MOE_F = 4 * P
MOE_ROUNDS = FFN_EXPERT // MOE_F

(K_ID, K_ONE, K_BLK, K_INC, K_LVL, K_COS, K_SIN, K_ROT, K_BAND, K_IOTA, K_SUM, K_END) = np.cumsum(
    [0, P, P, P, 2 * P, 2 * LEVELS * P, SEQ, SEQ, P, 2 * N_TOK, P, 2]).tolist()
(H_C, H_S, H_CT, H_ST, H_WIN, H_FEAT, H_END) = np.cumsum(
    [0, 2 * SEQ, 2 * SEQ, 2 * SEQ, 2 * SEQ, 2 * 2 * HY_CH, SEQ]).tolist()

(V_GMIX, V_GFFN, V_BMOD, V_DNC, V_HYC, V_DNG, V_FR1, V_B1, V_FR2, V_B2, V_END) = np.cumsum(
    [0, KT, KT, N_MOD_TILES, 3 * DN_TILES, 3 * HY_TILES, 1, 1, 1, 1, 1]).tolist()


def shape_constants():
    t = np.arange(P)
    k = np.zeros((P, K_END), np.float32)
    k[:, K_ID:K_ID + P] = np.eye(P)
    k[:, K_ONE:K_ONE + P] = 1.0
    k[:, K_BLK:K_BLK + P] = (t[:, None] // HEAD) == (t[None] // HEAD)
    k[:, K_INC:K_INC + P] = t[None] >= t[:, None]
    k[:, K_INC + P:K_INC + 2 * P] = t[None] <= t[:, None]
    for lv in range(LEVELS):
        b = 1 << lv
        same = (t[:, None] // (2 * b)) == (t[None] // (2 * b))
        fwd = same & (t[:, None] // b % 2 == 0) & (t[None] // b % 2 == 1)
        k[:, K_LVL + lv * P:K_LVL + (lv + 1) * P] = fwd
        k[:, K_LVL + (LEVELS + lv) * P:K_LVL + (LEVELS + lv + 1) * P] = fwd.T
    half, n = HEAD // 2, HEAD // 4
    inv = np.power(np.float32(10000.0), -np.arange(n, dtype=np.float32) / np.float32(n)).astype(np.float32)
    pos = np.arange(SEQ)
    for ch in range(P):
        c = ch % HEAD
        where = (pos // GRID_W if c < half else pos % GRID_W).astype(np.float32)
        ang = where * inv[c % n]
        k[ch, K_COS:K_COS + SEQ] = np.cos(ang)
        k[ch, K_SIN:K_SIN + SEQ] = np.sin(ang)
        first = c % half < n
        k[ch + n if first else ch - n, K_ROT + ch] = -1.0 if first else 1.0
    for qt in range(2):
        q = qt * P + t
        far = np.abs(q[:, None] - pos[None]) > SW_WINDOW
        k[:, K_BAND + qt * N_TOK + SEQ:K_BAND + (qt + 1) * N_TOK] = np.where(far, -1e30, 0.0)
    k[:, K_IOTA:K_IOTA + P] = np.arange(P)
    for r in range(2):
        k[r::32, K_SUM + r] = 1.0

    h = np.zeros((P, H_END), np.float32)
    m = np.arange(SEQ)
    ang = np.pi * np.mod(m[:, None] * (2 * m[None] + 1), 4 * SEQ) / (2 * SEQ)
    for base, tab in ((H_C, np.cos(ang)), (H_S, np.sin(ang)), (H_CT, np.cos(ang).T / SEQ),
                      (H_ST, -np.sin(ang).T / SEQ)):
        h[:, base:base + 2 * SEQ] = tab.reshape(2, P, SEQ).transpose(1, 0, 2).reshape(P, 2 * SEQ)
    tl = np.linspace(0.0, 1.0, SEQ, dtype=np.float32)
    omega = (np.float32(2.0 * np.pi) * m.astype(np.float32) / np.float32(SEQ)).astype(np.float32)
    bands = np.linspace(1e-4, 15, 16, dtype=np.float32)
    fa = (omega[:, None] * bands[None]).astype(np.float32)
    feats = np.concatenate([tl[:, None], np.cos(fa), -np.sin(fa)], axis=1).astype(np.float32)
    h[0:feats.shape[1], H_FEAT:H_FEAT + SEQ] = feats.T
    deltas = np.abs(np.linspace(np.log(1e-2) / 1.5, np.log(1e-2) / 0.3, HY_CH, dtype=np.float32))
    win = np.exp(-tl[:, None] * deltas[None]).astype(np.float32)
    both = np.stack([win, win], axis=1)
    both[0, 1] = 0.0
    h[:, H_WIN:H_WIN + 4 * HY_CH] = both.reshape(2, P, 2 * HY_CH).transpose(1, 0, 2).reshape(P, -1)
    return k, h


def build(nc, a, out):
    with ExitStack() as ctx:
        def sb(name, shape, dt=F32):
            return ctx.enter_context(nc.sbuf_tensor(name, shape, dt))

        def sem(name):
            return ctx.enter_context(nc.semaphore(name))

        ps = [ctx.enter_context(nc.psum_tensor(f"bank{i}", [P, 512], F32)) for i in range(8)]

        ring = sb("ring", [P, RING, SLOT])
        con = sb("con", [P, K_END])
        xT = sb("xT", [P, KT, N_TOK])
        hT = sb("hT", [P, KT, N_TOK])
        vrow = sb("vrow", [P, P])
        vcol = sb("vcol", [P, P])
        vrow2 = sb("vrow2", [P, P])
        vcol2 = sb("vcol2", [P, 3 * KT])
        cs = sb("cs", [P, KT, QUAD])
        mod = sb("mod", [P, N_MOD_TILES, 2])
        amul = sb("amul", [P, 2, KT, 2])
        rows = sb("rows", [P, 2 * PROBS + SW_HEADS])
        qkv = sb("qkv", [P, DN_TILES, N_TOK])
        zz = sb("zz", [P, PAIRS, N_TOK])
        abv = sb("abv", [P, TT, ABV])
        misc = sb("misc", [P, 2])
        WORK = 18500
        work = sb("work", [P, WORK])

        def carve(at, *shape):
            n = int(np.prod(shape))
            assert at + n <= WORK, (at, shape)
            v = work[:, at:at + n]
            if len(shape) == 2:
                v = v.rearrange("p (a b) -> p a b", a=shape[0])
            elif len(shape) == 3:
                v = v.rearrange("p (a b c) -> p a b c", a=shape[0], b=shape[1])
            return v, at + n

        SEG = lambda lo: (N_TOK - lo) // SEQ
        hy, at = carve(0, HY_TILES, N_TOK)
        qT, at = carve(at, SW_TILES, N_TOK)
        kT, after_proj = carve(at, N_TOK)
        hc, at = carve(after_proj, H_END)
        w3, at = carve(at, 4 * HY_CH)
        w12, at = carve(at, P)
        kre, at = carve(at, 2, 2 * HY_CH)
        kim, at = carve(at, 2, 2 * HY_CH)
        hy_scratch = at
        kern, at = carve(at, 2, 2, 2 * HY_CH)
        hh1, at = carve(at, SEQ)
        hh2, at = carve(at, SEQ)
        htmp, at = carve(at, SEQ)
        htmp2, at = carve(at, SEQ)
        hnorm, at = carve(at, 2 * HY_CH)
        hskip, at = carve(at, 2 * HY_CH)
        def modr(b):
            flat = (qkv if b < DN_TILES else zz)[:, :, :].rearrange("p a b -> p (a b)")
            b = b if b < DN_TILES else b - DN_TILES
            return flat[:, b * 4 * P:(b + 1) * 4 * P]

        ut, at = carve(hy_scratch, 2, N_TOK)
        x1t, at = carve(at, 2, N_TOK)
        pre, at = carve(at, 2, N_TOK)
        pim, at = carve(at, 2, N_TOK)
        ptmp, at = carve(at, N_TOK)
        SC_BUFS, SC_BANKS = 3, (0, 1, 6)
        sc, at = carve(after_proj, SC_BUFS, N_TOK)
        pT, at = carve(at, 2, N_TOK)
        rot, at = carve(at, 4, SEQ)
        st, at = carve(at, SC_BUFS, 8)
        sqb, at = carve(at, 2, N_TOK)
        unit, at = carve(at, 2, N_TOK)
        ktok, at = carve(0, TT, DN_HEADS * HEAD)
        vtok, at = carve(at, TT, DN_HEADS * HEAD)
        gt, at = carve(at, TT, PROBS)
        bt, at = carve(at, TT, PROBS)
        gc, at = carve(at, TT, PROBS)
        eg, at = carve(at, TT, PROBS)
        gtmp, at = carve(at, TT, PROBS)
        gtmp2, at = carve(at, TT, PROBS)
        kds, at = carve(at, PROBS)
        Amat, at = carve(at, PROBS, CHUNK)
        Xm, at = carve(at, PROBS, CHUNK)
        XT, at = carve(at, PROBS, CHUNK)
        Bm, at = carve(at, PROBS, CHUNK)
        QK, at = carve(at, PROBS, CHUNK)
        egb, at = carve(at, 2 * PAIRS, CHUNK)
        kb, at = carve(at, 2 * PAIRS, CHUNK)
        state, at = carve(at, 2 * PAIRS, P)
        kd, at = carve(at, 2 * PAIRS, P)
        rhs, at = carve(at, PROBS, HEAD)
        Am, at = carve(at, PROBS, CHUNK)
        qd, at = carve(at, 2 * PAIRS, CHUNK)
        vnew = kb.rearrange("p a b -> p (a b)").rearrange("p (q d) -> p q d", q=PROBS)
        sil, at = carve(0, 2, N_TOK)
        act, at = carve(at, 2, 2, N_TOK)
        htok, at = carve(0, 2, D_MODEL)
        sel, at = carve(at, 2, PASSES + 1, P)
        selT, at = carve(at, PASSES + 1, SEQ)
        xg, at = carve(at, KT, P)
        msil, at = carve(at, MOE_F)
        matok, at = carve(at, MOE_F)
        aT, at = carve(at, 2, 4, P)
        ytok, at = carve(at, D_MODEL)
        selnow, at = carve(at, SEQ)
        gplace, at = carve(at, PASSES + 1)
        gpass, at = carve(at, 1)
        lg, at = carve(at, 2, 8)
        top, at = carve(at, 2, 8)
        tix, at = carve(at, 2, 8)
        tmp8, at = carve(at, 2, 8)
        mx, at = carve(at, 2, PASSES + 1)
        gx, at = carve(at, 2, PASSES + 1)
        rx, at = carve(at, 2, PASSES + 1)
        over8, at = carve(at, 8)
        incl8, at = carve(at, 8)
        hot8, at = carve(at, EXTRA, 8)
        prod8, at = carve(at, 8, EXTRA, 8)
        metaf, at = carve(at, 1 + EXTRA + PASSES)
        rxn, at = carve(at, 2, PASSES)
        wr, at = carve(at, KT, N_EXPERTS)
        meta = sb("meta", [P, 1 + EXTRA + PASSES], mybir.dt.int32)
        topi = sb("topi", [P, 2, 8], U32)
        rms_r, at = carve(0, N_TOK)
        rms_s, at = carve(at, N_TOK)

        ident = con[:, K_ID:K_ID + P]
        ones = con[:, K_ONE:K_ONE + P]
        blk = con[:, K_BLK:K_BLK + P]

        eps_col, one_col = misc[:, 0:1], misc[:, 1:2]

        def XT_flat(i):
            return Xm.rearrange("p a b -> p (a b)")[:, i * N_TOK:(i + 1) * N_TOK] if i < 3 else \
                XT.rearrange("p a b -> p (a b)")[:, (i - 3) * N_TOK:(i - 2) * N_TOK]

        def row_loads(layer):
            def rows128(at, v):
                v = v.rearrange("(r p) -> r p", p=P)
                return vrow[at:at + v.shape[0], :], v
            flat = lambda v: v.rearrange("a b -> (a b)")
            every = lambda v: v.partition_broadcast(P)
            return [
                rows128(V_GMIX, a["norm_mix_g"][layer]), rows128(V_GFFN, a["norm_ffn_g"][layer]),
                rows128(V_BMOD, a["b_mod"][layer]), rows128(V_DNC, flat(a["dn_conv_w"][layer])),
                rows128(V_HYC, flat(a["hy_conv_w"][layer])),
                (vrow[V_DNG:V_DNG + 1, 0:HEAD], a["dn_norm_g"][layer:layer + 1, :]),
                (vrow[V_DNG:V_DNG + 1, HEAD:P], a["dn_norm_g"][layer:layer + 1, :]),
                (vrow[V_FR1:V_FR1 + 1, 0:HEAD], a["hy_freq1"][layer:layer + 1, :]),
                (vrow[V_B1:V_B1 + 1, 0:HEAD], a["hy_b1"][layer:layer + 1, :]),
                (vrow[V_FR2:V_FR2 + 1, 0:HEAD], a["hy_freq2"][layer:layer + 1, :]),
                (vrow[V_B2:V_B2 + 1, 0:HEAD], a["hy_b2"][layer:layer + 1, :]),
                (rows[:, 0:PROBS], every(flat(a["dn_a_log"][layer]))),
                (rows[:, PROBS:2 * PROBS], every(flat(a["dn_dt_bias"][layer]))),
                (rows[:, 2 * PROBS:2 * PROBS + SW_HEADS], every(a["sw_sink"][layer])),
                (hc[:, :], a["k_hy"]), (w12[0:33, 0:HEAD], a["hy_w1"][layer]), (w12[0:HEAD, HEAD:P], a["hy_w2"][layer]),
                (w3[0:HEAD, :], a["hy_w3"][layer]), (w3[HEAD:HEAD + 1, :], a["hy_b3"][layer:layer + 1, :]),
                (hskip[:, :], every(flat(a["hy_skip"][layer]))),
            ]

        ROW_LOADS = 20
        HY_PHASES = 8
        FILTER_STAGES, FILTER_FIRST = 15, 9
        phase = sem("phase")
        dve_chain, act_chain, pool_chain = sem("dve_chain"), sem("act_chain"), sem("pool_chain")
        slot_full = [sem(f"slot_full{i}") for i in range(RING)]
        rows_first = sem("rows_first")
        setup_in, rows_in, router_in = sem("setup_in"), sem("rows_in"), sem("router_in")
        mod_copied = sem("mod_copied")
        mod_ready = sem("mod_ready")
        sq_act, sq_dve = sem("sq_act"), sem("sq_dve")
        sum_sq, root_ready = sem("sum_sq"), sem("root_ready")
        normed = sem("normed")
        h_act, h_pool = sem("h_act"), sem("h_pool")
        POOL_TILES = (2, 5)
        ACT_TILES = [k for k in range(KT) if k not in POOL_TILES]
        proj_ready = sem("proj_ready")
        conv_done = sem("conv_done")
        copy_done = sem("copy_done")
        freq_ready = sem("freq_ready")
        sq_ready, sum_ready = sem("sq_ready"), sem("sum_ready")
        unit_ready, unit_used = sem("unit_ready"), sem("unit_used")
        ln_ready = sem("ln_ready")
        score_ready, score_read = sem("score_ready"), sem("score_read")
        max_ready, exp_ready, prob_ready = sem("max_ready"), sem("exp_ready"), sem("prob_ready")
        turn_ready, turn_read = sem("turn_ready"), sem("turn_read")
        pv_ready, pv_read = sem("pv_ready"), sem("pv_read")
        am_ready, b_ready, b_copied = sem("am_ready"), sem("b_ready"), sem("b_copied")
        p_ready, x_done = sem("p_ready"), sem("x_done")
        r_ready, diff_ready = sem("r_ready"), sem("diff_ready")
        egb_ready, decay_ready = sem("egb_ready"), sem("decay_ready")
        kds_ready, kd_ready = sem("kds_ready"), sem("kd_ready")
        beta_ready, kb_ready = sem("beta_ready"), sem("kb_ready")
        kq_ready, qk_read, qk_ready = sem("kq_ready"), sem("qk_read"), sem("qk_ready")
        kk_ready, a_ready = sem("kk_ready"), sem("a_ready")
        x0_ready, xt_turned, xm_ready = sem("x0_ready"), sem("xt_turned"), sem("xm_ready")
        qd_ready, ks_ready, rhs_ready = sem("qd_ready"), sem("ks_ready"), sem("rhs_ready")
        v_ready, vnew_ready = sem("v_ready"), sem("vnew_ready")
        out_ready, state_ready = sem("out_ready"), sem("state_ready")
        mix_ready, mix_added = sem("mix_ready"), sem("mix_added")
        gu_ready, sil_ready, act_ready = sem("gu_ready"), sem("sil_ready"), sem("act_ready")
        down_ready, down_added = sem("down_ready"), sem("down_added")
        slot_used = sem("slot_used")
        xg_ready, matok_turned = sem("xg_ready"), sem("matok_turned")
        aT_ready, y_copied = sem("aT_ready"), sem("y_copied")
        gathered, scattered = sem("gathered"), sem("scattered")
        meta_ready, gpass_set = sem("meta_ready"), sem("gpass_set")
        rows_out, out_done = sem("rows_out"), sem("out_done")

        w_in_v = a["w_in"].rearrange("l (k p) n -> l p k n", p=P)
        w_out_v = a["w_out"]
        w_mod_v = a["w_mod"].rearrange("l (k p) n -> l p k n", p=P)
        NS = {"mod": MOD_SLOTS, "in": IN_SLOTS, "out": OUT_SLOTS}

        def wide(s):
            return ring[:, s % RING, :].rearrange("p (k n) -> p k n", k=KT)

        def deep(s):
            return ring[:, s % RING, :].rearrange("p (k n) -> p k n", k=2)

        in_tiles = ([("dn", i) for i in range(DN_TILES)] + [("z", i) for i in range(PAIRS)]
                    + [("hy", i) for i in range(HY_TILES)] + [("q", i) for i in range(SW_TILES)] + [("k", 0)])

        def halves(dst, src):
            return [(dst[:, 0:KT // 2], src[:, 0:KT // 2]), (dst[:, KT // 2:KT], src[:, KT // 2:KT])]

        def in_slot_loads(layer, j, s):
            w = w_in_v[layer]
            if j == 0:
                return [(wide(s)[:, :, 0:24], w[:, :, C_A:C_A + 24]),
                        (wide(s)[:, :, 24:ABV], w[:, :, C_V:C_V + P])]
            pair = in_tiles[2 * (j - 1):2 * j]
            if pair[0][0] in ("q", "k") or pair[1][0] in ("q", "k"):
                loads = []
                for half, (kind, i) in enumerate(pair):
                    if kind == "q":
                        for hd in range(2):
                            c = C_Q + (i + 3 * hd) * HEAD
                            loads.append((wide(s)[:, :, half * P + hd * HEAD:half * P + (hd + 1) * HEAD],
                                          w[:, :, c:c + HEAD]))
                    else:
                        for hd in range(2):
                            loads.append((wide(s)[:, :, half * P + hd * HEAD:half * P + (hd + 1) * HEAD],
                                          w[:, :, C_K + hd * HEAD:C_K + (hd + 1) * HEAD]))
                return loads
            base = {"dn": C_DN, "z": C_Z, "hy": C_HY}[pair[0][0]] + pair[0][1] * P
            if pair[0][0] == pair[1][0]:
                return halves(wide(s), w[:, :, base:base + 2 * P])
            base2 = {"dn": C_DN, "z": C_Z, "hy": C_HY}[pair[1][0]] + pair[1][1] * P
            return [(wide(s)[:, :, 0:P], w[:, :, base:base + P]), (wide(s)[:, :, P:2 * P], w[:, :, base2:base2 + P])]

        def out_slot_loads(layer, j, s):
            cols = slice(j * 2 * P, (j + 1) * 2 * P)
            w = w_out_v[layer]
            plain = w[0:5 * P, cols].rearrange("(k p) n -> p k n", p=P)
            sw = w[5 * P:8 * P, cols].rearrange("(h i d) n -> h d i n", h=2, i=SW_TILES)
            return [(wide(s)[:, 0:5, :], plain), (wide(s)[0:HEAD, 5:8, :], sw[0]), (wide(s)[HEAD:P, 5:8, :], sw[1])]

        def gu_loads(wm, r, s):
            return halves(wide(s), wm[:, r * ROUND_F:(r + 1) * ROUND_F].rearrange("(k p) n -> p k n", p=P))

        def dn_loads(wm, r, s):
            src = wm[r * ROUND_F:(r + 1) * ROUND_F, :].rearrange("(k p) n -> p k n", p=P)
            return [(deep(s)[:, 0:1], src[:, 0:1]), (deep(s)[:, 1:2], src[:, 1:2])]

        def half_k(s):
            return ring[:, s % RING, :].rearrange("p (k n) -> p k n", k=4)

        def round_order(n):
            yield "g", 0
            yield "u", 0
            for r in range(1, n):
                yield "g", r
                yield "u", r
                yield "d", r - 1
            yield "d", n - 1

        plan = []
        for layer in range(N_LAYERS):
            for j in range(MOD_SLOTS):
                plan.append((lambda s, l=layer, j=j: halves(wide(s), w_mod_v[l][:, :, j * 2 * P:(j + 1) * 2 * P]),
                             (mod_ready, layer * MOD_SLOTS + j + 1)))
            for j in range(IN_SLOTS):
                plan.append((lambda s, l=layer, j=j: in_slot_loads(l, j, s),
                             (proj_ready, layer * 2 * IN_SLOTS + 2 * (j + 1))))
            for j in range(OUT_SLOTS):
                plan.append((lambda s, l=layer, j=j: out_slot_loads(l, j, s),
                             (mix_ready, layer * KT + 2 * (j + 1))))
            if layer == 0:
                for kind, r in round_order(DENSE_ROUNDS):
                    if kind == "d":
                        plan.append((lambda s, r=r: dn_loads(a["ffn_w_down"][0], r, s), (down_ready, KT * (r + 1))))
                    else:
                        w = a["ffn_w_gate" if kind == "g" else "ffn_w_up"][0]
                        plan.append((lambda s, r=r, w=w: gu_loads(w, r, s), (gu_ready, 2 * (r + 1))))
        S_MOE = len(plan)
        MOE_ORDER = [(kind, r, h) for kind, r in round_order(MOE_ROUNDS) for h in range(2)]
        assert len(MOE_ORDER) % RING == 0

        counts, landed = [0] * RING, []
        for n, (loads, _) in enumerate(plan):
            counts[n % RING] += 16 * len(loads(n))
            landed.append(counts[n % RING])
        g_done, u_done, d_done = ([j + 1 for j, (kind, r, h) in enumerate(MOE_ORDER) if kind == x and h]
                                  for x in "gud")
        MOE_USE = 32
        MOE_INC = MOE_USE * len(MOE_ORDER) // RING

        def moe_landed(j):
            n = S_MOE + j
            return counts[n % RING] + MOE_USE * (j // RING + 1)

        block = ctx.enter_context(nc.Block())

        @block.sync
        def _(sp):
            def load(loads, s):
                for dst, src in loads:
                    sp.dma_start(dst, src).then_inc(slot_full[s % RING], 16)
            for s, (loads, _) in enumerate(plan):
                if s == 0:
                    sp.dma_start(con[:, :], a["k_con"]).then_inc(setup_in, 16)
                    sp.dma_start(hT[:, 0:4, :].rearrange("p (t k) n -> p t (k n)", t=2),
                                 a["ctx"][0].rearrange("(t p) n -> p t n", p=P)).then_inc(setup_in, 16)
                    sp.dma_start(hT[:, 4:8, :].rearrange("p (t k) n -> p t (k n)", t=2),
                                 a["x"][0].rearrange("(t p) n -> p t n", p=P)).then_inc(setup_in, 16)
                    sp.dma_start(vrow2[0:KT, :], a["c_ctx"].rearrange("(k p) -> k p", p=P)).then_inc(setup_in, 16)
                    sp.dma_start(vrow2[KT:2 * KT, :], a["c"][0].rearrange("(k p) -> k p", p=P)).then_inc(setup_in, 16)
                    sp.dma_start(vrow2[2 * KT:3 * KT, :],
                                 a["final_norm_g"].rearrange("(k p) -> k p", p=P)).then_inc(setup_in, 16)
                if s >= RING:
                    used, count = plan[s - RING][1]
                    sp.wait_ge(used, count)
                load(loads(s), s)
                if s == RING - 1:
                    sp.wait_ge(pool_chain, 2)
                    for dst, src in row_loads(0):
                        sp.dma_start(dst, src).then_inc(rows_first, 16)

            def moe_load(e, j):
                s = S_MOE + j
                kind, r, h = MOE_ORDER[j]
                if kind == "d":
                    f0 = r * MOE_F + h * 2 * P
                    src = a["moe_w_down"][0][bass.ds(e, 1), f0:f0 + 2 * P, :].rearrange("e (k p) n -> p (e k) n", p=P)
                    load([(deep(s)[:, i:i + 1], src[:, i:i + 1]) for i in range(2)], s)
                else:
                    wm = a["moe_w_gate" if kind == "g" else "moe_w_up"][0]
                    src = wm[bass.ds(e, 1), h * 4 * P:(h + 1) * 4 * P, r * MOE_F:(r + 1) * MOE_F].rearrange(
                        "e (k p) n -> p (e k) n", p=P)
                    load([(half_k(s)[:, 2 * i:2 * i + 2], src[:, 2 * i:2 * i + 2]) for i in range(2)], s)

            def moe_pass(pi, e):
                for j in range(len(MOE_ORDER)):
                    sp.wait_ge(slot_used, pi * len(MOE_ORDER) + (j - RING + 1))
                    moe_load(e, j)

            for j in range(len(MOE_ORDER)):
                if j < RING:
                    sp.wait_ge(*plan[S_MOE + j - RING][1])
                else:
                    sp.wait_ge(slot_used, j - RING + 1)
                moe_load(0, j)
            with sp.Fori(1, N_EXPERTS) as e:
                moe_pass(e, e)
            sp.wait_ge(meta_ready, 1)
            n_over = sp.value_load(meta[0:1, 0:1], min_val=0, max_val=EXTRA)
            with sp.Fori(0, EXTRA) as p:
                with sp.If(p < n_over):
                    e = sp.value_load(meta[0:1, bass.ds(p + 1, 1)], min_val=0, max_val=N_EXPERTS - 1)
                    moe_pass(p + N_EXPERTS, e)
            sp.wait_ge(rows_out, 2)
            sp.dma_start(out[0].rearrange("(t p) n -> p t n", p=P),
                         hT[:, 0:4, :].rearrange("p (t k) n -> p t (k n)", t=2)).then_inc(out_done, 16)
            sp.wait_ge(out_done, 16)


        class Link:

            def __init__(self, eng, chain):
                self.eng, self.chain, self.n, self.phases, self.told = eng, chain, 0, 0, {}

            def __call__(self, ins):
                self.n += 1
                ins.then_inc(self.chain, 1)
                self.eng.wait_ge(self.chain, self.n)

            def later(self, ins):
                self.n += 1
                ins.then_inc(self.chain, 1)
                return self.n

            def end_phase(self):
                self.phases += 1
                self.eng.drain().then_inc(phase, 1)
                self.eng.wait_ge(phase, 4 * self.phases)

        STEP_TILES = [(0, 1), (1, 0), (2, 3), (3, 2)]
        GROUPS = [(g, g // 2, slice(3 * g, 3 * g + 3)) for g in range(4)]

        def col(q):
            return q // DN_HEADS * DN_HEADS + q % PAIRS * 2 + q // PAIRS % 2

        def cols3(g):
            return slice(col(3 * g), col(3 * g) + 2 * PAIRS - 1, 2)

        ended = []

        def three(b):
            return ps[b][:, 0:3 * P].rearrange("p (a b) -> p a b", a=3)

        def six(b):
            return ps[b][:, 0:DN_HEADS * HEAD].rearrange("p (a b) -> p a b", a=DN_HEADS)

        def seg(ap, lo):
            return ap[:, lo:N_TOK].rearrange("p (s t) -> p s t", t=SEQ)

        def mask(col, n=3):
            return con[:, col:col + P].unsqueeze(1).to_broadcast([P, n, P])

        def over(ap, n):
            return ap.unsqueeze(2).to_broadcast([P, ap.shape[1], n])

        def jobs(layer):
            lat = [(1, i, h, t) for i in range(SW_TILES) for h in range(2) for t in range(2)]
            return lat if layer == N_LAYERS - 1 else lat + [(0,) + j[1:] for j in lat]

        SIL0, A0, ADD0 = 2 * DENSE_ROUNDS, 2 * DENSE_ROUNDS, KT * DENSE_ROUNDS
        PRIME = 2

        ATT_BASE = [0, len(jobs(0))]

        def read_before(n):
            kinds = ["abv"] * 2 + [k for k, _ in in_tiles]
            mine = ("z", "q", "k")
            per = [sum(k not in mine for k in kinds), sum(k in mine for k in kinds)]
            who = kinds[n] in mine
            return (copy_done if who else conv_done), per[who], sum((k in mine) == who for k in kinds[:n + 1])

        def split(lv):
            return (2 << lv) <= CHUNK // 2

        def halves_of(lv):
            if not split(lv):
                return [slice(0, CHUNK)]
            return [slice(0, CHUNK // 2), slice(CHUNK // 2, CHUNK)]

        def blocks(b, r_):
            w = r_.stop - r_.start
            return ps[b][r_, 0:3 * w].rearrange("p (a b) -> p a b", a=3)

        def lvl_index(layer, i, lv, g):
            return ((layer * 4 + i) * (LEVELS - 1) + lv - 1) * 4 + g

        @block.tensor
        def _(pe):
            link = Link(pe, None)
            T = nc.tensor
            s = 0

            def full(s):
                pe.wait_ge(slot_full[s % RING], landed[s])

            def rms(lo, m):
                for i in range(KT):
                    k = i // 2 + i % 2 * 4
                    pe.wait_ge(sq_dve if i % 2 else sq_act, 4 * m + i // 2 + 1)
                    last = T.matmul(ps[0][:, lo:N_TOK], ones, hT[:, k, lo:N_TOK], start=(i == 0), stop=(i == KT - 1))
                last.then_inc(sum_sq, 1)

            def modulated(m, k):
                if k in POOL_TILES:
                    pe.wait_ge(h_pool, len(POOL_TILES) * m + POOL_TILES.index(k) + 1)
                else:
                    pe.wait_ge(h_act, len(ACT_TILES) * m + ACT_TILES.index(k) + 1)

            pe.wait_ge(setup_in, 16 * 6)
            tok = hT[:, :, :].rearrange("p (t k) n -> p t (k n)", t=TT)
            for k in range(KT):
                for t in range(TT):
                    T.transpose(ps[k][:, t * P:(t + 1) * P], tok[:, t, k * P:(k + 1) * P], ident)
            link.end_phase()
            link.end_phase()
            T.transpose(ps[0][:, 0:3 * KT], vrow2[0:3 * KT, :], ident[0:3 * KT, 0:3 * KT])
            link.end_phase()
            link.end_phase()

            def fourier(dst, tab, src, lo=0):
                for f in range(2):
                    for t in range(2):
                        T.matmul(ps[dst + f][:, lo:N_TOK], hc[:, tab + t * SEQ + f * P:tab + t * SEQ + (f + 1) * P],
                                 src(t), start=(t == 0), stop=(t == 1))

            def filter_stage(layer, n):
                if n == 0:
                    pe.wait_ge(rows_in if layer else rows_first, ROW_LOADS * 16)
                    T.transpose(ps[1][:, 0:V_END], vrow[0:V_END, :], ident[0:V_END, 0:V_END])
                elif n == 2:
                    T.matmul(ps[0][0:HEAD, 0:SEQ], w12[0:33, 0:HEAD], hc[0:33, H_FEAT:H_FEAT + SEQ], start=True, stop=True)
                elif n == 5:
                    T.matmul(ps[0][0:HEAD, 0:SEQ], w12[0:HEAD, HEAD:P], hh1[0:HEAD, :], start=True, stop=True)
                elif n == 8:
                    for mt in range(2):
                        for d in range(2):
                            T.matmul(ps[2 * mt + d][:, :], hh2[0:HEAD + 1, mt * P:(mt + 1) * P],
                                     w3[0:HEAD + 1, d * 2 * HY_CH:(d + 1) * 2 * HY_CH], start=True, stop=True)
                elif n == 11:
                    for m, sq in enumerate([kre[:, 0], kre[:, 1], kim[:, 0], kim[:, 1]]):
                        T.matmul(ps[4][:, :], ones, sq, start=(m == 0), stop=(m == 3))
                elif n == 13:
                    fourier(0, H_C, lambda t: kre[:, t])
                    fourier(2, H_S, lambda t: kern[:, t, 1])
                link.end_phase()

            def hyena(layer, lo):
                for tt in range(2):
                    for st_ in range(lo // SEQ, 2):
                        for i in range(2):
                            tok0 = st_ * SEQ + tt * P
                            at = slice(st_ * SEQ + i * P, st_ * SEQ + (i + 1) * P)
                            T.transpose(ps[tt][:, at], hy[:, i, tok0:tok0 + P], ident)
                            T.transpose(ps[2 + tt][:, at], hy[:, 2 + i, tok0:tok0 + P], ident)
                link.end_phase()
                link.end_phase()
                for order in range(2):
                    for f in range(2):
                        for dst, tab in ((0, H_C), (2, H_S)):
                            for t in range(2):
                                c = tab + t * SEQ + f * P
                                last = T.matmul(ps[dst + f][:, lo:N_TOK], hc[:, c:c + P], ut[:, t, lo:N_TOK],
                                                start=(t == 0), stop=(t == 1))
                        last.then_inc(freq_ready, 1)
                    link.end_phase()
                    for t in range(2):
                        if order == 0:
                            for n, (tab, src) in enumerate([(H_CT, pre), (H_ST, pim)]):
                                for f in range(2):
                                    c = tab + f * SEQ + t * P
                                    T.matmul(ps[t][:, lo:N_TOK], hc[:, c:c + P], src[:, f, lo:N_TOK],
                                             start=(n + f == 0), stop=(n + f == 2))
                        else:
                            for st_ in range(lo // SEQ, 2):
                                for n, (tab, src) in enumerate([(H_CT, pre), (H_ST, pim)]):
                                    for f in range(2):
                                        c = st_ * SEQ + t * P
                                        T.matmul(ps[t][:, st_ * SEQ:(st_ + 1) * SEQ], src[:, f, c:c + P],
                                                 hc[:, tab + f * SEQ:tab + (f + 1) * SEQ],
                                                 start=(n + f == 0), stop=(n + f == 2))
                    link.end_phase()
                    link.end_phase()

            def attention(layer):
                for i in range(4):
                    src = qT[:, i, SEQ:N_TOK] if i < SW_TILES else kT[:, SEQ:N_TOK]
                    T.matmul(ps[i // 2][:, i % 2 * SEQ:(i % 2 + 1) * SEQ], con[:, K_ROT:K_ROT + P], src,
                             start=True, stop=True)
                link.end_phase()
                link.end_phase()
                base, todo = ATT_BASE[layer], jobs(layer)

                def scores(n):
                    lat, i, half, qt = todo[n]
                    rows_ = slice(half * HEAD, (half + 1) * HEAD)
                    if n >= SC_BUFS:
                        pe.wait_ge(score_read, base + n - SC_BUFS + 1)
                    q0 = lat * SEQ + qt * P
                    keys = N_TOK if lat else SEQ
                    T.matmul(ps[SC_BANKS[n % SC_BUFS]][:, 0:keys], qT[rows_, i, q0:q0 + P], kT[rows_, 0:keys],
                             start=True, stop=True).then_inc(score_ready, 1)

                def turns(n):
                    pe.wait_ge(prob_ready, base + n + 1)
                    if n >= 2:
                        pe.wait_ge(turn_read, base + n - 1)
                    for kt_ in range(4 if todo[n][0] else 2):
                        last = T.transpose(ps[2 + n % 2][:, kt_ * P:(kt_ + 1) * P], sc[:, n % SC_BUFS, kt_ * P:(kt_ + 1) * P],
                                           ident)
                    last.then_inc(turn_ready, 1)

                def values(n):
                    lat, i, half, qt = todo[n]
                    rows_ = slice(half * HEAD, (half + 1) * HEAD)
                    nk = 4 if lat else 2
                    pe.wait_ge(turn_read, base + n + 1)
                    if n >= 2:
                        pe.wait_ge(pv_read, base + n - 1)
                    for kt_ in range(nk):
                        last = T.matmul(ps[4 + n % 2][rows_, 0:P], abv[:, kt_, 24 + half * HEAD:24 + (half + 1) * HEAD],
                                        pT[:, n % 2, kt_ * P:(kt_ + 1) * P], start=(kt_ == 0), stop=(kt_ == nk - 1))
                    last.then_inc(pv_ready, 1)

                def norms(i):
                    m = layer * 2 * PAIRS + i
                    pe.wait_ge(sq_ready, m + 1)
                    if i:
                        pe.wait_ge(ln_ready, m)
                    T.matmul(ps[7][:, :], blk, sqb[:, i % 2, :], start=True, stop=True).then_inc(sum_ready, 1)

                scores(0)
                scores(1)
                for it in range(len(todo) + 1):
                    if it + 2 < len(todo):
                        scores(it + 2)
                    if it < len(todo):
                        turns(it)
                    if it:
                        values(it - 1)
                    if it % 2 == 0 and it // 2 < 2 * PAIRS:
                        norms(it // 2)
                link.end_phase()

            def delta(layer, lo):
                link.end_phase()
                link.end_phase()
                link.end_phase()
                link.end_phase()
                for t in range(TT):
                    for kind in range(2):
                        for i in range(PAIRS):
                            T.transpose(ps[2 * t + kind][:, i * P:(i + 1) * P],
                                        qkv[:, (kind + 1) * PAIRS + i, t * P:(t + 1) * P], ident)
                link.end_phase()
                link.end_phase()
                for t in range(TT):
                    for d in range(DIRS):
                        c = t * PROBS + d * DN_HEADS
                        T.matmul(ps[0][:, c:c + DN_HEADS], con[:, K_INC + d * P:K_INC + (d + 1) * P],
                                 gt[:, t, d * DN_HEADS:(d + 1) * DN_HEADS], start=True, stop=True)
                link.end_phase()
                link.end_phase()
                for i in range(4):
                    want_o = not (layer == N_LAYERS - 1 and i < 2)
                    G0, D0 = (layer * 4 + i) * 4, (layer * 4 + i) * DIRS

                    def rows_of(g, n):
                        h = col(3 * g + n) % DN_HEADS
                        tile = STEP_TILES[i][g // 2]
                        return slice(h % 2 * HEAD, (h % 2 + 1) * HEAD), h // 2, slice(tile * P, (tile + 1) * P)

                    for g, d, qs in GROUPS:
                        for n, q in enumerate(range(3 * g, 3 * g + 3)):
                            tile = STEP_TILES[i][d]
                            last = T.matmul(ps[g][:, n * P:(n + 1) * P], gt[:, tile, col(q):col(q) + 1].to_broadcast([P, P]),
                                            con[:, K_INC + d * P:K_INC + (d + 1) * P], start=True, stop=True)
                        last.then_inc(r_ready, 1)
                    if i:
                        pe.wait_ge(state_ready, D0)
                    for d in range(DIRS):
                        tile = STEP_TILES[i][d]
                        for j in range(PAIRS):
                            for half in range(2):
                                q = d * DN_HEADS + 2 * j + half
                                r_ = slice(half * HEAD, (half + 1) * HEAD)
                                last = T.matmul(ps[4 + d][r_, j * P:(j + 1) * P], bt[:, tile, q:q + 1].to_broadcast([P, HEAD]),
                                                ident, start=True, stop=True)
                        last.then_inc(beta_ready, 1)

                    def kq(g):
                        for n in range(3):
                            r_, j, c_ = rows_of(g, n)
                            last = T.matmul(ps[6 + g % 2][:, n * P:(n + 1) * P], qkv[r_, PAIRS + j, c_], qkv[r_, j, c_],
                                            start=True, stop=True)
                        last.then_inc(kq_ready, 1)

                    def kk(g):
                        for n in range(3):
                            r_, j, c_ = rows_of(g, n)
                            last = T.matmul(ps[4 + g % 2][:, n * P:(n + 1) * P], qkv[r_, PAIRS + j, c_],
                                            kb[r_, g // 2 * PAIRS + j, :], start=True, stop=True)
                        last.then_inc(kk_ready, 1)

                    kq(0)
                    kq(1)
                    pe.wait_ge(kb_ready, D0 + 2)
                    kk(0)
                    kk(1)
                    for g in (2, 3):
                        pe.wait_ge(qk_read, G0 + g - 1)
                        kq(g)
                    for g in (2, 3):
                        pe.wait_ge(a_ready, G0 + g - 1)
                        kk(g)
                    for d in range(DIRS):
                        pe.wait_ge(qk_read, G0 + d + 3)
                        cols = slice(STEP_TILES[i][d] * P, (STEP_TILES[i][d] + 1) * P)
                        for j in range(PAIRS):
                            last = T.matmul(ps[6 + d][:, j * P:(j + 1) * P], qkv[:, PAIRS + j, cols],
                                            state[:, d * PAIRS + j, :], start=True, stop=True)
                        last.then_inc(ks_ready, 1)
                    for g, d, qs in GROUPS:
                        pe.wait_ge(x0_ready, G0 + g + 1)
                        for n, q in enumerate(range(3 * g, 3 * g + 3)):
                            last = T.transpose(ps[g][:, n * P:(n + 1) * P], XT[:, q, :], ident)
                        last.then_inc(xt_turned, 1)
                    for lv in range(1, LEVELS):
                        for g, d, qs in GROUPS:
                            ix = lvl_index(layer, i, lv, g)
                            pe.wait_ge(am_ready, ix + 1)
                            if lv > 1:
                                pe.wait_ge(x_done, ix - 3)
                            else:
                                pe.wait_ge(xm_ready, G0 + g + 1)
                            for n, q in enumerate(range(3 * g, 3 * g + 3)):
                                for r_ in halves_of(lv):
                                    last = T.matmul(blocks(g, r_)[:, n, :], Am[:, q, r_], Xm[:, q, r_],
                                                    start=True, stop=True)
                            last.then_inc(b_ready, 1)
                        for g, d, qs in GROUPS:
                            ix = lvl_index(layer, i, lv, g)
                            pe.wait_ge(b_copied, ix + 1)
                            if g >= 2:
                                pe.wait_ge(x_done, ix - 1)
                            elif lv == 1:
                                pe.wait_ge(rhs_ready, D0 + 2)
                            for n, q in enumerate(range(3 * g, 3 * g + 3)):
                                if lv < LEVELS - 1:
                                    for r_ in halves_of(lv):
                                        T.matmul(blocks(4 + g % 2 * 2, r_)[:, n, :], XT[:, q, r_], Bm[:, q, r_],
                                                 start=True, stop=True)
                                for r_ in halves_of(lv):
                                    last = T.matmul(blocks(5 + g % 2 * 2, r_)[:, n, :], Bm[:, q, r_], XT[:, q, r_],
                                                    start=True, stop=True)
                            last.then_inc(p_ready, 1)
                    for d in range(DIRS):
                        pe.wait_ge(x_done, lvl_index(layer, i, LEVELS - 1, 2 * d + 1) + 1)
                        for q in range(d * DN_HEADS, (d + 1) * DN_HEADS):
                            h = col(q) % DN_HEADS
                            last = T.matmul(ps[2 + d][:, h * HEAD:(h + 1) * HEAD], XT[:, q, :], rhs[:, col(q), :],
                                            start=True, stop=True)
                        last.then_inc(v_ready, 1)
                    for d in range(DIRS):
                        pe.wait_ge(vnew_ready, D0 + d + 1)
                        pe.wait_ge(kd_ready, D0 + d + 1)
                        if want_o:
                            pe.wait_ge(qd_ready, D0 + d + 1)
                            pe.wait_ge(qk_ready, G0 + 2 * d + 2)
                        for j in range(PAIRS):
                            if want_o:
                                T.matmul(ps[4 + d][:, j * P:(j + 1) * P], state[:, d * PAIRS + j, :],
                                         qd[:, d * PAIRS + j, :], start=True, stop=False, skip_group_check=True)
                                for half in range(2):
                                    q = d * DN_HEADS + half * PAIRS + j
                                    T.matmul(ps[4 + d][half * HEAD:(half + 1) * HEAD, j * P:(j + 1) * P],
                                             vnew[:, col(q), :], QK[:, q, :], start=False, stop=True, skip_group_check=True)
                            q = d * DN_HEADS + 2 * j
                            last = T.matmul(ps[6 + d][:, j * P:(j + 1) * P], kd[:, d * PAIRS + j, :],
                                            vnew[:, q:q + 2, :].rearrange("p a b -> p (a b)"), start=True, stop=True)
                        last.then_inc(out_ready, 1)
                link.end_phase()
                link.end_phase()
                for j in range(PAIRS):
                    T.matmul(ps[j][:, lo:N_TOK], blk, XT_flat(j)[:, lo:N_TOK], start=True, stop=True)
                link.end_phase()
                link.end_phase()
                link.end_phase()

            def gate_up(R, ft, sg, lo, first):
                if not first:
                    pe.wait_ge(act_ready, 2 * R + ft - 1)
                for which in range(2):
                    for k in range(KT):
                        if first and ft == which == 0:
                            modulated(1, k)
                        last = T.matmul(ps[2 * ft + which][:, lo:N_TOK], wide(sg + which)[:, k, ft * P:(ft + 1) * P],
                                        hT[:, k, lo:N_TOK], start=(k == 0), stop=(k == KT - 1))
                last.then_inc(gu_ready, 1)

            def down(R, par, sd, lo, first):
                pe.wait_ge(act_ready, 2 * R + 2)
                for d in range(KT):
                    if not (first and d < 4):
                        pe.wait_ge(down_added, KT * R + d - 3)
                    for ft in range(2):
                        last = T.matmul(ps[4 + d % 4][:, lo:N_TOK], deep(sd)[:, ft, d * P:(d + 1) * P],
                                        act[:, par, ft, lo:N_TOK], start=(ft == 0), stop=(ft == 1))
                    last.then_inc(down_ready, 1)

            for layer in range(N_LAYERS):
                last_layer = layer == N_LAYERS - 1
                lo = SEQ if last_layer else 0
                for j in range(MOD_SLOTS):
                    full(s)
                    b = j // 2
                    if j % 2 == 0 and b >= 3:
                        pe.wait_ge(mod_copied, layer * MOD_SLOTS // 2 + b - 2)
                    for k in range(KT):
                        r_ = slice(k % 4 * QUAD, (k % 4 + 1) * QUAD)
                        last = T.matmul(ps[5 + b % 3][r_, j % 2 * 2 * P:(j % 2 + 1) * 2 * P], cs[:, k, :],
                                        wide(s)[:, k, :], start=(k < 4), stop=(k >= 4))
                    last.then_inc(mod_ready, 1)
                    s += 1
                    if 0 <= j - FILTER_FIRST < FILTER_STAGES:
                        filter_stage(layer, j - FILTER_FIRST)
                for b in range(MOD_SLOTS // 2):
                    pe.wait_ge(mod_copied, layer * MOD_SLOTS // 2 + b + 1)
                    for m in range(4):
                        T.matmul(ps[0][:, 8 * b + 2 * m:8 * b + 2 * m + 2], modr(b)[:, m * P:(m + 1) * P],
                                 con[:, K_SUM:K_SUM + 2], start=True, stop=True)
                link.end_phase()
                link.end_phase()
                rms(0, 2 * layer)
                for j in range(IN_SLOTS):
                    full(s)
                    for half in range(2):
                        n = 2 * j + half
                        if n - 2 >= len(in_tiles):
                            break
                        if j == 0:
                            for tt in range(2):
                                for k in range(KT):
                                    if half == tt == 0:
                                        modulated(2 * layer, k)
                                    last = T.matmul(ps[half][:, tt * ABV:(tt + 1) * ABV],
                                                    hT[:, k, (2 * half + tt) * P:(2 * half + tt + 1) * P],
                                                    wide(s)[:, k, 0:ABV], start=(k == 0), stop=(k == KT - 1))
                        else:
                            t0 = lo if in_tiles[n - 2][0] in ("z", "hy", "q") else 0
                            if n >= 4:
                                who, per, upto = read_before(n - 4)
                                pe.wait_ge(who, layer * per + upto)
                            for k in range(KT):
                                last = T.matmul(ps[n % 4][:, t0:N_TOK], wide(s)[:, k, half * P:(half + 1) * P],
                                                hT[:, k, t0:N_TOK], start=(k == 0), stop=(k == KT - 1))
                        last.then_inc(proj_ready, 1)
                    s += 1
                link.end_phase()
                hyena(layer, lo)
                attention(layer)
                delta(layer, lo)
                for j in range(OUT_SLOTS):
                    full(s)
                    for half in range(2):
                        n = 2 * j + half
                        if n >= 4:
                            pe.wait_ge(mix_added, layer * KT + n - 3)
                        for k in range(KT):
                            last = T.matmul(ps[n % 4][:, lo:N_TOK], wide(s)[:, k, half * P:(half + 1) * P],
                                            hT[:, k, lo:N_TOK], start=(k == 0), stop=(k == KT - 1))
                        last.then_inc(mix_ready, 1)
                    s += 1
                link.end_phase()
                rms(lo, 2 * layer + 1)
                if not last_layer:
                    for r in range(DENSE_ROUNDS):
                        full(s)
                        full(s + 1)
                        for ft in range(2):
                            gate_up(r, ft, s, lo, r == 0)
                        s += 2
                        if r:
                            full(s)
                            down(r - 1, (r - 1) % 2, s, lo, r == 1)
                            s += 1
                    full(s)
                    down(DENSE_ROUNDS - 1, (DENSE_ROUNDS - 1) % 2, s, lo, False)
                    s += 1
                    link.end_phase()
                else:
                    pe.wait_ge(router_in, 16)
                    for k in range(KT):
                        modulated(2 * layer + 1, k)
                    for t in range(2):
                        for k in range(KT):
                            T.matmul(ps[0][:, 8 * t:8 * t + 8], hT[:, k, SEQ + t * P:SEQ + (t + 1) * P],
                                     wr[:, k, :], start=(k == 0), stop=(k == KT - 1))
                    for t in range(2):
                        for k in range(KT):
                            T.transpose(ps[1 + 2 * t + k // 4][:, k % 4 * P:(k % 4 + 1) * P],
                                        hT[:, k, SEQ + t * P:SEQ + (t + 1) * P], ident)
                    link.end_phase()
                    link.end_phase()
                    link.end_phase()
                    link.end_phase()
                    inc = con[:, K_INC:K_INC + P]
                    T.matmul(ps[0][:, 0:8], inc, mx[:, 0, 0:8], start=True, stop=True)
                    T.matmul(ps[0][:, 8:16], ones, mx[:, 0, 0:8], start=True, stop=False)
                    T.matmul(ps[0][:, 8:16], inc, mx[:, 1, 0:8], start=False, stop=True)
                    T.matmul(ps[0][:, 16:24], ones, mx[:, 0, 0:8], start=True, stop=False)
                    T.matmul(ps[0][:, 16:24], ones, mx[:, 1, 0:8], start=False, stop=True)
                    link.end_phase()
                    link.end_phase()
                    for p in range(PASSES):
                        for t in range(2):
                            T.transpose(ps[p // 2][:, (p % 2 * 2 + t) * P:(p % 2 * 2 + t + 1) * P], sel[:, t, p, :], ident)
                            last = T.matmul(ps[7][:, p:p + 1], sel[:, t, p, :], gx[:, t, p:p + 1],
                                            start=(t == 0), stop=(t == 1))
                            if t and p < 2:
                                last.then_inc(scattered if p else matok_turned, PRIME)
                    link.end_phase()
                    link.end_phase()

                    def gather(pi):
                        for k in range(KT):
                            for t in range(2):
                                last = T.matmul(ps[6 + k // 4][:, k % 4 * P:(k % 4 + 1) * P],
                                                htok[:, t, k * P:(k + 1) * P],
                                                sel[:, t, bass.ds(pi, 1), :].rearrange("p a b -> p (a b)"),
                                                start=(t == 0), stop=(t == 1))
                        last.then_inc(gathered, 1)

                    def expert(pi, narrow):
                        j = 0

                        def full_moe(j):
                            pe.wait_ge(slot_full[(S_MOE + j) % RING], pi * MOE_INC + moe_landed(j))

                        def project(bank, j):
                            for h in range(2):
                                full_moe(j + h)
                                for k in range(4):
                                    for ct in range(2 if narrow else 1):
                                        r_ = slice(ct * NARROW, (ct + 1) * NARROW) if narrow else slice(0, P)
                                        c_ = slice(ct * 2 * P, (ct + 1) * 2 * P) if narrow else slice(0, MOE_F)
                                        last = T.matmul(ps[bank][r_, 0:c_.stop - c_.start], xg[:, 4 * h + k, r_],
                                                        half_k(S_MOE + j + h)[:, k, c_],
                                                        start=(h + k == 0), stop=(h + k == 4))
                                last.then_inc(slot_used, 1)

                        def turn(r):
                            pe.wait_ge(act_ready, pi * MOE_ROUNDS + (A0 + r + 1))
                            if r == 0:
                                pe.wait_ge(down_added, (pi - 1) * KT + (ADD0 + 8))
                            pe.wait_ge(aT_ready, pi * MOE_ROUNDS + (PRIME + r))
                            for f in range(2 if narrow else 4):
                                last = T.transpose(ps[3][:, f * P:(f + 1) * P], matok[:, f * P:(f + 1) * P], ident)
                            last.then_inc(matok_turned, 1)

                        def down(r, j):
                            pe.wait_ge(aT_ready, pi * MOE_ROUNDS + (PRIME + r + 1))
                            if r == 0:
                                pe.wait_ge(y_copied, pi * 2 + PRIME)
                            for h in range(2):
                                full_moe(j + h)
                                for f in range(2):
                                    for half in range(2):
                                        r_ = slice(half * NARROW, (half + 1) * NARROW) if narrow else slice(0, P)
                                        last = T.matmul(ps[4 + half][r_, :], aT[:, r % 2, 2 * h + f, 0:r_.stop - r_.start],
                                                        deep(S_MOE + j + h)[:, f, half * 512:(half + 1) * 512],
                                                        start=(r + h + f == 0),
                                                        stop=(r == MOE_ROUNDS - 1 and h + f == 2))
                                last.then_inc(slot_used, 1)

                        pe.wait_ge(xg_ready, pi + 1)
                        for r in range(MOE_ROUNDS):
                            if r == 0:
                                pe.wait_ge(down_added, (pi - 1) * KT + (ADD0 + 2))
                            if r == 1:
                                pe.wait_ge(down_added, (pi - 1) * KT + (ADD0 + 4))
                            pe.wait_ge(sil_ready, pi * MOE_ROUNDS + (SIL0 + r - (r > 0)))
                            project(r % 2, j)
                            j += 2
                            if r:
                                turn(r - 1)
                            else:
                                pe.wait_ge(down_added, (pi - 1) * KT + (ADD0 + 6))
                            pe.wait_ge(act_ready, pi * MOE_ROUNDS + (A0 + r))
                            project(2, j)
                            j += 2
                            if r:
                                down(r - 1, j)
                                j += 2
                        turn(MOE_ROUNDS - 1)
                        gather(pi + 1)
                        down(MOE_ROUNDS - 1, j)
                        pe.wait_ge(y_copied, pi * 2 + (PRIME + 2))
                        for d in range(KT):
                            r_ = slice(d // 4 * NARROW, (d // 4 + 1) * NARROW) if narrow else slice(0, P)
                            last = T.matmul(ps[d // 2][:, d % 2 * SEQ:(d % 2 + 1) * SEQ], ytok[r_, d * P:(d + 1) * P],
                                            selnow[r_, :], start=True,
                                            stop=True)
                            last.then_inc(scattered, 1)

                    gather(0)
                    def either(pi):
                        slim = pe.value_load(meta[0:1, bass.ds(pi + (1 + EXTRA), 1)], min_val=0, max_val=1)
                        with pe.If(slim > 0):
                            expert(pi, True)
                        with pe.If(slim < 1):
                            expert(pi, False)

                    pe.wait_ge(meta_ready, 1)
                    with pe.Fori(0, N_EXPERTS) as pi:
                        either(pi)
                    n_over = pe.value_load(meta[0:1, 0:1], min_val=0, max_val=EXTRA)
                    with pe.Fori(0, EXTRA) as p:
                        with pe.If(p < n_over):
                            either(p + N_EXPERTS)
                    link.end_phase()
            rms(SEQ, 2 * N_LAYERS)
            link.end_phase()
            for k in range(KT):
                for t in range(2):
                    T.transpose(ps[k][:, t * P:(t + 1) * P], hT[:, k, SEQ + t * P:SEQ + (t + 1) * P], ident)
            link.end_phase()
            ended.append(link.phases)

        @block.scalar
        def _(ac):
            link = Link(ac, act_chain)
            A = nc.scalar

            def rms(lo, m):
                for k in range(4):
                    A.activation(hT[:, k, lo:N_TOK], xT[:, k, lo:N_TOK], ACT.Square).then_inc(sq_act, 1)
                ac.wait_ge(sum_sq, m + 1)
                link(A.activation(rms_s[:, lo:N_TOK], ps[0][:, lo:N_TOK], ACT.Ln, scale=1.0 / D_MODEL,
                                  bias=eps_col))
                A.activation(rms_r[:, lo:N_TOK], rms_s[:, lo:N_TOK], ACT.Exp, scale=-0.5).then_inc(root_ready, 1)

            def modulated(which, lo, base):
                for k in ACT_TILES:
                    ac.wait_ge(normed, base + k + 1)
                    for st_ in range(lo // SEQ, 2):
                        cols = slice(st_ * SEQ, (st_ + 1) * SEQ)
                        last = A.activation(hT[:, k, cols], hT[:, k, cols], ACT.Identity,
                                            scale=amul[:, which, k, st_:st_ + 1],
                                            bias=mod[:, 3 * which * KT + k, st_:st_ + 1])
                    last.then_inc(h_act, 1)

            link.end_phase()
            for k in range(4, KT):
                link(A.copy(xT[:, k, :], ps[k][:, :]))
            link.end_phase()
            link.end_phase()
            link(A.copy(vcol2[:, :], ps[0][:, 0:3 * KT]))
            for st_ in range(2):
                link(A.activation(cs[:, :, st_], vcol2[:, st_ * KT:(st_ + 1) * KT], ACT.Silu))
            link.end_phase()

            def filter_stage(n):
                if n in (4, 7):
                    link(A.activation((hh1 if n == 4 else hh2)[0:HEAD, :], htmp[0:HEAD, :], ACT.Sin))
                elif n == 10:
                    for m, sq in enumerate([kre[:, 0], kre[:, 1], kim[:, 0], kim[:, 1]]):
                        link(A.activation(sq, kern[:, m // 2, m % 2, :], ACT.Square))
                elif n == 12:
                    link(A.activation(hnorm[:, :], ps[4][:, :], ACT.Sqrt, bias=eps_col))
                link.end_phase()

            def hyena(lo):
                link.end_phase()
                for t in range(2):
                    link(A.copy(ut[:, t, lo:N_TOK], ps[t][:, lo:N_TOK]))
                link.end_phase()
                for _ in range(6):
                    link.end_phase()

            def attention(layer):
                link.end_phase()
                link.end_phase()
                base, todo = ATT_BASE[layer], jobs(layer)

                def exps(n):
                    lat, i, half, qt = todo[n]
                    keys = N_TOK if lat else SEQ
                    b = n % SC_BUFS
                    h = i + SW_TILES * half
                    ac.wait_ge(max_ready, base + n + 1)
                    link(A.activation(st[:, b, 2:3], rows[:, 24 + h:25 + h], ACT.Exp, bias=st[:, b, 0:1]))
                    A.activation(sc[:, b, 0:keys], sc[:, b, 0:keys], ACT.Exp, bias=st[:, b, 0:1],
                                 accum_out=st[:, b, 1:2]).then_inc(exp_ready, 1)
                    ac.wait_ge(exp_ready, base + n + 1)

                def copies(n):
                    nk = 4 if todo[n][0] else 2
                    ac.wait_ge(turn_ready, base + n + 1)
                    if n >= 2:
                        ac.wait_ge(pv_ready, base + n - 1)
                    A.copy(pT[:, n % 2, 0:nk * P], ps[2 + n % 2][:, 0:nk * P]).then_inc(turn_read, 1)
                    ac.wait_ge(turn_read, base + n + 1)

                def units(i):
                    m = layer * 2 * PAIRS + i
                    ac.wait_ge(sum_ready, m + 1)
                    if i >= 2:
                        ac.wait_ge(unit_used, m - 1)
                    A.activation(unit[:, i % 2, :], ps[7][:, :], ACT.Ln, bias=eps_col).then_inc(ln_ready, 1)
                    ac.wait_ge(ln_ready, m + 1)
                    A.activation(unit[:, i % 2, :], unit[:, i % 2, :], ACT.Exp, scale=-0.5).then_inc(unit_ready, 1)

                for it in range(len(todo) + 1):
                    if it < len(todo):
                        exps(it)
                    if it:
                        copies(it - 1)
                    if it % 2 == 1 and it // 2 < 2 * PAIRS:
                        units(it // 2)
                link.end_phase()

            def delta(layer, lo):
                link(A.activation(bt[:, :, :], abv[:, :, 12:24], ACT.Sigmoid))
                link.end_phase()
                link.end_phase()
                link(A.activation(gtmp[:, :, :], gtmp[:, :, :], ACT.Exp, scale=-1.0))
                link(A.activation(gtmp2[:, :, :], gtmp[:, :, :], ACT.Ln, bias=one_col))
                link(A.activation(rows[:, 0:12], rows[:, 0:12], ACT.Exp))
                link.end_phase()
                link.end_phase()
                link.end_phase()
                for t in range(TT):
                    link(A.copy(ktok[:, t, :], ps[2 * t][:, 0:3 * P]))
                link.end_phase()
                link.end_phase()
                link(A.copy(gc[:, :, :].rearrange("p a b -> p (a b)"), ps[0][:, 0:TT * PROBS]))
                link(A.activation(eg[:, :, :], gc[:, :, :], ACT.Exp))
                link.end_phase()
                for i in range(4):
                    G0, D0 = (layer * 4 + i) * 4, (layer * 4 + i) * DIRS
                    if i:
                        ac.wait_ge(state_ready, D0)
                    for g, d, qs in GROUPS:
                        r_ = slice(g % 2 * HEAD, (g % 2 + 1) * HEAD)
                        ac.wait_ge(r_ready, G0 + g + 1)
                        A.activation(egb[r_, d * PAIRS:(d + 1) * PAIRS, :], three(g)[r_, :, :],
                                     ACT.Exp).then_inc(egb_ready, 1)
                    for g, d, qs in GROUPS:
                        ac.wait_ge(diff_ready, G0 + g + 1)
                        A.activation(Amat[:, qs, :], Amat[:, qs, :], ACT.Exp).then_inc(decay_ready, 1)
                    A.activation(kds[:, :], kds[:, :], ACT.Exp).then_inc(kds_ready, 1)
                    for g, d, qs in GROUPS:
                        ac.wait_ge(xt_turned, G0 + g + 1)
                        A.copy(Xm[:, qs, :], three(g)).then_inc(xm_ready, 1)
                    for lv in range(1, LEVELS):
                        for g, d, qs in GROUPS:
                            ix = lvl_index(layer, i, lv, g)
                            ac.wait_ge(b_ready, ix + 1)
                            if lv > 1:
                                ac.wait_ge(p_ready, ix - 3)
                            for r_ in halves_of(lv):
                                last = A.copy(Bm[r_, qs, r_], blocks(g, r_))
                            last.then_inc(b_copied, 1)
                            ac.wait_ge(b_copied, ix + 1)
                    for d in range(DIRS):
                        ac.wait_ge(v_ready, D0 + d + 1)
                        A.copy(vnew[:, d * DN_HEADS:(d + 1) * DN_HEADS, :], six(2 + d)).then_inc(vnew_ready, 1)
                link.end_phase()
                for j in range(PAIRS):
                    link(A.activation(XT_flat(j)[:, lo:N_TOK], hT[:, j, lo:N_TOK], ACT.Square))
                link.end_phase()
                link.end_phase()
                for j in range(PAIRS):
                    link(A.activation(XT_flat(j)[:, lo:N_TOK], ps[j][:, lo:N_TOK], ACT.Ln, scale=1.0 / HEAD,
                                      bias=eps_col))
                for j in range(PAIRS):
                    link(A.activation(XT_flat(j)[:, lo:N_TOK], XT_flat(j)[:, lo:N_TOK], ACT.Exp, scale=-0.5))
                link.end_phase()
                link.end_phase()

            def silus(R, ft, lo, first):
                ac.wait_ge(gu_ready, 2 * R + ft + 1)
                if not first:
                    ac.wait_ge(act_ready, 2 * R + ft - 1)
                A.activation(sil[:, ft, lo:N_TOK], ps[2 * ft][:, lo:N_TOK], ACT.Silu).then_inc(sil_ready, 1)

            n_normed = 0
            for layer in range(N_LAYERS):
                last_layer = layer == N_LAYERS - 1
                lo = SEQ if last_layer else 0
                for j in range(MOD_SLOTS):
                    b = j // 2
                    if j % 2:
                        ac.wait_ge(mod_ready, layer * MOD_SLOTS + j + 1)
                        A.copy(modr(b), ps[5 + b % 3][:, :]).then_inc(mod_copied, 1)
                    if 0 <= j - FILTER_FIRST < FILTER_STAGES:
                        filter_stage(j - FILTER_FIRST)
                link.end_phase()
                link.end_phase()
                rms(0, 2 * layer)
                modulated(0, 0, n_normed)
                n_normed += KT
                kinds = ["abv"] * 2 + [k for k, _ in in_tiles]
                for n in range(2, len(kinds)):
                    kind, i = in_tiles[n - 2]
                    if kind == "hy":
                        continue
                    if kind == "dn":
                        who, per, upto = read_before(n)
                        ac.wait_ge(who, layer * per + upto)
                        link(A.activation(qkv[:, i, :], qkv[:, i, :], ACT.Silu))
                        continue
                    ac.wait_ge(proj_ready, layer * len(kinds) + n + 1)
                    _, per, upto = read_before(n)
                    if kind == "z":
                        A.activation(zz[:, i, lo:N_TOK], ps[n % 4][:, lo:N_TOK], ACT.Silu).then_inc(copy_done, 1)
                    elif kind == "q":
                        A.copy(qT[:, i, lo:N_TOK], ps[n % 4][:, lo:N_TOK]).then_inc(copy_done, 1)
                    else:
                        A.copy(kT[:, :], ps[n % 4][:, :]).then_inc(copy_done, 1)
                    ac.wait_ge(copy_done, layer * per + upto)
                link.end_phase()
                hyena(lo)
                attention(layer)
                delta(layer, lo)
                link.end_phase()
                rms(lo, 2 * layer + 1)
                modulated(1, lo, n_normed)
                n_normed += KT
                if not last_layer:
                    for r in range(DENSE_ROUNDS):
                        for ft in range(2):
                            silus(r, ft, lo, r == 0)
                    link.end_phase()
                else:
                    link.end_phase()
                    for n in range(4):
                        link(A.copy(htok[:, n // 2, n % 2 * 512:(n % 2 + 1) * 512], ps[1 + n][:, :]))
                    link.end_phase()
                    link(A.activation(tmp8[:, :, 0:1], tmp8[:, :, 0:1], ACT.Exp))
                    link.end_phase()
                    link.end_phase()
                    link.end_phase()
                    link.end_phase()
                    link.end_phase()
                    for b in range(6):
                        w = min(2, PASSES - 2 * b)
                        last = A.copy(selT[:, 2 * b:2 * b + w, :], ps[b][:, 0:w * SEQ].rearrange("p (a b) -> p a b", a=w))
                        if b == 4:
                            last.then_inc(aT_ready, PRIME)
                        elif b == 5:
                            last.then_inc(y_copied, PRIME)
                        else:
                            link(last)
                    ac.wait_ge(y_copied, PRIME)
                    link.end_phase()

                    def fetch(pi):
                        A.copy(xg[:, 0:4, :], ps[6][:, :].rearrange("p (a b) -> p a b", a=4))
                        A.copy(xg[:, 4:8, :], ps[7][:, :].rearrange("p (a b) -> p a b", a=4)).then_inc(xg_ready, 1)

                    def copy_turn(pi, r, narrow):
                        ac.wait_ge(matok_turned, pi * MOE_ROUNDS + (PRIME + r + 1))
                        if r >= 2:
                            ac.wait_ge(slot_used, pi * len(MOE_ORDER) + (d_done[r - 2]))
                        elif r == 0:
                            ac.wait_ge(y_copied, pi * 2 + PRIME)
                        if narrow:
                            A.copy(aT[:, r % 2, :, 0:NARROW].rearrange("p (a f) n -> p f a n", f=2),
                                   ps[3][:, 0:2 * P].rearrange("p (f a n) -> p f a n", f=2, a=2)).then_inc(aT_ready, 1)
                        else:
                            A.copy(aT[:, r % 2, :, :],
                                   ps[3][:, :].rearrange("p (a b) -> p a b", a=4)).then_inc(aT_ready, 1)

                    def expert(pi, narrow):
                        w = MOE_F // 2 if narrow else MOE_F
                        for r in range(MOE_ROUNDS):
                            ac.wait_ge(slot_used, pi * len(MOE_ORDER) + g_done[r])
                            ac.wait_ge(act_ready, pi * MOE_ROUNDS + (A0 + r))
                            A.activation(msil[:, 0:w], ps[r % 2][:, 0:w], ACT.Silu).then_inc(sil_ready, 1)
                            if r:
                                copy_turn(pi, r - 1, narrow)
                        copy_turn(pi, MOE_ROUNDS - 1, narrow)
                        fetch_next(pi)
                        ac.wait_ge(scattered, pi * KT + PRIME)
                        A.copy(selnow[:, :], selT[:, bass.ds(pi, 1), :].rearrange("p a b -> p (a b)"))
                        ac.wait_ge(slot_used, (pi + 1) * len(MOE_ORDER))
                        for half in range(2):
                            r_ = slice(half * NARROW, (half + 1) * NARROW) if narrow else slice(0, P)
                            A.copy(ytok[r_, half * 512:(half + 1) * 512], ps[4 + half][r_, :]).then_inc(y_copied, 1)

                    def fetch_next(pi):
                        ac.wait_ge(gathered, pi + 2)
                        fetch(pi + 1)

                    ac.wait_ge(gathered, 1)
                    fetch(0)
                    def either(pi):
                        slim = ac.value_load(meta[0:1, bass.ds(pi + (1 + EXTRA), 1)], min_val=0, max_val=1)
                        with ac.If(slim > 0):
                            expert(pi, True)
                        with ac.If(slim < 1):
                            expert(pi, False)

                    ac.wait_ge(meta_ready, 1)
                    with ac.Fori(0, N_EXPERTS) as pi:
                        either(pi)
                    n_over = ac.value_load(meta[0:1, 0:1], min_val=0, max_val=EXTRA)
                    with ac.Fori(0, EXTRA) as p:
                        with ac.If(p < n_over):
                            either(p + N_EXPERTS)
                    link.end_phase()
            rms(SEQ, 2 * N_LAYERS)
            for k in range(KT):
                ac.wait_ge(normed, n_normed + k + 1)
                link(A.activation(hT[:, k, SEQ:N_TOK], hT[:, k, SEQ:N_TOK], ACT.Copy,
                                  scale=vcol2[:, 2 * KT + k:2 * KT + k + 1]))
            link.end_phase()
            link.end_phase()
            for k in range(4):
                for t in range(2):
                    link(A.copy(hT[:, 2 * t + k // 4, k % 4 * P:(k % 4 + 1) * P], ps[k][:, t * P:(t + 1) * P]))
            ac.drain().then_inc(rows_out, 1)
            ended.append(link.phases)

        @block.vector
        def _(ve):
            link = Link(ve, dve_chain)
            V = nc.vector

            def tt(out, a_, b_, op):
                link(V.tensor_tensor(out, a_, b_, op))

            def rms(lo, base):
                for k in range(4, KT):
                    V.tensor_tensor(hT[:, k, lo:N_TOK], xT[:, k, lo:N_TOK], xT[:, k, lo:N_TOK],
                                    ALU.mult).then_inc(sq_dve, 1)
                ve.wait_ge(root_ready, base // KT + 1)
                for k in range(KT):
                    V.tensor_tensor(hT[:, k, lo:N_TOK], xT[:, k, lo:N_TOK], rms_r[:, lo:N_TOK],
                                    ALU.mult).then_inc(normed, 1)

            link(V.memset(eps_col, RMS_EPS))
            link(V.memset(cs[:, :, :], 0.0))
            link(V.memset(one_col, 1.0))
            link.end_phase()
            for k in range(4):
                link(V.tensor_copy(xT[:, k, :], ps[k][:, :]))
            link.end_phase()
            link.end_phase()
            link.end_phase()

            def conv(dst, src, lo, w, j0, j, n):
                d3, s3 = seg(dst, lo), seg(src, lo)
                link(V.tensor_scalar(dst[:, lo:N_TOK], src[:, lo:N_TOK], vcol[:, w + n + j:w + n + j + 1], None, ALU.mult))
                link(V.scalar_tensor_tensor(out=d3[:, :, 1:SEQ], in0=s3[:, :, 0:SEQ - 1], scalar=vcol[:, w + j:w + j + 1],
                                            in1=d3[:, :, 1:SEQ], op0=ALU.mult, op1=ALU.add))
                return V.scalar_tensor_tensor(out=d3[:, :, 0:SEQ - 1], in0=s3[:, :, 1:SEQ],
                                              scalar=vcol[:, w + 2 * n + j:w + 2 * n + j + 1],
                                              in1=d3[:, :, 0:SEQ - 1], op0=ALU.mult, op1=ALU.add)

            def filter_stage(n):
                if n == 1:
                    link(V.tensor_copy(vcol[:, 0:V_END], ps[1][:, 0:V_END]))
                elif n in (3, 6):
                    layer_b, layer_f = (V_B1, V_FR1) if n == 3 else (V_B2, V_FR2)
                    h, n_ = htmp[0:HEAD, :], htmp2[0:HEAD, :]
                    link(V.tensor_scalar(h, ps[0][0:HEAD, 0:SEQ], vcol[0:HEAD, layer_b:layer_b + 1],
                                         vcol[0:HEAD, layer_f:layer_f + 1], ALU.add, ALU.mult))
                    link(V.tensor_scalar(n_, h, 1.0 / (2 * np.pi), None, ALU.mult))
                    link(V.tensor_scalar(n_, n_, ROUND, None, ALU.add))
                    link(V.tensor_scalar(n_, n_, -ROUND, None, ALU.add))
                    for part in TWO_PI:
                        link(V.scalar_tensor_tensor(out=h, in0=n_, scalar=-part, in1=h, op0=ALU.mult, op1=ALU.add))
                    link(V.tensor_scalar(h, h, PI_BELOW, -PI_BELOW, ALU.min, ALU.max))
                elif n == 9:
                    for mt in range(2):
                        for d in range(2):
                            w = hc[:, H_WIN + (2 * mt + d) * HY_CH:H_WIN + (2 * mt + d + 1) * HY_CH]
                            tt(kern[:, mt, d, :].rearrange("p (o c) -> p o c", o=2),
                               ps[2 * mt + d][:, :].rearrange("p (o c) -> p o c", o=2),
                               w.unsqueeze(1).to_broadcast([P, 2, HY_CH]), ALU.mult)
                elif n == 12:
                    for mt in range(2):
                        tt(kre[:, mt], kern[:, mt, 0, :], kern[:, mt, 1, :], ALU.add)
                        tt(kern[:, mt, 1, :], kern[:, mt, 1, :], kern[:, mt, 0, :], ALU.subtract)
                elif n == 13:
                    link(V.reciprocal(hnorm[:, :], hnorm[:, :]))
                elif n == 14:
                    for f in range(2):
                        tt(kre[:, f], ps[f][:, :], hnorm[:, :], ALU.mult)
                        tt(kre[:, f], kre[:, f], hskip[:, :], ALU.add)
                        tt(kim[:, f], ps[2 + f][:, :], hnorm[:, :], ALU.mult)
                link.end_phase()

            def hyena(layer, lo):
                link.end_phase()
                for t in range(2):
                    link(V.tensor_copy(x1t[:, t, lo:N_TOK], ps[2 + t][:, lo:N_TOK]))
                link.end_phase()
                for order in range(2):
                    for f in range(2):
                        ve.wait_ge(freq_ready, 4 * layer + 2 * order + f + 1)
                        o = slice(order * HY_CH, (order + 1) * HY_CH)
                        kr = kre[:, f, o].unsqueeze(1).to_broadcast([P, SEG(lo), HY_CH])
                        ki = kim[:, f, o].unsqueeze(1).to_broadcast([P, SEG(lo), HY_CH])
                        ur, us = seg(ps[f], lo), seg(ps[2 + f], lo)
                        pr, pi_, tm = seg(pre[:, f], lo), seg(pim[:, f], lo), seg(ptmp, lo)
                        tt(pr, ur, kr, ALU.mult)
                        tt(tm, us, ki, ALU.mult)
                        tt(pr, pr, tm, ALU.add)
                        tt(pi_, ur, ki, ALU.mult)
                        tt(tm, us, kr, ALU.mult)
                        tt(pi_, pi_, tm, ALU.subtract)
                    link.end_phase()
                    link.end_phase()
                    for t in range(2):
                        if order == 0:
                            tt(ut[:, t, lo:N_TOK], ps[t][:, lo:N_TOK], x1t[:, t, lo:N_TOK], ALU.mult)
                        else:
                            tt(hT[:, PAIRS + t, lo:N_TOK], ps[t][:, lo:N_TOK], hy[:, 4 + t, lo:N_TOK], ALU.mult)
                    link.end_phase()

            def attention(layer):
                link.end_phase()
                for i in range(4):
                    x_ = qT[:, i, SEQ:N_TOK] if i < SW_TILES else kT[:, SEQ:N_TOK]
                    tt(rot[:, i, :], ps[i // 2][:, i % 2 * SEQ:(i % 2 + 1) * SEQ], con[:, K_SIN:K_SIN + SEQ], ALU.mult)
                    tt(x_, x_, con[:, K_COS:K_COS + SEQ], ALU.mult)
                    tt(x_, x_, rot[:, i, :], ALU.add)
                link.end_phase()
                base, todo = ATT_BASE[layer], jobs(layer)

                def bufs(n):
                    b = n % SC_BUFS
                    return sc[:, b, :], st[:, b, :], ps[SC_BANKS[b]], N_TOK if todo[n][0] else SEQ

                def softmax_step(n):
                    if n < len(todo):
                        lat, i, half, qt = todo[n]
                        sc_n, st_n, bank, keys = bufs(n)
                        h = i + SW_TILES * half
                        ve.wait_ge(score_ready, base + n + 1)
                        if n >= SC_BUFS:
                            ve.wait_ge(turn_ready, base + n - SC_BUFS + 1)
                        if lat:
                            band = con[:, K_BAND + qt * N_TOK:K_BAND + (qt + 1) * N_TOK]
                            V.scalar_tensor_tensor(out=sc_n, in0=bank[:, :], scalar=HEAD ** -0.5, in1=band,
                                                   op0=ALU.mult, op1=ALU.add).then_inc(score_read, 1)
                        else:
                            V.tensor_scalar(sc_n[:, 0:keys], bank[:, 0:keys], HEAD ** -0.5, None,
                                            ALU.mult).then_inc(score_read, 1)
                    if n:
                        sc_m, st_m, _, keys_m = bufs(n - 1)
                        ve.wait_ge(exp_ready, base + n)
                        added = link.later(V.tensor_tensor(st_m[:, 4:5], st_m[:, 1:2], st_m[:, 2:3], ALU.add))
                    if n < len(todo):
                        ve.wait_ge(score_read, base + n + 1)
                        reduced = link.later(V.tensor_reduce(st_n[:, 3:4], sc_n[:, 0:keys], X_AXIS, ALU.max))
                    if n:
                        ve.wait_ge(dve_chain, added)
                        turned = link.later(V.reciprocal(st_m[:, 5:6], st_m[:, 4:5]))
                    if n < len(todo):
                        ve.wait_ge(dve_chain, reduced)
                        V.tensor_scalar(st_n[:, 0:1], st_n[:, 3:4], rows[:, 24 + h:25 + h], -1.0, ALU.max,
                                        ALU.mult).then_inc(max_ready, 1)
                    if n:
                        ve.wait_ge(dve_chain, turned)
                        V.tensor_scalar(sc_m[:, 0:keys_m], sc_m[:, 0:keys_m], st_m[:, 5:6], None,
                                        ALU.mult).then_inc(prob_ready, 1)

                def outputs(n):
                    lat, i, half, qt = todo[n]
                    rows_ = slice(half * HEAD, (half + 1) * HEAD)
                    ve.wait_ge(pv_ready, base + n + 1)
                    q0 = lat * SEQ + qt * P
                    V.tensor_copy(hT[rows_, PAIRS + 2 + i, q0:q0 + P], ps[4 + n % 2][rows_, 0:P]).then_inc(pv_read, 1)

                def to_unit(i):
                    ve.wait_ge(unit_ready, layer * 2 * PAIRS + i + 1)
                    V.scalar_tensor_tensor(out=qkv[:, i, :], in0=qkv[:, i, :], scalar=(HEAD ** -0.5 if i < PAIRS else 1.0),
                                           in1=unit[:, i % 2, :], op0=ALU.mult, op1=ALU.mult).then_inc(unit_used, 1)

                for it in range(len(todo) + 3):
                    if it <= len(todo):
                        softmax_step(it)
                    if it >= 3:
                        outputs(it - 3)
                    if it % 2 == 1 and 3 <= it and (it - 3) // 2 < 2 * PAIRS:
                        to_unit((it - 3) // 2)
                link.end_phase()

            def delta(layer, lo):
                dtb = rows[:, 12:24].unsqueeze(1).to_broadcast([P, TT, PROBS])
                tt(gt[:, :, :], abv[:, :, 0:12], dtb, ALU.add)
                link(V.tensor_scalar(gtmp2[:, :, :], gt[:, :, :], -1.0, None, ALU.mult))
                tt(gtmp[:, :, :], gt[:, :, :], gtmp2[:, :, :], ALU.max)
                link.end_phase()
                link.end_phase()
                link.end_phase()
                link(V.tensor_scalar(gc[:, :, :], gtmp[:, :, :], 1.0, None, ALU.add))
                link(V.tensor_scalar(gc[:, :, :], gc[:, :, :], -1.0, None, ALU.add))
                link(V.tensor_scalar(gc[:, :, :], gc[:, :, :], TINY, None, ALU.add))
                link(V.reciprocal(eg[:, :, :], gc[:, :, :]))
                link(V.tensor_scalar(gtmp2[:, :, :], gtmp2[:, :, :], TINY, None, ALU.add))
                tt(gtmp2[:, :, :], gtmp2[:, :, :], eg[:, :, :], ALU.mult)
                tt(gtmp2[:, :, :], gtmp2[:, :, :], gtmp[:, :, :], ALU.mult)
                link(V.scalar_tensor_tensor(out=gt[:, :, :], in0=gt[:, :, :], scalar=0.0, in1=gtmp2[:, :, :],
                                            op0=ALU.max, op1=ALU.add))
                link(V.scalar_tensor_tensor(out=gt[:, :, :], in0=gt[:, :, :], scalar=-1.0,
                                            in1=rows[:, 0:12].unsqueeze(1).to_broadcast([P, TT, PROBS]),
                                            op0=ALU.mult, op1=ALU.mult))
                link.end_phase()
                link.end_phase()
                for t in range(TT):
                    link(V.tensor_copy(vtok[:, t, :], ps[2 * t + 1][:, 0:3 * P]))
                link.end_phase()
                link.end_phase()
                link.end_phase()
                for i in range(4):
                    G0, D0 = (layer * 4 + i) * 4, (layer * 4 + i) * DIRS
                    for g, d, qs in GROUPS:
                        tile = STEP_TILES[i][d]
                        end = P - 1 if d == 0 else 0
                        ve.wait_ge(egb_ready, G0 + g + 1)
                        for n, q in enumerate(range(3 * g, 3 * g + 3)):
                            V.tensor_scalar(Amat[:, q, :], ps[g][:, n * P:(n + 1) * P], gc[:, tile, col(q):col(q) + 1], 0.0,
                                            ALU.subtract, ALU.min)
                        V.tensor_tensor(kds[:, cols3(g)], three(g)[:, :, end:end + 1].rearrange("p a b -> p (a b)"),
                                        gc[:, tile, cols3(g)], ALU.subtract).then_inc(diff_ready, 1)
                    for d in range(DIRS):
                        cols = slice(STEP_TILES[i][d] * P, (STEP_TILES[i][d] + 1) * P)
                        ve.wait_ge(beta_ready, D0 + d + 1)
                        V.tensor_tensor(kb[:, d * PAIRS:(d + 1) * PAIRS, :], three(4 + d), qkv[:, PAIRS:2 * PAIRS, cols],
                                        ALU.mult).then_inc(kb_ready, 1)

                    def mask_scores(g):
                        ve.wait_ge(kq_ready, G0 + g + 1)
                        ve.wait_ge(decay_ready, G0 + g + 1)
                        V.tensor_tensor(QK[:, 3 * g:3 * g + 3, :], three(6 + g % 2), Amat[:, 3 * g:3 * g + 3, :],
                                        ALU.mult).then_inc(qk_read, 1)

                    def first_inverse(g):
                        qs = slice(3 * g, 3 * g + 3)
                        ve.wait_ge(kk_ready, G0 + g + 1)
                        V.tensor_tensor(Amat[:, qs, :], three(4 + g % 2), Amat[:, qs, :], ALU.mult).then_inc(a_ready, 1)
                        ve.wait_ge(a_ready, G0 + g + 1)
                        tt(XT[:, qs, :], Amat[:, qs, :], mask(K_LVL + g // 2 * LEVELS * P), ALU.mult)
                        V.tensor_tensor(XT[:, qs, :], mask(K_ID), XT[:, qs, :], ALU.subtract).then_inc(x0_ready, 1)

                    mask_scores(0)
                    mask_scores(1)
                    first_inverse(0)
                    first_inverse(1)
                    mask_scores(2)
                    mask_scores(3)
                    first_inverse(2)
                    first_inverse(3)
                    for d in range(DIRS):
                        tile = STEP_TILES[i][d]
                        qs = slice(d * DN_HEADS, (d + 1) * DN_HEADS)
                        ve.wait_ge(ks_ready, D0 + d + 1)
                        tt(rhs[:, qs, :], six(6 + d), over(eg[:, tile, qs], HEAD), ALU.mult)
                        tt(rhs[:, qs, :], vtok[:, tile, :].rearrange("p (a b) -> p a b", a=DN_HEADS), rhs[:, qs, :],
                           ALU.subtract)
                        V.tensor_tensor(rhs[:, qs, :], rhs[:, qs, :], over(bt[:, tile, qs], HEAD),
                                        ALU.mult).then_inc(rhs_ready, 1)
                    ve.wait_ge(egb_ready, G0 + 4)
                    for d in range(DIRS):
                        cols = slice(STEP_TILES[i][d] * P, (STEP_TILES[i][d] + 1) * P)
                        V.tensor_tensor(qd[:, d * PAIRS:(d + 1) * PAIRS, :], egb[:, d * PAIRS:(d + 1) * PAIRS, :],
                                        qkv[:, 0:PAIRS, cols], ALU.mult).then_inc(qd_ready, 1)
                    for lv in range(1, LEVELS):
                        for g, d, qs in GROUPS:
                            ix = lvl_index(layer, i, lv, g)
                            ve.wait_ge(p_ready, ix + 1)
                            for r_ in halves_of(lv):
                                if lv < LEVELS - 1:
                                    V.tensor_tensor(Xm[r_, qs, r_], Xm[r_, qs, r_], blocks(4 + g % 2 * 2, r_), ALU.subtract)
                                last = V.tensor_tensor(XT[r_, qs, r_], XT[r_, qs, r_], blocks(5 + g % 2 * 2, r_),
                                                       ALU.subtract)
                            last.then_inc(x_done, 1)
                            ve.wait_ge(x_done, ix + 1)
                    for d in range(DIRS):
                        end = P - 1 if d == 0 else 0
                        pd = slice(d * PAIRS, (d + 1) * PAIRS)
                        ve.wait_ge(out_ready, D0 + d + 1)
                        tile = STEP_TILES[i][d]
                        o_ = hT[:, 0:PAIRS, tile * P:(tile + 1) * P]
                        if i % 2 == 0 and not (layer == N_LAYERS - 1 and i < 2):
                            V.tensor_copy(o_, three(4 + d))
                        elif not (layer == N_LAYERS - 1 and i < 2):
                            V.tensor_tensor(o_, three(4 + d), o_, ALU.add)
                        for half in range(2):
                            r_ = slice(half * HEAD, (half + 1) * HEAD)
                            tt(state[r_, pd, r_], state[r_, pd, r_],
                               egb[r_, pd, end:end + 1].to_broadcast([HEAD, PAIRS, HEAD]), ALU.mult)
                            last = V.tensor_tensor(state[r_, pd, r_], three(6 + d)[r_, :, r_], state[r_, pd, r_], ALU.add)
                        last.then_inc(state_ready, 1)
                        ve.wait_ge(state_ready, D0 + d + 1)
                link.end_phase()
                link.end_phase()
                link.end_phase()
                link.end_phase()
                for j in range(PAIRS):
                    x_ = XT_flat(j)[:, lo:N_TOK]
                    link(V.scalar_tensor_tensor(out=x_, in0=x_, scalar=vcol[:, V_DNG:V_DNG + 1], in1=zz[:, j, lo:N_TOK],
                                                op0=ALU.mult, op1=ALU.mult))
                    tt(hT[:, j, lo:N_TOK], hT[:, j, lo:N_TOK], x_, ALU.mult)
                link.end_phase()

            def gated(R, ft, par, lo, first):
                ve.wait_ge(sil_ready, 2 * R + ft + 1)
                if not first:
                    ve.wait_ge(down_ready, KT * (R - 1))
                V.tensor_tensor(act[:, par, ft, lo:N_TOK], sil[:, ft, lo:N_TOK], ps[2 * ft + 1][:, lo:N_TOK],
                                ALU.mult).then_inc(act_ready, 1)

            def add_down(R, lo):
                for d in range(KT):
                    ve.wait_ge(down_ready, KT * R + d + 1)
                    for st_ in range(lo // SEQ, 2):
                        c = slice(st_ * SEQ, (st_ + 1) * SEQ)
                        last = V.scalar_tensor_tensor(out=xT[:, d, c], in0=ps[4 + d % 4][:, c],
                                                      scalar=mod[:, 5 * KT + d, st_:st_ + 1], in1=xT[:, d, c],
                                                      op0=ALU.mult, op1=ALU.add)
                    last.then_inc(down_added, 1)

            n_normed = 0
            for layer in range(N_LAYERS):
                last_layer = layer == N_LAYERS - 1
                lo = SEQ if last_layer else 0
                for n in range(FILTER_STAGES):
                    filter_stage(n)
                link.end_phase()
                tt(mod[:, :, :], ps[0][:, 0:2 * N_MOD_TILES].rearrange("p (a b) -> p a b", b=2),
                   over(vcol[:, V_BMOD:V_BMOD + N_MOD_TILES], 2), ALU.add)
                for which, gcol in ((0, V_GMIX), (1, V_GFFN)):
                    m0 = (3 * which + 1) * KT
                    link(V.scalar_tensor_tensor(out=amul[:, which], in0=mod[:, m0:m0 + KT, :], scalar=1.0,
                                                in1=over(vcol[:, gcol:gcol + KT], 2), op0=ALU.add, op1=ALU.mult))
                link.end_phase()
                rms(0, n_normed)
                n_normed += KT
                kinds = ["abv"] * 2 + [k for k, _ in in_tiles]
                for n in range(len(kinds)):
                    if kinds[n] in ("z", "q", "k"):
                        continue
                    ve.wait_ge(proj_ready, layer * len(kinds) + n + 1)
                    _, per, upto = read_before(n)
                    if n < 2:
                        last = V.tensor_copy(abv[:, 2 * n:2 * n + 2, :],
                                             ps[n][:, 0:2 * ABV].rearrange("p (a b) -> p a b", a=2))
                    elif kinds[n] == "dn":
                        i = in_tiles[n - 2][1]
                        last = conv(qkv[:, i, :], ps[n % 4], 0, V_DNC, 0, i, DN_TILES)
                    else:
                        i = in_tiles[n - 2][1]
                        last = conv(hy[:, i, :], ps[n % 4], lo, V_HYC, 0, i, HY_TILES)
                    last.then_inc(conv_done, 1)
                    ve.wait_ge(conv_done, layer * per + upto)
                link.end_phase()
                hyena(layer, lo)
                attention(layer)
                delta(layer, lo)
                for n in range(KT):
                    ve.wait_ge(mix_ready, layer * KT + n + 1)
                    for st_ in range(lo // SEQ, 2):
                        c = slice(st_ * SEQ, (st_ + 1) * SEQ)
                        last = V.scalar_tensor_tensor(out=xT[:, n, c], in0=ps[n % 4][:, c],
                                                      scalar=mod[:, 2 * KT + n, st_:st_ + 1], in1=xT[:, n, c],
                                                      op0=ALU.mult, op1=ALU.add)
                    last.then_inc(mix_added, 1)
                link.end_phase()
                rms(lo, n_normed)
                n_normed += KT
                if not last_layer:
                    for r in range(DENSE_ROUNDS):
                        for ft in range(2):
                            gated(r, ft, r % 2, lo, r < 2)
                        if r:
                            add_down(r - 1, lo)
                    add_down(DENSE_ROUNDS - 1, lo)
                    link.end_phase()
                else:
                    link.end_phase()
                    link(V.tensor_copy(lg[:, :, :], ps[0][:, 0:16].rearrange("p (a b) -> p a b", a=2)))
                    for t in range(2):
                        link(V.max(top[:, t, :], lg[:, t, :]))
                        link(V.max_index(topi[:, t, :], top[:, t, :], lg[:, t, :]))
                    link(V.tensor_copy(tix[:, :, :], topi[:, :, :]))
                    tt(tmp8[:, :, 0:1], top[:, :, 1:2], top[:, :, 0:1], ALU.subtract)
                    link.end_phase()
                    for x_ in (mx, gx, rx):
                        link(V.memset(x_[:, :, :], 0.0))
                    link(V.memset(sel[:, :, PASSES, :], 0.0))
                    link.end_phase()
                    link(V.tensor_scalar(tmp8[:, :, 1:2], tmp8[:, :, 0:1], 1.0, None, ALU.add))
                    link(V.reciprocal(tmp8[:, :, 2:3], tmp8[:, :, 1:2]))
                    tt(tmp8[:, :, 3:4], tmp8[:, :, 2:3], tmp8[:, :, 0:1], ALU.mult)
                    iota = con[:, K_IOTA:K_IOTA + 8]
                    for t in range(2):
                        first, second = tix[:, t, 0:1], tix[:, t, 1:2]
                        for x_, w in ((mx, None), (gx, tmp8)):
                            ops = (ALU.is_equal,) if w is None else (ALU.is_equal, ALU.mult)
                            w1, w2 = (None, None) if w is None else (w[:, t, 2:3], w[:, t, 3:4])
                            link(V.tensor_scalar(x_[:, t, 0:8], iota, first, w1, *ops))
                            link(V.tensor_scalar(top[:, t, :], iota, second, w2, *ops))
                            tt(x_[:, t, 0:8], x_[:, t, 0:8], top[:, t, :], ALU.add)
                    link.end_phase()
                    link.end_phase()
                    link(V.tensor_scalar(rx[:, :, 0:8], ps[0][:, 0:16].rearrange("p (a b) -> p a b", a=2), -1.0, None,
                                         ALU.add))
                    link(V.tensor_scalar(over8[:, :], ps[0][:, 16:24], float(CAP), None, ALU.is_gt))
                    link(V.tensor_tensor_scan(incl8[:, :], ones[:, 0:8], over8[:, :], 0.0, ALU.mult, ALU.add))
                    slim = metaf[:, 1 + EXTRA:]
                    link(V.tensor_scalar(slim[:, 0:8], ps[0][:, 16:24], float(NARROW), None, ALU.is_le))
                    nth = con[:, K_IOTA + 1:K_IOTA + 1 + EXTRA].unsqueeze(2).to_broadcast([P, EXTRA, 8])
                    tt(hot8[:, :, :], incl8.unsqueeze(1).to_broadcast([P, EXTRA, 8]), nth, ALU.is_equal)
                    tt(hot8[:, :, :], hot8[:, :, :], over8.unsqueeze(1).to_broadcast([P, EXTRA, 8]), ALU.mult)
                    picks = [(iota, metaf[:, 1:1 + EXTRA]), (ps[0][:, 16:24], slim[:, 8:8 + EXTRA])]
                    picks += [(x_[:, t, 0:8], x_[:, t, 8:8 + EXTRA]) for x_ in (mx, gx, rx) for t in range(2)]
                    for m, (src, _) in enumerate(picks):
                        V.tensor_tensor(prod8[:, m, :, :], hot8[:, :, :], src.unsqueeze(1).to_broadcast([P, EXTRA, 8]),
                                        ALU.mult)
                    prods_done = link.later(V.tensor_copy(metaf[:, 0:1], incl8[:, 7:8]))
                    ve.wait_ge(dve_chain, prods_done)
                    for m, (_, dst) in enumerate(picks):
                        last = V.tensor_reduce(dst, prod8[:, m, :, :], X_AXIS, ALU.add)
                    link(last)
                    V.tensor_scalar(slim[:, 8:8 + EXTRA], slim[:, 8:8 + EXTRA], float(CAP + NARROW), None, ALU.is_le)
                    link(V.tensor_scalar(rx[:, :, 8:8 + EXTRA], rx[:, :, 8:8 + EXTRA], -float(CAP), None, ALU.add))
                    V.tensor_copy(meta[:, :], metaf[:, :]).then_inc(meta_ready, 1)
                    ve.wait_ge(meta_ready, 1)
                    for t in range(2):
                        link(V.scalar_tensor_tensor(out=rxn[:, t, :], in0=slim, scalar=float(NARROW), in1=rx[:, t, 0:PASSES],
                                                    op0=ALU.mult, op1=ALU.add))
                    for p in range(PASSES):
                        for t in range(2):
                            for c0, place in ((0, rx), (NARROW, rxn)):
                                V.tensor_scalar(sel[:, t, p, c0:c0 + NARROW], con[:, K_IOTA + c0:K_IOTA + c0 + NARROW],
                                                place[:, t, p:p + 1], mx[:, t, p:p + 1], ALU.is_equal, ALU.mult)
                    link.end_phase()
                    link.end_phase()
                    link(V.tensor_copy(gplace[:, 0:PASSES], ps[7][:, 0:PASSES]))
                    link.end_phase()

                    def expert(pi, narrow):
                        w = MOE_F // 2 if narrow else MOE_F
                        V.tensor_copy(gpass[:, :], gplace[:, bass.ds(pi, 1)]).then_inc(gpass_set, 1)
                        ve.wait_ge(gpass_set, pi + 1)
                        for r in range(MOE_ROUNDS):
                            ve.wait_ge(sil_ready, pi * MOE_ROUNDS + (SIL0 + r + 1))
                            ve.wait_ge(slot_used, pi * len(MOE_ORDER) + u_done[r])
                            ve.wait_ge(matok_turned, pi * MOE_ROUNDS + (PRIME + r))
                            V.scalar_tensor_tensor(out=matok[:, 0:w], in0=msil[:, 0:w], scalar=gpass, in1=ps[2][:, 0:w],
                                                   op0=ALU.mult, op1=ALU.mult).then_inc(act_ready, 1)
                        for d in range(KT):
                            ve.wait_ge(scattered, pi * KT + (PRIME + d // 2 * 2 + 2))
                            V.scalar_tensor_tensor(out=xT[:, d, SEQ:N_TOK], in0=ps[d // 2][:, d % 2 * SEQ:(d % 2 + 1) * SEQ],
                                                   scalar=mod[:, 5 * KT + d, 1:2], in1=xT[:, d, SEQ:N_TOK],
                                                   op0=ALU.mult, op1=ALU.add).then_inc(down_added, 1)

                    def either(pi):
                        slim = ve.value_load(meta[0:1, bass.ds(pi + (1 + EXTRA), 1)], min_val=0, max_val=1)
                        with ve.If(slim > 0):
                            expert(pi, True)
                        with ve.If(slim < 1):
                            expert(pi, False)

                    ve.wait_ge(meta_ready, 1)
                    with ve.Fori(0, N_EXPERTS) as pi:
                        either(pi)
                    n_over = ve.value_load(meta[0:1, 0:1], min_val=0, max_val=EXTRA)
                    with ve.Fori(0, EXTRA) as p:
                        with ve.If(p < n_over):
                            either(p + N_EXPERTS)
                    link.end_phase()
            rms(SEQ, n_normed)
            link.end_phase()
            link.end_phase()
            for k in range(4, KT):
                for t in range(2):
                    link(V.tensor_copy(hT[:, 2 * t + k // 4, k % 4 * P:(k % 4 + 1) * P], ps[k][:, t * P:(t + 1) * P]))
            ve.drain().then_inc(rows_out, 1)
            ended.append(link.phases)

        @block.gpsimd
        def _(po):
            link = Link(po, pool_chain)
            G = nc.gpsimd
            link(G.memset(vrow[:, :], 0.0))
            def modulated(which, lo, m):
                for k in POOL_TILES:
                    po.wait_ge(normed, m * KT + k + 1)
                    for st_ in range(lo // SEQ, 2):
                        cols = slice(st_ * SEQ, (st_ + 1) * SEQ)
                        last = G.tensor_scalar(hT[:, k, cols], hT[:, k, cols], amul[:, which, k, st_:st_ + 1],
                                               mod[:, 3 * which * KT + k, st_:st_ + 1], ALU.mult, ALU.add)
                    last.then_inc(h_pool, 1)

            def load_rows(layer):
                link(G.memset(hh2[HEAD:HEAD + 1, :], 1.0))
                for dst, src in row_loads(layer):
                    po.dma_start(dst, src).then_inc(rows_in, 16)

            link(G.memset(hh2[HEAD:HEAD + 1, :], 1.0))
            for _ in range(4):
                link.end_phase()
            for layer in range(N_LAYERS):
                last_layer = layer == N_LAYERS - 1
                for _ in range(FILTER_STAGES + 2):
                    link.end_phase()
                modulated(0, 0, 2 * layer)
                for _ in range(1 + HY_PHASES):
                    link.end_phase()
                link.end_phase()
                link.end_phase()
                for i in range(2 * PAIRS):
                    if i >= 2:
                        po.wait_ge(sum_ready, layer * 2 * PAIRS + i - 1)
                    G.tensor_tensor(sqb[:, i % 2, :], qkv[:, i, :], qkv[:, i, :], ALU.mult).then_inc(sq_ready, 1)
                link.end_phase()
                link(G.memset(state[:, :, :], 0.0))
                for _ in range(8):
                    link.end_phase()
                for i in range(4):
                    G0, D0 = (layer * 4 + i) * 4, (layer * 4 + i) * DIRS
                    po.wait_ge(kds_ready, layer * 4 + i + 1)
                    for d in range(DIRS):
                        tile = STEP_TILES[i][d]
                        qs = slice(d * DN_HEADS, (d + 1) * DN_HEADS)
                        G.tensor_tensor(kd[:, d * PAIRS:(d + 1) * PAIRS, :].rearrange("p a (b c) -> p (a b) c", b=2),
                                        ktok[:, tile, :].rearrange("p (a b) -> p a b", a=DN_HEADS),
                                        over(kds[:, qs], HEAD), ALU.mult).then_inc(kd_ready, 1)
                    G.memset(Bm[:, :, :], 0.0)
                    for lv in range(1, LEVELS):
                        for g, d, qs in GROUPS:
                            ix = lvl_index(layer, i, lv, g)
                            if lv > 1:
                                po.wait_ge(b_ready, ix - 3)
                            else:
                                po.wait_ge(a_ready, G0 + g + 1)
                            G.tensor_tensor(Am[:, qs, :], Amat[:, qs, :], mask(K_LVL + (d * LEVELS + lv) * P),
                                            ALU.mult).then_inc(am_ready, 1)
                        if lv == 1:
                            for g, d, qs in GROUPS:
                                po.wait_ge(qk_read, G0 + g + 1)
                                G.tensor_tensor(QK[:, qs, :], QK[:, qs, :], mask(K_INC + d * P),
                                                ALU.mult).then_inc(qk_ready, 1)
                link.end_phase()
                for _ in range(4):
                    link.end_phase()
                link.end_phase()
                if last_layer:
                    po.dma_start(wr[:, :, :], a["moe_router"][0].rearrange("(k p) e -> p k e", p=P)).then_inc(router_in, 16)
                modulated(1, SEQ if last_layer else 0, 2 * layer + 1)
                if not last_layer:
                    po.wait_ge(h_pool, len(POOL_TILES) * (2 * layer + 2))
                    load_rows(layer + 1)
                for _ in range(9 if last_layer else 1):
                    link.end_phase()
            for _ in range(2):
                link.end_phase()
            ended.append(link.phases)

        assert len(set(ended)) == 1, ended


_NAMES = ["x", "c", "ctx", "c_ctx", "w_mod", "b_mod", "norm_mix_g", "norm_ffn_g", "w_in", "dn_conv_w", "dn_a_log",
          "dn_dt_bias", "dn_norm_g", "hy_conv_w", "hy_w1", "hy_b1", "hy_freq1", "hy_w2", "hy_b2", "hy_freq2", "hy_w3",
          "hy_b3", "hy_skip", "sw_sink", "w_out", "ffn_w_gate", "ffn_w_up", "ffn_w_down", "moe_router", "moe_w_gate",
          "moe_w_up", "moe_w_down", "final_norm_g"]


def kernel(**inputs):
    import concourse.bacc as bacc
    from concourse.bass_utils import run_bass_kernel_spmd

    nc = bacc.Bacc("TRN2", target_bir_lowering=False, num_devices=1)
    arrays, aps = {}, {}
    k_con, k_hy = shape_constants()
    tensors = {n: np.ascontiguousarray(inputs[n]) for n in _NAMES}
    tensors["k_con"], tensors["k_hy"] = k_con, k_hy
    for name, t in tensors.items():
        arrays[f"in_{name}"] = t
        aps[name] = nc.dram_tensor(f"in_{name}", t.shape, mybir.dt.from_np(t.dtype), kind="ExternalInput").ap()
    out = nc.dram_tensor("out", (1, SEQ, D_MODEL), F32, kind="ExternalOutput").ap()
    build(nc, aps, out)
    r = run_bass_kernel_spmd(nc, [arrays], core_ids=[0])
    return r.results[0]["out"]
```
